# Optimizing a Trainium2 kernel written in Bass

```python
import jax, jax.numpy as jnp
from jax import lax
import numpy as np

D_MODEL = 1024
BATCH = 1
SEQ = 2048
DEPTH = 1

GRID_W = 64
CTX_LEN = 256
N_MIXERS = 4
QBLK = 128
EPS = 1e-6
ROPE_THETA = 10000.0
NEG_INF = -1e30

MLA_HEADS = 8
MLA_Q_RANK = 512
MLA_KV_RANK = 256
MLA_NOPE = 128
MLA_ROPE = 64
MLA_V = 128
FNET_GROUPS = 4
FNET_GC = D_MODEL // FNET_GROUPS
NA_HEADS = 16
NA_HD = D_MODEL // NA_HEADS
NA_KR_MAX = 8
NA_KC = 16
SW_HEADS = 16
SW_KV_HEADS = 4
SW_HD = 64
SW_WINDOW = 128
MOE_GROUPS = 4
MOE_PER_GROUP = 8
MOE_EXPERTS = MOE_GROUPS * MOE_PER_GROUP
MOE_TOPK = 2
MOE_FF = 512
MOE_BLK = 128

kernel_name = 'hybrid_mla_fnet_na_swa_hmoe'

def _n_uses(m):
    return len(range(m, DEPTH, N_MIXERS))

def rmsnorm(x, g):
    xf = x.astype(jnp.float32)
    y = xf * lax.rsqrt(jnp.mean(xf * xf, axis=-1, keepdims=True) + EPS)
    return (y * g.astype(jnp.float32)).astype(x.dtype)

def softmax_f32(s, dtype):
    return jax.nn.softmax(s.astype(jnp.float32), axis=-1).astype(dtype)

def axial_rope_angles(row, col, d_rot):
    n = d_rot // 4
    inv = ROPE_THETA ** (-jnp.arange(n, dtype=jnp.float32) / n)
    return jnp.concatenate([row.astype(jnp.float32)[:, None] * inv,
                            col.astype(jnp.float32)[:, None] * inv], axis=-1)

def apply_rope(x, ang):
    cos = jnp.cos(ang)[None, :, None, :]
    sin = jnp.sin(ang)[None, :, None, :]
    x1, x2 = jnp.split(x.astype(jnp.float32), 2, axis=-1)
    return jnp.concatenate([x1 * cos - x2 * sin, x1 * sin + x2 * cos], axis=-1).astype(x.dtype)

def mla_project(h, w_dq, g_q, w_uq, w_dkv, g_kv, w_ukv, ang):
    B, L, _ = h.shape
    q = (rmsnorm(h @ w_dq, g_q) @ w_uq).reshape(B, L, MLA_HEADS, MLA_NOPE + MLA_ROPE)
    q_nope, q_rope = q[..., :MLA_NOPE], q[..., MLA_NOPE:]
    kv_a = h @ w_dkv
    c_kv = rmsnorm(kv_a[..., :MLA_KV_RANK], g_kv)
    k_rope = kv_a[..., None, MLA_KV_RANK:]
    kv = (c_kv @ w_ukv).reshape(B, L, MLA_HEADS, MLA_NOPE + MLA_V)
    k_nope, v = kv[..., :MLA_NOPE], kv[..., MLA_NOPE:]
    if ang is not None:
        q_rope = apply_rope(q_rope, ang)
        k_rope = apply_rope(k_rope, ang)
    return q_nope, q_rope, k_nope, k_rope[:, :, 0], v

def mla_mixer(h_c, h_l, ang, w_dq, g_q, w_uq, w_dkv, g_kv, w_ukv, w_o, with_ctx):
    B, S, _ = h_l.shape
    qn_c, qr_c, kn_c, kr_c, v_c = mla_project(h_c, w_dq, g_q, w_uq, w_dkv, g_kv, w_ukv, None)
    qn_l, qr_l, kn_l, kr_l, v_l = mla_project(h_l, w_dq, g_q, w_uq, w_dkv, g_kv, w_ukv, ang)
    kn = jnp.concatenate([kn_c, kn_l], axis=1)
    kr = jnp.concatenate([kr_c, kr_l], axis=1)
    v = jnp.concatenate([v_c, v_l], axis=1)
    scale = (MLA_NOPE + MLA_ROPE) ** -0.5

    def attend(qn, qr, kn_, kr_, v_):
        s = (jnp.einsum('bqhd,bkhd->bhqk', qn, kn_) + jnp.einsum('bqhd,bkd->bhqk', qr, kr_)) * scale
        return jnp.einsum('bhqk,bkhd->bqhd', softmax_f32(s, v_.dtype), v_)

    def block(i):
        sl = lambda a: lax.dynamic_slice_in_dim(a, i * QBLK, QBLK, 1)
        return attend(sl(qn_l), sl(qr_l), kn, kr, v)

    o = lax.map(block, jnp.arange(S // QBLK))
    y_l = o.transpose(1, 0, 2, 3, 4).reshape(B, S, MLA_HEADS * MLA_V) @ w_o
    y_c = None
    if with_ctx:
        y_c = attend(qn_c, qr_c, kn_c, kr_c, v_c).reshape(B, h_c.shape[1], MLA_HEADS * MLA_V) @ w_o
    return y_c, y_l

def grouped_fourier(h):
    B, L, D = h.shape
    hg = h.astype(jnp.float32).reshape(B, L, FNET_GROUPS, FNET_GC)
    f = jnp.fft.fft2(hg, axes=(1, 3), norm='ortho').real
    return f.reshape(B, L, D).astype(h.dtype)

def fnet_mixer(h_c, h_l, w_o, b_o, with_ctx):
    y_l = grouped_fourier(h_l) @ w_o + b_o
    y_c = grouped_fourier(h_c) @ w_o + b_o if with_ctx else None
    return y_c, y_l

def na_mixer(h_c, h_l, w_qkv, rpb, w_o, with_ctx):
    B, S, D = h_l.shape
    C = h_c.shape[1]
    rows = S // GRID_W
    kr = min(NA_KR_MAX, rows)
    nloc = kr * NA_KC
    scale = NA_HD ** -0.5
    qkv_l = (h_l @ w_qkv).reshape(B, S, 3, NA_HEADS, NA_HD)
    qkv_c = (h_c @ w_qkv).reshape(B, C, 3, NA_HEADS, NA_HD)
    q_c, k_c, v_c = qkv_c[:, :, 0], qkv_c[:, :, 1], qkv_c[:, :, 2]
    qg = qkv_l[:, :, 0].reshape(B, rows, GRID_W, NA_HEADS, NA_HD)
    kg = qkv_l[:, :, 1].reshape(B, rows, GRID_W, NA_HEADS, NA_HD)
    vg = qkv_l[:, :, 2].reshape(B, rows, GRID_W, NA_HEADS, NA_HD)
    colq = jnp.arange(GRID_W)
    cidx = jnp.clip(colq - NA_KC // 2, 0, GRID_W - NA_KC)[:, None] + jnp.arange(NA_KC)
    dc = cidx - colq[:, None]

    def row_block(r):
        rs = jnp.clip(r - kr // 2, 0, rows - kr)
        kb = lax.dynamic_slice_in_dim(kg, rs, kr, 1)[:, :, cidx]
        vb = lax.dynamic_slice_in_dim(vg, rs, kr, 1)[:, :, cidx]
        qb = lax.dynamic_index_in_dim(qg, r, 1, keepdims=False)
        dr = rs + jnp.arange(kr) - r
        bias = rpb[:, dr[None, :, None] + NA_KR_MAX - 1, dc[:, None, :] + NA_KC - 1]
        s_loc = jnp.einsum('bqhd,brqchd->bhqrc', qb, kb) * scale + bias[None]
        s_ctx = jnp.einsum('bqhd,bkhd->bhqk', qb, k_c) * scale
        p = softmax_f32(jnp.concatenate([s_loc.reshape(B, NA_HEADS, GRID_W, nloc), s_ctx], -1), vb.dtype)
        p_loc = p[..., :nloc].reshape(B, NA_HEADS, GRID_W, kr, NA_KC)
        return (jnp.einsum('bhqrc,brqchd->bqhd', p_loc, vb)
                + jnp.einsum('bhqk,bkhd->bqhd', p[..., nloc:], v_c))

    o = lax.map(row_block, jnp.arange(rows))
    y_l = o.transpose(1, 0, 2, 3, 4).reshape(B, S, NA_HEADS * NA_HD) @ w_o
    y_c = None
    if with_ctx:
        s = jnp.einsum('bqhd,bkhd->bhqk', q_c, k_c) * scale
        o_c = jnp.einsum('bhqk,bkhd->bqhd', softmax_f32(s, v_c.dtype), v_c)
        y_c = o_c.reshape(B, C, NA_HEADS * NA_HD) @ w_o
    return y_c, y_l

def swa_mixer(h_c, h_l, ang, w_qkv, sinks, w_o, with_ctx):
    B, S, _ = h_l.shape
    G = SW_HEADS // SW_KV_HEADS
    nq, nk = SW_HEADS * SW_HD, SW_KV_HEADS * SW_HD
    scale = SW_HD ** -0.5
    sink = sinks.reshape(SW_KV_HEADS, G).astype(jnp.float32)

    def proj(h):
        L = h.shape[1]
        qkv = h @ w_qkv
        q = qkv[..., :nq].reshape(B, L, SW_HEADS, SW_HD)
        k = qkv[..., nq:nq + nk].reshape(B, L, SW_KV_HEADS, SW_HD)
        v = qkv[..., nq + nk:].reshape(B, L, SW_KV_HEADS, SW_HD)
        return q, k, v

    def scores(q, k):
        qg = q.reshape(q.shape[0], q.shape[1], SW_KV_HEADS, G, SW_HD)
        return (jnp.einsum('bqkgd,bnkd->bkgqn', qg, k) * scale).astype(jnp.float32)

    def out(p, v):
        o = jnp.einsum('bkgqn,bnkd->bqkgd', p, v)
        return o.reshape(o.shape[0], o.shape[1], nq)

    def with_sink(s):
        return jnp.concatenate([s, jnp.broadcast_to(sink[None, :, :, None, None], s.shape[:-1] + (1,))], -1)

    q_l, k_l, v_l = proj(h_l)
    q_l, k_l = apply_rope(q_l, ang), apply_rope(k_l, ang)
    q_c, k_c, v_c = proj(h_c)
    band = QBLK + 2 * SW_WINDOW
    pad = ((0, 0), (SW_WINDOW, SW_WINDOW), (0, 0), (0, 0))
    kp, vp = jnp.pad(k_l, pad), jnp.pad(v_l, pad)
    rel = (jnp.arange(band) - SW_WINDOW)[None, :] - jnp.arange(QBLK)[:, None]

    def block(i):
        qb = lax.dynamic_slice_in_dim(q_l, i * QBLK, QBLK, 1)
        kb = lax.dynamic_slice_in_dim(kp, i * QBLK, band, 1)
        vb = lax.dynamic_slice_in_dim(vp, i * QBLK, band, 1)
        kpos = i * QBLK - SW_WINDOW + jnp.arange(band)
        ok = (jnp.abs(rel) <= SW_WINDOW) & (kpos >= 0)[None, :] & (kpos < S)[None, :]
        s_loc = jnp.where(ok, scores(qb, kb), NEG_INF)
        s = with_sink(jnp.concatenate([s_loc, scores(qb, k_c)], -1))
        p = jax.nn.softmax(s, axis=-1)[..., :-1].astype(vb.dtype)
        return out(p[..., :band], vb) + out(p[..., band:], v_c)

    o = lax.map(block, jnp.arange(S // QBLK))
    y_l = o.transpose(1, 0, 2, 3).reshape(B, S, nq) @ w_o
    y_c = None
    if with_ctx:
        p = jax.nn.softmax(with_sink(scores(q_c, k_c)), axis=-1)[..., :-1].astype(v_c.dtype)
        y_c = out(p, v_c) @ w_o
    return y_c, y_l

def hier_moe(h, w_grp, b_grp, w_rt, b_rt, w_gate, w_up, w_down):
    N, D = h.shape
    hf = h.astype(jnp.float32)
    p_grp = jax.nn.softmax(hf @ w_grp.astype(jnp.float32) + b_grp.astype(jnp.float32), axis=-1)
    w_g, g_idx = lax.top_k(p_grp, 1)
    logit_e = (hf @ w_rt.astype(jnp.float32) + b_rt.astype(jnp.float32)).reshape(N, MOE_GROUPS, MOE_PER_GROUP)
    logit_e = jnp.take_along_axis(logit_e, g_idx[:, :, None], axis=1)[:, 0]
    w_e, e_idx = lax.top_k(jax.nn.softmax(logit_e, axis=-1), MOE_TOPK)
    gate = (w_g * w_e / jnp.sum(w_e, axis=-1, keepdims=True)).reshape(-1)
    eid = (g_idx * MOE_PER_GROUP + e_idx).reshape(-1)
    tok = jnp.repeat(jnp.arange(N, dtype=jnp.int32), MOE_TOPK)
    T = N * MOE_TOPK
    order = jnp.argsort(eid)
    se = eid[order]
    counts = jnp.bincount(eid, length=MOE_EXPERTS)
    start = jnp.cumsum(counts) - counts
    pcounts = (counts + MOE_BLK - 1) // MOE_BLK * MOE_BLK
    pend = jnp.cumsum(pcounts)
    dest = pend[se] - pcounts[se] + jnp.arange(T) - start[se]
    cap = -(-T // MOE_BLK) * MOE_BLK + MOE_EXPERTS * MOE_BLK
    nblk = cap // MOE_BLK
    buf_tok = jnp.zeros((cap,), jnp.int32).at[dest].set(tok[order])
    buf_gate = jnp.zeros((cap,), jnp.float32).at[dest].set(gate[order])
    blk_e = jnp.minimum(jnp.searchsorted(pend, jnp.arange(nblk) * MOE_BLK, side='right'), MOE_EXPERTS - 1)
    xb = h[buf_tok].reshape(nblk, MOE_BLK, D)

    def expert_block(args):
        xe, e = args
        return (jax.nn.silu(xe @ w_gate[e]) * (xe @ w_up[e])) @ w_down[e]

    yb = lax.map(expert_block, (xb, blk_e)).reshape(cap, D)
    return jnp.zeros_like(h).at[buf_tok].add(yb * buf_gate[:, None].astype(h.dtype))

def setup_inputs(seed: int = 0) -> dict:
    key = jax.random.key(seed)
    keys = iter(jax.random.split(key, 40))
    D = D_MODEL

    def nrm(shape, scale):
        return jax.random.normal(next(keys), shape, jnp.float32) * scale

    def gain(shape):
        return 1.0 + nrm(shape, 0.05)

    nA, nB, nC, nD = (_n_uses(m) for m in range(N_MIXERS))
    mla_qk = MLA_NOPE + MLA_ROPE
    sw_qkv = (SW_HEADS + 2 * SW_KV_HEADS) * SW_HD
    return {
        'x': nrm((BATCH, SEQ, D), 1.0),
        'c': nrm((BATCH, D), 1.0),
        'ctx': nrm((BATCH, CTX_LEN, D), 1.0),
        'c_ctx': nrm((D,), 1.0),
        'mod_w': nrm((DEPTH, D, 6 * D), 0.5 * D ** -0.5),
        'mod_b': nrm((DEPTH, 6 * D), 0.02),
        'norm1_g': gain((DEPTH, D)),
        'norm2_g': gain((DEPTH, D)),
        'mla_w_dq': nrm((nA, D, MLA_Q_RANK), D ** -0.5),
        'mla_g_q': gain((nA, MLA_Q_RANK)),
        'mla_w_uq': nrm((nA, MLA_Q_RANK, MLA_HEADS * mla_qk), MLA_Q_RANK ** -0.5),
        'mla_w_dkv': nrm((nA, D, MLA_KV_RANK + MLA_ROPE), D ** -0.5),
        'mla_g_kv': gain((nA, MLA_KV_RANK)),
        'mla_w_ukv': nrm((nA, MLA_KV_RANK, MLA_HEADS * (MLA_NOPE + MLA_V)), MLA_KV_RANK ** -0.5),
        'mla_w_o': nrm((nA, MLA_HEADS * MLA_V, D), (MLA_HEADS * MLA_V) ** -0.5),
        'fnet_w_o': nrm((nB, D, D), D ** -0.5),
        'fnet_b_o': nrm((nB, D), 0.02),
        'na_w_qkv': nrm((nC, D, 3 * NA_HEADS * NA_HD), D ** -0.5),
        'na_rpb': nrm((nC, NA_HEADS, 2 * NA_KR_MAX - 1, 2 * NA_KC - 1), 0.5),
        'na_w_o': nrm((nC, NA_HEADS * NA_HD, D), (NA_HEADS * NA_HD) ** -0.5),
        'swa_w_qkv': nrm((nD, D, sw_qkv), D ** -0.5),
        'swa_sinks': nrm((nD, SW_HEADS), 0.5),
        'swa_w_o': nrm((nD, SW_HEADS * SW_HD, D), (SW_HEADS * SW_HD) ** -0.5),
        'moe_w_grp': nrm((DEPTH, D, MOE_GROUPS), D ** -0.5),
        'moe_b_grp': nrm((DEPTH, MOE_GROUPS), 0.01),
        'moe_w_rt': nrm((DEPTH, D, MOE_EXPERTS), D ** -0.5),
        'moe_b_rt': nrm((DEPTH, MOE_EXPERTS), 0.01),
        'moe_w_gate': nrm((DEPTH, MOE_EXPERTS, D, MOE_FF), D ** -0.5),
        'moe_w_up': nrm((DEPTH, MOE_EXPERTS, D, MOE_FF), D ** -0.5),
        'moe_w_down': nrm((DEPTH, MOE_EXPERTS, MOE_FF, D), MOE_FF ** -0.5),
        'final_g': gain((D,)),
    }

def reference(x, c, ctx, c_ctx, mod_w, mod_b, norm1_g, norm2_g,
              mla_w_dq, mla_g_q, mla_w_uq, mla_w_dkv, mla_g_kv, mla_w_ukv, mla_w_o,
              fnet_w_o, fnet_b_o,
              na_w_qkv, na_rpb, na_w_o,
              swa_w_qkv, swa_sinks, swa_w_o,
              moe_w_grp, moe_b_grp, moe_w_rt, moe_b_rt, moe_w_gate, moe_w_up, moe_w_down,
              final_g):
    B, S, D = x.shape
    t = jnp.arange(S)
    ang = axial_rope_angles(t // GRID_W, t % GRID_W, MLA_ROPE)
    c_act = jax.nn.silu(c)
    cc_act = jax.nn.silu(c_ctx)
    x_lat, x_ctx = x, ctx
    for i in range(DEPTH):
        m, j = i % N_MIXERS, i // N_MIXERS
        with_ctx = i < DEPTH - 1
        mod_l = (c_act @ mod_w[i] + mod_b[i])[:, None, :]
        mod_c = cc_act @ mod_w[i] + mod_b[i]
        sh1_l, sc1_l, g1_l, sh2_l, sc2_l, g2_l = jnp.split(mod_l, 6, axis=-1)
        sh1_c, sc1_c, g1_c, sh2_c, sc2_c, g2_c = jnp.split(mod_c, 6, axis=-1)
        h_l = rmsnorm(x_lat, norm1_g[i]) * (1 + sc1_l) + sh1_l
        h_c = rmsnorm(x_ctx, norm1_g[i]) * (1 + sc1_c) + sh1_c
        if m == 0:
            y_c, y_l = mla_mixer(h_c, h_l, ang, mla_w_dq[j], mla_g_q[j], mla_w_uq[j], mla_w_dkv[j],
                                 mla_g_kv[j], mla_w_ukv[j], mla_w_o[j], with_ctx)
        elif m == 1:
            y_c, y_l = fnet_mixer(h_c, h_l, fnet_w_o[j], fnet_b_o[j], with_ctx)
        elif m == 2:
            y_c, y_l = na_mixer(h_c, h_l, na_w_qkv[j], na_rpb[j], na_w_o[j], with_ctx)
        else:
            y_c, y_l = swa_mixer(h_c, h_l, ang, swa_w_qkv[j], swa_sinks[j], swa_w_o[j], with_ctx)
        x_lat = x_lat + g1_l * y_l
        h2_l = rmsnorm(x_lat, norm2_g[i]) * (1 + sc2_l) + sh2_l
        moe_args = (moe_w_grp[i], moe_b_grp[i], moe_w_rt[i], moe_b_rt[i],
                    moe_w_gate[i], moe_w_up[i], moe_w_down[i])
        if with_ctx:
            x_ctx = x_ctx + g1_c * y_c
            h2_c = rmsnorm(x_ctx, norm2_g[i]) * (1 + sc2_c) + sh2_c
            n_c = h2_c.shape[0] * h2_c.shape[1]
            f = hier_moe(jnp.concatenate([h2_c.reshape(-1, D), h2_l.reshape(-1, D)], axis=0), *moe_args)
            x_ctx = x_ctx + g2_c * f[:n_c].reshape(h2_c.shape)
            x_lat = x_lat + g2_l * f[n_c:].reshape(h2_l.shape)
        else:
            x_lat = x_lat + g2_l * hier_moe(h2_l.reshape(-1, D), *moe_args).reshape(h2_l.shape)
    return rmsnorm(x_lat, final_g)


_drawn_inputs = setup_inputs


def setup_inputs(seed=0):
    import zlib

    import numpy as np

    out = dict(_drawn_inputs(seed))
    spreads = {}
    factors = {'ctx': 8.0,
     'c_ctx': 4.201,
     'mod_b': 3.05,
     'norm1_g': 8.0,
     'norm2_g': 2.788,
     'mla_g_q': 8.0,
     'mla_g_kv': 8.0,
     'moe_b_grp': 8.0,
     'moe_b_rt': 8.0}
    for name, (base, spread) in spreads.items():
        noise = np.random.default_rng([zlib.crc32(name.encode()), seed]).standard_normal(out[name].shape)
        drawn = base * np.exp(spread * noise) if base else spread * noise
        out[name] = __import__('jax').numpy.asarray(drawn.astype(out[name].dtype))
    for name, factor in factors.items():
        out[name] = (out[name] * factor).astype(out[name].dtype)
    return out
```

```python
from contextlib import ExitStack

import numpy as np

import concourse.bass as bass
from concourse import mybir
from concourse.alu_op_type import AluOpType as ALU

F32, F16, BF16, I32 = mybir.dt.float32, mybir.dt.float16, mybir.dt.bfloat16, mybir.dt.int32
ACT = mybir.ActivationFunctionType
AX = mybir.AxisListType
ds = bass.ds

P = 128
D = 1024
SEQ, CTX = 2048, 256
KEYS = SEQ + CTX
GRID_W = 64
EPS = 1e-6
ROPE_THETA = 10000.0
HEADS, Q_RANK, KV_RANK, NOPE, ROPE, VD = 8, 512, 256, 128, 64, 128
HALF = ROPE // 2
QK = NOPE + ROPE
KV = NOPE + VD
SOFTMAX_SCALE = float(QK) ** -0.5
GROUPS_E, PER_GROUP = 4, 8
EXPERTS = GROUPS_E * PER_GROUP
TOPK = 2
FF = 512
BLK = 128

DC = D // P
RC = Q_RANK // P
KC = KV_RANK // P
FC = FF // P
BANK = 512
G = 256
TG = G // P
NG = KEYS // G
NGL = SEQ // G
NT = SEQ // P
KT = KEYS // P
WS = 64.0
LOG_P_SCALE = 6.931471805599453


class Steps:

    def __init__(self, eng, sem):
        self.eng, self.sem, self.base, self.n = eng, sem, 0, 0

    def did(self, ins):
        ins.then_inc(self.sem, 1)
        self.n += 1

    def settle(self):
        if not isinstance(self.base, int) or self.base + self.n:
            self.eng.wait_ge(self.sem, self.base + self.n)

    def enter(self, before, per):
        self.outer, self.per = self.base + self.n, per
        self.base, self.n = self.outer + before, 0

    def leave(self, count):
        assert self.n == self.per, (self.n, self.per)
        self.base, self.n = self.outer + count * self.per, 0


def wait_alone(eng, sem, value, passed):
    eng.wait_ge(sem, value)
    eng.sem_inc(passed, 1)


def three_pass(pe, out, lhs, rhs, first, last):
    pe.matmul(out, lhs[0], rhs[0], start=first, stop=False)
    pe.matmul(out, lhs[0], rhs[1], start=False, stop=False)
    return pe.matmul(out, lhs[1], rhs[0], start=False, stop=last)


def project(nc, io, keep):
    ctx = ExitStack()
    with ctx:
        sb = lambda name, shape, dt=F32: ctx.enter_context(nc.sbuf_tensor(f"project_{name}", shape, dt))
        sem = lambda name: ctx.enter_context(nc.semaphore(f"project_{name}"))
        bank = lambda name: ctx.enter_context(nc.psum_tensor(f"project_{name}", [P, BANK], F32))

        cqT, ckvT, krT, qrT, ident = keep["cqT"], keep["ckvT"], keep["krT"], keep["qrT"], keep["ident"]

        x_t = sb("x_t", [P, TG, D])
        junk = sb("junk", [P, D], BF16)
        hT = [sb(f"hT{s}", [P, 2, DC, G], F16) for s in ("hi", "lo")]
        f_t = sb("f_t", [P, 2, BANK])
        w_dq = [sb(f"w_dq{s}", [P, DC, Q_RANK], F16) for s in ("hi", "lo")]
        w_dkv = [sb(f"w_dkv{s}", [P, DC, KV_RANK + ROPE], F16) for s in ("hi", "lo")]
        w_qr = [sb(f"w_qr{s}", [P, RC, HEADS * ROPE], F16) for s in ("hi", "lo")]
        stage = sb("stage", [P, DC, BANK])
        cqn = sb("cqn", [P, TG, Q_RANK])
        ckn = sb("ckn", [P, TG, KV_RANK])
        k_raw = sb("k_raw", [P, TG, ROPE])
        k_rot = sb("k_rot", [P, TG, 2 * ROPE])
        q_raw = sb("q_raw", [P, HEADS, ROPE])
        q_rot = sb("q_rot", [P, TG, HEADS, 2 * ROPE])
        rt = [sb(f"rt{i}", [P, HEADS, HALF]) for i in range(4)]
        cos_t = sb("cos_t", [P, KT, HALF])
        sin_t = sb("sin_t", [P, KT, HALF])
        mod_acc = sb("mod_acc", [P, BANK])
        mod_row = sb("mod_row", [1, BANK])
        ones = sb("ones", [P, 1])
        cond_in = sb("cond_in", [P, DC, 2])
        cond = sb("cond", [P, DC, 2])
        modb_col = sb("modb_col", [P, 2 * DC])
        g1_col = sb("g1_col", [P, DC])
        gq_col = sb("gq_col", [P, RC])
        gkv_col = sb("gkv_col", [P, KC])
        shsc = sb("shsc", [P, 2 * DC, 2])
        aff = sb("aff", [P, DC, 2])
        ssum = sb("ssum", [P, 6])
        rms = sb("rms", [P, 6])
        rstd = sb("rstd", [P, 6])
        eps_t = sb("eps_t", [P, 1])
        early = [qrT[:, 4 * i:4 * i + 4, :].rearrange("p h t -> p (h t)").bitcast(F32)
                 .rearrange("p (k n) -> p k n", k=DC) for i in range(2)]

        tb = [bank(f"tb{i}") for i in range(2)]
        cq_ps = [bank(f"cq_ps{i}") for i in range(TG)]
        ck_ps = [bank(f"ck_ps{i}") for i in range(TG)]
        qr_ps, mr_ps = bank("qr_ps"), bank("mr_ps")

        small_in = sem("small_in")
        ident_in = sem("ident_in")
        rope_in = sem("rope_in")
        slot_in = [sem(f"slot_in{i}") for i in range(3)]
        x_in = sem("x_in")
        cond_ready = sem("cond_ready")
        mod_read = sem("mod_read")
        aff_ready = sem("aff_ready")
        w_hi = sem("w_hi")
        w_ready = sem("w_ready")
        stats = sem("stats")
        rms_ready = sem("rms_ready")
        dve_step = sem("dve_step")
        xn_ready = sem("xn_ready")
        t_full = sem("t_full")
        t_copied = sem("t_copied")
        t_free = sem("t_free")
        cq_full = sem("cq_full")
        ck_full = sem("ck_full")
        cqn_ready = sem("cqn_ready")
        ckn_ready = sem("ckn_ready")
        k_rot_ready = sem("k_rot_ready")
        qr_full = sem("qr_full")
        q_raw_ready = sem("q_raw_ready")
        q_rot_ready = sem("q_rot_ready")
        acc_ready = sem("acc_ready")
        mr_full = sem("mr_full")
        mod_row_ready = sem("mod_row_ready")
        mod_row_out = sem("mod_row_out")
        ones_ready = sem("ones_ready")
        sp_passed = sem("sp_passed")

        slots = [stage, early[0], early[1]]
        mod_v = io["mod_w"].rearrange("(k p) n -> p k n", p=P)
        loads = [(1, "mod0"), (2, "mod1"), (0, "mod2"), (1, "mod3"), (2, "dq"), (0, "dkv"), (1, "qr")]
        weights = {
            "dq": (io["w_dq"].rearrange("(k p) n -> p k n", p=P), w_dq, DC, Q_RANK),
            "dkv": (io["w_dkv"].rearrange("(k p) n -> p k n", p=P), w_dkv, DC, KV_RANK + ROPE),
            "qr": (io["w_uq_rope"].rearrange("(k p) n -> p k n", p=P), w_qr, RC, HEADS * ROPE),
        }
        seen = [0, 0, 0]
        nth = {}
        for s, what in loads:
            seen[s] += 1
            nth[what] = (s, seen[s])

        def slot_view(what):
            s = slots[nth[what][0]]
            if what.startswith("mod"):
                return s[:, :, :]
            _, _, k, n = weights[what]
            return s[:, :, :].rearrange("p k n -> p (k n)")[:, 0:k * n].rearrange("p (k n) -> p k n", k=k)

        def wait_slot(eng, what):
            s, n = nth[what]
            eng.wait_ge(slot_in[s], 16 * n)

        def fill(g, i):
            return 4 + 12 * g + i

        T_X, T_CQ, T_CKV, T_KR, T_QR = 0, 4, 6, 7, 8
        CTX_FILL = 4 + 12 * NGL
        block = ctx.enter_context(nc.Block())

        @block.sync
        def _(sp):
            sp.sem_inc(mod_row_out, 1)
            for dst, src in ((cond_in[:, :, 0], io["c"]), (cond_in[:, :, 1], io["c_ctx"])):
                sp.dma_start(dst, src.rearrange("(k p) -> p k", p=P), allow_slow_non_contiguous=True).then_inc(small_in, 16)
            for dst, src in ((modb_col, io["mod_b"][0:2 * D]), (g1_col, io["norm1_g"]),
                             (gq_col, io["g_q"]), (gkv_col, io["g_kv"])):
                sp.dma_start(dst[:, :], src.rearrange("(k p) -> p k", p=P), allow_slow_non_contiguous=True).then_inc(small_in, 16)
            sp.dma_start(slots[1][:, :, :], mod_v[:, :, 0:BANK]).then_inc(slot_in[1], 16)
            sp.dma_start(slots[2][:, :, :], mod_v[:, :, BANK:2 * BANK]).then_inc(slot_in[2], 16)
            sp.dma_start(slots[0][:, :, :], mod_v[:, :, 2 * BANK:3 * BANK]).then_inc(slot_in[0], 16)
            sp.dma_start(ident[:, :], io["ident"]).then_inc(ident_in, 16)
            sp.dma_start(x_t[:, :, :], io["xc"][0:G, :].rearrange("(j p) d -> p j d", p=P)).then_inc(x_in, 16)
            sp.wait_ge(mod_read, 1)
            sp.dma_start(slots[1][:, :, :], mod_v[:, :, 3 * BANK:4 * BANK]).then_inc(slot_in[1], 16)
            sp.dma_start(cos_t[:, :, :], io["cos"]).then_inc(rope_in, 16)
            sp.dma_start(sin_t[:, :, :], io["sin"]).then_inc(rope_in, 16)
            for what, used in (("dq", 2), ("dkv", 3), ("qr", 4)):
                sp.wait_ge(mod_read, used)
                sp.dma_start(slot_view(what), weights[what][0]).then_inc(slot_in[nth[what][0]], 16)
            sp.wait_ge(w_ready, 2)
            with sp.Fori(0, NGL) as g:
                sp.dma_start(stage[:, :, :], mod_v[:, :, ds(2 * D + g * BANK, BANK)]).then_inc(slot_in[0], 16)
                wait_alone(sp, t_full, 12 * g + 4, sp_passed)
                sp.dma_start(x_t[:, :, :], io["xc"][ds(g * G + G, G), :].rearrange("(j p) d -> p j d", p=P)).then_inc(x_in, 16)
                wait_alone(sp, mod_row_ready, g + 1, sp_passed)
                sp.dma_start(io["mod_rows"][:, ds(g * BANK, BANK)], mod_row[0:1, :]).then_inc(mod_row_out, 16)
                wait_alone(sp, acc_ready, g + 1, sp_passed)
            sp.wait_ge(mod_row_out, 16 * NGL + 1)

        @block.scalar
        def _(act):
            act.preload_act_table(ACT.Silu)
            act.wait_ge(small_in, 6 * 16)
            act.activation(cond[:, :, :], cond_in[:, :, :], ACT.Silu).then_inc(cond_ready, 1)
            for n, what in enumerate(("dq", "dkv", "qr")):
                wait_slot(act, what)
                act.activation(weights[what][1][0][:, :, :], slot_view(what), ACT.Copy, scale=WS).then_inc(w_hi, 1)

            stat = Steps(act, stats)

            def squares(src, i):
                stat.settle()
                stat.did(act.activation(junk[:, 0:src.shape[1]], src, ACT.Square, accum_out=ssum[:, i:i + 1]))

            def root(lo, hi, n, scale):
                stat.settle()
                act.activation(rms[:, lo:hi], ssum[:, lo:hi], ACT.Sqrt, bias=eps_t[:, :], scale=1.0 / (n * scale * scale)).then_inc(rms_ready, 1)

            def prep():
                for j in range(TG):
                    squares(x_t[:, j, :], j)
                root(0, TG, D, 1.0)

            def h_fills(n0, c):
                for i in range(4):
                    act.wait_ge(t_full, n0 + i + 1)
                    for u in range(2):
                        k = 2 * i + u
                        ins = act.activation(f_t[:, i % 2, u * G:(u + 1) * G], tb[i % 2][:, u * G:(u + 1) * G],
                                             ACT.Identity, bias=shsc[:, k, c:c + 1], scale=aff[:, k, c:c + 1])
                    ins.then_inc(t_copied, 1)

            def latent_stats(g, tiles, ctx_group):
                for j in range(tiles):
                    if not ctx_group:
                        act.wait_ge(cq_full, TG * g + j + 1)
                        squares(cq_ps[j][:, :], 2 + j)
                        root(2 + j, 3 + j, Q_RANK, WS)
                    act.wait_ge(ck_full, TG * g + j + 1)
                    act.activation(k_raw[:, j, :], ck_ps[j][:, KV_RANK:KV_RANK + ROPE], ACT.Copy, scale=1 / WS)
                    squares(ck_ps[j][:, 0:KV_RANK], 4 + j)
                    root(4 + j, 5 + j, KV_RANK, WS)

            def kv_fills(n0, g, i0):
                act.wait_ge(t_full, n0 + 1)
                for u in range(KC):
                    ins = act.activation(f_t[:, i0 % 2, u * G:(u + 1) * G], tb[i0 % 2][:, u * G:(u + 1) * G],
                                         ACT.Copy, scale=gkv_col[:, u:u + 1])
                ins.then_inc(t_copied, 1)
                act.wait_ge(t_full, n0 + 2)
                act.activation(krT[0][:, ds(g * G, G)], tb[(i0 + 1) % 2][:, 0:G], ACT.Copy).then_inc(t_copied, 1)

            act.preload_act_table(ACT.Sqrt)
            act.wait_ge(ones_ready, 2)
            act.wait_ge(x_in, 16)
            prep()
            act.wait_ge(aff_ready, 1)
            h_fills(0, 0)

            def group(g, c_next):
                act.wait_ge(x_in, 16 * g + 32)
                prep()
                latent_stats(g, TG, False)
                act.wait_ge(mr_full, g + 2)
                act.wait_ge(mod_row_out, 16 * g + 1)
                act.activation(mod_row[0:1, :], mr_ps[0:1, :], ACT.Copy).then_inc(mod_row_ready, 1)
                h_fills(fill(g, T_X), c_next)
                for i in range(2):
                    act.wait_ge(t_full, fill(g, T_CQ + i) + 1)
                    for u in range(2):
                        ins = act.activation(f_t[:, i, u * G:(u + 1) * G], tb[i][:, u * G:(u + 1) * G],
                                             ACT.Copy, scale=gq_col[:, 2 * i + u:2 * i + u + 1])
                    ins.then_inc(t_copied, 1)
                kv_fills(fill(g, T_CKV), g, T_CKV)
                for j in range(TG):
                    act.wait_ge(qr_full, TG * g + j + 1)
                    act.wait_ge(q_rot_ready, TG * g + j + 1)
                    act.activation(q_raw[:, :, :], qr_ps[:, :].rearrange("p (h r) -> p h r", h=HEADS), ACT.Copy,
                                   scale=1 / WS).then_inc(q_raw_ready, 1)
                for j in range(TG):
                    for u in range(2):
                        act.wait_ge(t_full, fill(g, T_QR + 2 * j + u) + 1)
                        act.activation(qrT[:, 4 * u:4 * u + 4, ds(g * G + j * P, P)],
                                       tb[u][:, :].rearrange("p (h t) -> p h t", h=4), ACT.Copy).then_inc(t_copied, 1)

            with act.Fori(0, NGL - 1) as g:
                stat.enter(6 * g, 6)
                group(g, 0)
            stat.leave(NGL - 1)
            group(NGL - 1, 1)
            latent_stats(NGL, TG, True)
            kv_fills(CTX_FILL, NGL, 0)

        @block.vector
        def _(dve):
            dve.sem_inc(q_rot_ready, 1)
            step = Steps(dve, dve_step)
            dve.memset(ones[:, :], 1.0).then_inc(ones_ready, 1)
            dve.memset(eps_t[:, :], EPS).then_inc(ones_ready, 1)
            dve.wait_ge(small_in, 6 * 16)
            dve.wait_ge(mod_read, 4)
            step.did(dve.tensor_tensor(shsc[:, :, :], mr_ps[:, 0:4 * DC].rearrange("p (k c) -> p k c", c=2),
                                       modb_col[:, :].unsqueeze(2).broadcast_to([P, 2 * DC, 2]), ALU.add))
            step.settle()
            dve.scalar_tensor_tensor(out=aff[:, :, :], in0=shsc[:, DC:2 * DC, :], scalar=1.0,
                                     in1=g1_col[:, :].unsqueeze(2).broadcast_to([P, DC, 2]),
                                     op0=ALU.add, op1=ALU.mult).then_inc(aff_ready, 1)

            def inverse_rms(n, lo, hi):
                dve.wait_ge(rms_ready, n + 1)
                step.did(dve.reciprocal(rstd[:, lo:hi], rms[:, lo:hi]))
                step.settle()

            def prep(n):
                inverse_rms(n, 0, TG)
                for j in range(TG):
                    dve.tensor_scalar(x_t[:, j, :], x_t[:, j, :], rstd[:, j:j + 1], None, ALU.mult).then_inc(xn_ready, 1)

            def split(src, hi, lo):
                step.did(dve.tensor_copy(hi, src))
                step.settle()
                dve.tensor_tensor(lo, src, hi, ALU.subtract).then_inc(t_free, 1)

            def h_fills(n0, par):
                for i in range(4):
                    dve.wait_ge(t_copied, n0 + i + 1)
                    split(f_t[:, i % 2, :].rearrange("p (k t) -> p k t", k=2),
                          hT[0][:, par, 2 * i:2 * i + 2, :], hT[1][:, par, 2 * i:2 * i + 2, :])

            def split_weight(n, what):
                dve.wait_ge(w_hi, n + 1)
                hi, lo = (t[:, :, :] for t in weights[what][1])
                dve.scalar_tensor_tensor(out=lo, in0=slot_view(what), scalar=WS, in1=hi,
                                         op0=ALU.mult, op1=ALU.subtract).then_inc(w_ready, 1)

            split_weight(0, "dq")
            split_weight(1, "dkv")
            prep(0)
            h_fills(0, 0)
            split_weight(2, "qr")
            dve.wait_ge(rope_in, 32)

            def normed(n, j, ctx_group):
                if not ctx_group:
                    inverse_rms(n, 2 + j, 3 + j)
                    n = n + 1
                    dve.tensor_scalar(cqn[:, j, :], cq_ps[j][:, :], rstd[:, 2 + j:3 + j], 1 / WS, ALU.mult, ALU.mult).then_inc(cqn_ready, 1)
                inverse_rms(n, 4 + j, 5 + j)
                dve.tensor_scalar(ckn[:, j, :], ck_ps[j][:, 0:KV_RANK], rstd[:, 4 + j:5 + j], 1 / WS, ALU.mult, ALU.mult).then_inc(ckn_ready, 1)

            def rotate(x, cs, sn, out, dup, n, ready):
                x1, x2 = x[:, :, 0:HALF], x[:, :, HALF:ROPE]
                a, b, c, d = (t[:, 0:n, :] for t in rt)
                for o, x_, w in ((a, x1, cs), (b, x2, sn), (c, x1, sn), (d, x2, cs)):
                    step.did(dve.tensor_tensor(o, x_, w, ALU.mult))
                step.settle()
                step.did(dve.tensor_tensor(out[:, :, 0:HALF], a, b, ALU.subtract))
                step.did(dve.tensor_tensor(out[:, :, HALF:ROPE], c, d, ALU.add))
                step.settle()
                dve.tensor_copy(dup, out).then_inc(ready, 1)

            def rotate_keys(g):
                rotate(k_raw[:, :, :], cos_t[:, ds(g * TG, TG), :], sin_t[:, ds(g * TG, TG), :],
                       k_rot[:, :, 0:ROPE], k_rot[:, :, ROPE:2 * ROPE], TG, k_rot_ready)

            def kv_fills(n0, g, i0):
                dve.wait_ge(t_copied, n0 + 1)
                split(f_t[:, i0 % 2, :].rearrange("p (k t) -> p k t", k=KC),
                      ckvT[0][:, :, ds(g * G, G)], ckvT[1][:, :, ds(g * G, G)])
                dve.wait_ge(t_copied, n0 + 2)
                dve.tensor_tensor(krT[1][:, ds(g * G, G)], tb[(i0 + 1) % 2][:, 0:G], krT[0][:, ds(g * G, G)],
                                  ALU.subtract).then_inc(t_free, 1)

            def group(g, par):
                prep(1 + 5 * g)
                dve.wait_ge(slot_in[0], 16 * g + 48)
                dve.wait_ge(mr_full, g + 1)
                step.did(dve.tensor_scalar(mod_acc[:, :], stage[:, 0, :], cond[:, 0, 0:1], None, ALU.mult))
                for k in range(1, DC):
                    step.settle()
                    ins = dve.scalar_tensor_tensor(out=mod_acc[:, :], in0=stage[:, k, :], scalar=cond[:, k, 0:1],
                                                   in1=mod_acc[:, :], op0=ALU.mult, op1=ALU.add)
                    if k < DC - 1:
                        step.did(ins)
                ins.then_inc(acc_ready, 1)
                for j in range(TG):
                    normed(2 + 5 * g + 2 * j, j, False)
                h_fills(fill(g, T_X), par)
                rotate_keys(g)
                for i in range(2):
                    dve.wait_ge(t_copied, fill(g, T_CQ + i) + 1)
                    split(f_t[:, i, :].rearrange("p (k t) -> p k t", k=2),
                          cqT[0][:, 2 * i:2 * i + 2, ds(g * G, G)], cqT[1][:, 2 * i:2 * i + 2, ds(g * G, G)])
                kv_fills(fill(g, T_CKV), g, T_CKV)
                for j in range(TG):
                    dve.wait_ge(q_raw_ready, TG * g + j + 1)
                    cs = cos_t[:, ds(g * TG + j, 1), :].broadcast_to([P, HEADS, HALF])
                    sn = sin_t[:, ds(g * TG + j, 1), :].broadcast_to([P, HEADS, HALF])
                    rotate(q_raw[:, :, :], cs, sn, q_rot[:, j, :, 0:ROPE], q_rot[:, j, :, ROPE:2 * ROPE], HEADS, q_rot_ready)
                for j in range(TG):
                    for u in range(2):
                        dve.wait_ge(t_copied, fill(g, T_QR + 2 * j + u) + 1)
                        lo = qrT[ROPE:P, 4 * u:4 * u + 4, ds(g * G + j * P, P)]
                        dve.tensor_tensor(lo, tb[u][ROPE:P, :].rearrange("p (h t) -> p h t", h=4), lo,
                                          ALU.subtract).then_inc(t_free, 1)

            per = 1 + 7 + 2 * 2 + 4 + 6 + 2 + 1 + 2 * 6
            with dve.Fori(0, NGL // 2) as gg:
                step.enter(gg * (2 * per), 2 * per)
                group(gg * 2, 1)
                group(gg * 2 + 1, 0)
            step.leave(NGL // 2)
            for j in range(TG):
                normed(1 + 5 * NGL + j, j, True)
            rotate_keys(NGL)
            kv_fills(CTX_FILL, NGL, 0)

        @block.tensor
        def _(pe):
            pe.sem_inc(mr_full, 1)
            pe.wait_ge(cond_ready, 1)
            for i in range(4):
                wait_slot(pe, f"mod{i}")
                for cc in range(4):
                    col = 4 * i + cc
                    for k in range(DC):
                        ins = pe.matmul(mr_ps[:, 2 * col:2 * col + 2], slots[nth[f"mod{i}"][0]][:, k, cc * P:(cc + 1) * P],
                                        cond[:, k, :], start=(k == 0), stop=(k == DC - 1))
                ins.then_inc(mod_read, 1)

            def transpose_x(n0, first=False):
                for i in range(4):
                    if not (first and i < 2):
                        pe.wait_ge(t_free, n0 + i - 1)
                    for u in range(2):
                        k = 2 * i + u
                        for j in range(TG):
                            ins = pe.transpose(tb[i % 2][:, u * G + j * P:u * G + (j + 1) * P], x_t[:, j, k * P:(k + 1) * P], ident[:, :])
                    ins.then_inc(t_full, 1)

            pe.wait_ge(ident_in, 16)
            pe.wait_ge(xn_ready, TG)
            transpose_x(0, first=True)
            pe.wait_ge(w_ready, 2)

            def down(g, j, par, ctx_group, first=False):
                tok = slice(j * P, (j + 1) * P)
                if not ctx_group:
                    if not first:
                        pe.wait_ge(cqn_ready, TG * g + j - TG + 1)
                    for k in range(DC):
                        ins = three_pass(pe, cq_ps[j][:, :], [t[:, par, k, tok] for t in hT], [t[:, k, :] for t in w_dq],
                                         k == 0, k == DC - 1)
                    ins.then_inc(cq_full, 1)
                if not first:
                    pe.wait_ge(ckn_ready, TG * g + j - TG + 1)
                for k in range(DC):
                    ins = three_pass(pe, ck_ps[j][:, 0:KV_RANK + ROPE], [t[:, par, k, tok] for t in hT],
                                     [t[:, k, :] for t in w_dkv], k == 0, k == DC - 1)
                ins.then_inc(ck_full, 1)

            def transpose_kv(g, n0, i0):
                pe.wait_ge(ckn_ready, TG * g + TG)
                pe.wait_ge(t_free, n0 - 1)
                for u in range(KC):
                    for j in range(TG):
                        ins = pe.transpose(tb[i0 % 2][:, u * G + j * P:u * G + (j + 1) * P], ckn[:, j, u * P:(u + 1) * P], ident[:, :])
                ins.then_inc(t_full, 1)
                pe.wait_ge(k_rot_ready, g + 1)
                pe.wait_ge(t_free, n0)
                for j in range(TG):
                    ins = pe.transpose(tb[(i0 + 1) % 2][:, j * P:(j + 1) * P], k_rot[:, j, :], ident[:, :])
                ins.then_inc(t_full, 1)

            def group(g, par, first=False):
                for j in range(TG):
                    if j == 0:
                        pe.wait_ge(t_free, 4 if first else 12 * g - 4)
                    down(g, j, par, False, first)
                pe.wait_ge(acc_ready, g + 1)
                if not first:
                    pe.wait_ge(mod_row_ready, g)
                pe.matmul(mr_ps[0:1, :], ones[:, :], mod_acc[:, :], start=True, stop=True).then_inc(mr_full, 1)
                pe.wait_ge(xn_ready, TG * g + 2 * TG)
                transpose_x(fill(g, T_X))
                pe.wait_ge(cqn_ready, TG * g + TG)
                for i in range(2):
                    pe.wait_ge(t_free, fill(g, T_CQ + i) - 1)
                    for u in range(2):
                        for j in range(TG):
                            ins = pe.transpose(tb[i][:, u * G + j * P:u * G + (j + 1) * P],
                                               cqn[:, j, (2 * i + u) * P:(2 * i + u + 1) * P], ident[:, :])
                    ins.then_inc(t_full, 1)
                transpose_kv(g, fill(g, T_CKV), T_CKV)
                if first:
                    pe.wait_ge(w_ready, 3)
                pe.wait_ge(t_free, fill(g, T_CQ + 2))
                for j in range(TG):
                    if not (first and j == 0):
                        pe.wait_ge(q_raw_ready, TG * g + j)
                    for k in range(RC):
                        ins = three_pass(pe, qr_ps[:, :], [t[:, k, ds(g * G + j * P, P)] for t in cqT], [t[:, k, :] for t in w_qr],
                                         k == 0, k == RC - 1)
                    ins.then_inc(qr_full, 1)
                for j in range(TG):
                    pe.wait_ge(q_rot_ready, TG * g + j + 2)
                    for u in range(2):
                        pe.wait_ge(t_free, fill(g, T_QR + 2 * j + u) - 1)
                        for v in range(4):
                            ins = pe.transpose(tb[u][:, v * P:(v + 1) * P], q_rot[:, j, 4 * u + v, :], ident[:, :])
                        ins.then_inc(t_full, 1)

            group(0, 0, first=True)
            group(1, 1)
            with pe.Fori(1, NGL // 2) as gg:
                group(gg * 2, 0)
                group(gg * 2 + 1, 1)
            pe.wait_ge(t_free, fill(NGL - 1, 4))
            for j in range(TG):
                down(NGL, j, 0, True)
            transpose_kv(NGL, CTX_FILL, 0)


SB = [(c * BANK, min(BANK, KEYS - c * BANK)) for c in range(-(-KEYS // BANK))]
NS = len(SB)
QB = SEQ // BANK
KPB = BANK // P


def attend(nc, io, keep):
    ctx = ExitStack()
    with ctx:
        sb = lambda name, shape, dt=F32: ctx.enter_context(nc.sbuf_tensor(f"attend_{name}", shape, dt))
        sem = lambda name: ctx.enter_context(nc.semaphore(f"attend_{name}"))
        cqT, ckvT, krT, qrT, ident = keep["cqT"], keep["ckvT"], keep["krT"], keep["qrT"], keep["ident"]

        NW = RC + 2 * KC
        w_raw = sb("w_raw", [P, NW, P])
        w_h = [sb(f"w_h{s}", [P, NW, P], F16) for s in ("hi", "lo")]
        qT = [sb(f"qT{s}", [P, SEQ], F16) for s in ("hi", "lo")]
        kT = [sb(f"kT{s}", [P, KEYS], F16) for s in ("hi", "lo")]
        v = sb("v", [P, KT, 2, VD], F16)
        prob = sb("prob", [P, KEYS])
        pT = [sb(f"pT{s}", [P, KT, P], F16) for s in ("hi", "lo")]
        o_lo = sb("o_lo", [P, VD])
        o_out = sb("o_out", [P, VD])
        mx = sb("mx", [P, NS])
        neg_max = sb("neg_max", [P, 2])
        rsum = sb("rsum", [P, NS])
        inv = sb("inv", [P, 2])

        s_ps = ctx.enter_context(nc.psum_tensor("attend_s_ps", [P, NS, BANK], F32))
        tb = [ctx.enter_context(nc.psum_tensor(f"attend_tp{i}", [P, BANK], F32)) for i in range(2)]
        o_ps = ctx.enter_context(nc.psum_tensor("attend_o_ps", [P, BANK], F32))

        w_in = sem("w_in")
        w_hi = sem("w_hi")
        w_ready = sem("w_ready")
        b_full = sem("b_full")
        b_copied = sem("b_copied")
        b_free = sem("b_free")
        s_full = sem("s_full")
        s_free = sem("s_free")
        max_step = sem("max_step")
        max_ready = sem("max_ready")
        inv_ready = sem("inv_ready")
        o_full = sem("o_full")
        o_lo_ready = sem("o_lo_ready")
        o_ready = sem("o_ready")
        o_stored = sem("o_stored")
        sp_passed = sem("sp_passed2")

        QKF, VF = QB + NS, NS
        PER = VF + NT * NS + QKF
        F_V, F_T, F_QK, F_LAST = 0, VF, VF + (NT - 1) * NS, VF + (NT - 1) * NS + QKF

        def head_fill(h, i):
            return QKF + PER * h + i

        wq = lambda t: [x[:, 0:RC, :] for x in t]
        wk = lambda t: [x[:, RC:RC + KC, :] for x in t]
        wv = lambda t: [x[:, RC + KC:NW, :] for x in t]
        LAST = HEADS - 1
        block = ctx.enter_context(nc.Block())

        @block.sync
        def _(sp):
            sp.sem_inc(o_stored, 1)
            def load(h):
                for dst, src, k in ((w_raw[:, 0:RC, :], io["w_uq"], RC), (w_raw[:, RC:RC + KC, :], io["w_uk"], KC),
                                    (w_raw[:, RC + KC:NW, :], io["w_uv"], KC)):
                    src = src[ds(h, 1)] if not isinstance(h, int) else src[h:h + 1]
                    sp.dma_start(dst, src.rearrange("a (k p) n -> p (a k) n", p=P)).then_inc(w_in, 16)

            load(0)
            sp.wait_ge(w_ready, 1)
            load(1)

            def stores(h):
                with sp.Fori(0, NT) as t:
                    wait_alone(sp, o_ready, h * NT + t + 2, sp_passed)
                    sp.dma_start(io["attn"][ds(t * P, P), ds(h * VD, VD)], o_out[:, :]).then_inc(o_stored, 16)

            with sp.Fori(0, HEADS - 2) as h:
                wait_alone(sp, w_ready, h + 2, sp_passed)
                load(h + 2)
                stores(h)
            with sp.Fori(HEADS - 2, HEADS) as h:
                stores(h)
            sp.wait_ge(o_stored, 16 * HEADS * NT + 1)

        @block.scalar
        def _(act):
            act.preload_act_table(ACT.Exp)

            def copy_fill(n, bank_, dst, width, scale):
                act.wait_ge(b_full, n + 1)
                src = bank_[:, 0:width]
                if len(dst.shape) == 3:
                    src = src.rearrange("p (k t) -> p k t", t=P)
                act.activation(dst, src, ACT.Copy, scale=scale).then_inc(b_copied, 1)

            def split_weights(h):
                act.wait_ge(w_in, 48 * h + 48)
                act.activation(w_h[0][:, :, :], w_raw[:, :, :], ACT.Copy, scale=WS).then_inc(w_hi, 1)

            def queries_keys(n, par):
                for c in range(QB):
                    copy_fill(n + c, tb[(par + c) % 2], qT[0][:, c * BANK:(c + 1) * BANK], BANK, 1 / WS)
                for c, (k0, w) in enumerate(SB):
                    copy_fill(n + QB + c, tb[(par + QB + c) % 2], kT[0][:, k0:k0 + w], w, 1 / WS)

            def values(n, par):
                for c, (k0, w) in enumerate(SB):
                    copy_fill(n + c, tb[(par + c) % 2], v[:, c * KPB:c * KPB + w // P, 0, :], w, 1 / WS)

            def exps(step):
                act.wait_ge(max_ready, step + 1)
                for c, (k0, w) in enumerate(SB):
                    act.activation(prob[:, k0:k0 + w], s_ps[:, c, 0:w], ACT.Exp, bias=neg_max[:, 1:2], scale=SOFTMAX_SCALE,
                                   accum_out=rsum[:, c:c + 1]).then_inc(s_free, 1)

            def transposed(n):
                for c, (k0, w) in enumerate(SB):
                    copy_fill(n + c, tb[c % 2], pT[0][:, c * KPB:c * KPB + w // P, :], w, 1.0)

            def low_output(step):
                act.wait_ge(o_full, step + 1)
                act.wait_ge(inv_ready, step + 1)
                act.activation(o_lo[:, :], o_ps[:, VD:2 * VD], ACT.Copy, scale=inv[:, 1:2]).then_inc(o_lo_ready, 1)

            def head(h, last):
                values(head_fill(h, F_V), 0)
                if not last:
                    act.wait_ge(b_full, head_fill(h, F_V) + VF)
                    split_weights(h + 1)
                exps(h * NT)
                with act.Fori(1, NT) as t:
                    transposed(head_fill(h, F_T) + (t - 1) * NS)
                    exps(h * NT + t)
                    low_output(h * NT + t - 1)
                n = head_fill(h, F_QK)
                if not last:
                    queries_keys(n, 0)
                    n = head_fill(h, F_LAST)
                transposed(n)
                low_output(h * NT + NT - 1)

            act.sem_inc(s_free, NS)
            split_weights(0)
            queries_keys(0, 0)
            with act.Fori(0, LAST) as h:
                head(h, False)
            head(LAST, True)

        @block.vector
        def _(dve):
            dve.sem_inc(o_ready, 1)
            step = Steps(dve, max_step)

            def split_fill(n, bank_, hi, lo, width, scale):
                dve.wait_ge(b_copied, n + 1)
                src = bank_[:, 0:width]
                if len(hi.shape) == 3:
                    src = src.rearrange("p (k t) -> p k t", t=P)
                if scale == 1.0:
                    ins = dve.tensor_tensor(lo, src, hi, ALU.subtract)
                else:
                    ins = dve.scalar_tensor_tensor(out=lo, in0=src, scalar=scale, in1=hi, op0=ALU.mult, op1=ALU.subtract)
                ins.then_inc(b_free, 1)

            def split_weights(h):
                dve.wait_ge(w_hi, h + 1)
                dve.scalar_tensor_tensor(out=w_h[1][:, :, :], in0=w_raw[:, :, :], scalar=WS, in1=w_h[0][:, :, :],
                                         op0=ALU.mult, op1=ALU.subtract).then_inc(w_ready, 1)

            def queries_keys(n, par):
                for c in range(QB):
                    s = slice(c * BANK, (c + 1) * BANK)
                    split_fill(n + c, tb[(par + c) % 2], qT[0][:, s], qT[1][:, s], BANK, 1 / WS)
                for c, (k0, w) in enumerate(SB):
                    s = slice(k0, k0 + w)
                    split_fill(n + QB + c, tb[(par + QB + c) % 2], kT[0][:, s], kT[1][:, s], w, 1 / WS)

            def values(n, par):
                for c, (k0, w) in enumerate(SB):
                    s = slice(c * KPB, c * KPB + w // P)
                    split_fill(n + c, tb[(par + c) % 2], v[:, s, 0, :], v[:, s, 1, :], w, 1 / WS)

            def chunk_max(st, c):
                dve.wait_ge(s_full, st * NS + c + 1)
                step.did(dve.tensor_reduce(mx[:, c:c + 1], s_ps[:, c, 0:SB[c][1]], AX.X, ALU.max))

            def row_max():
                step.settle()
                step.did(dve.tensor_reduce(neg_max[:, 0:1], mx[:, :], AX.X, ALU.max))
                step.settle()
                dve.tensor_scalar(neg_max[:, 1:2], neg_max[:, 0:1], -SOFTMAX_SCALE, LOG_P_SCALE, ALU.mult, ALU.add).then_inc(max_ready, 1)

            def inverse(st):
                dve.wait_ge(s_free, (st + 2) * NS)
                step.did(dve.tensor_reduce(inv[:, 0:1], rsum[:, :], AX.X, ALU.add))
                step.settle()
                dve.reciprocal(inv[:, 1:2], inv[:, 0:1]).then_inc(inv_ready, 1)

            def output(st):
                dve.wait_ge(o_lo_ready, st + 1)
                dve.wait_ge(o_stored, st * 16 + 1)
                dve.scalar_tensor_tensor(out=o_out[:, :], in0=o_ps[:, 0:VD], scalar=inv[:, 1:2], in1=o_lo[:, :],
                                         op0=ALU.mult, op1=ALU.add).then_inc(o_ready, 1)

            def low_fill(n, c):
                k0, w = SB[c]
                s = slice(c * KPB, c * KPB + w // P)
                split_fill(n + c, tb[c % 2], pT[0][:, s, :], pT[1][:, s, :], w, 1.0)

            MAX_STEPS = NS + 1
            TILE_STEPS = MAX_STEPS + 1
            HEAD_STEPS = MAX_STEPS + (NT - 1) * TILE_STEPS + 1

            def head(h, last):
                values(head_fill(h, F_V), 0)
                if not last:
                    split_weights(h + 1)
                for c in range(NS):
                    chunk_max(h * NT, c)
                row_max()
                with dve.Fori(1, NT) as t:
                    step.enter((t - 1) * TILE_STEPS, TILE_STEPS)
                    st = h * NT + t
                    inverse(st - 1)
                    for c in range(NS):
                        chunk_max(st, c)
                        low_fill(head_fill(h, F_T) + (t - 1) * NS, c)
                    row_max()
                    output(st - 1)
                step.leave(NT - 1)
                inverse(h * NT + NT - 1)
                n = head_fill(h, F_QK)
                if not last:
                    queries_keys(n, 0)
                    n = head_fill(h, F_LAST)
                for c in range(NS):
                    low_fill(n, c)
                output(h * NT + NT - 1)

            split_weights(0)
            queries_keys(0, 0)
            with dve.Fori(0, LAST) as h:
                step.enter(h * HEAD_STEPS, HEAD_STEPS)
                outer = step.outer
                head(h, False)
            step.base, step.n = outer + LAST * HEAD_STEPS, 0
            head(LAST, True)

        @block.tensor
        def _(pe):
            def wait_bank(n, lag=1):
                if isinstance(n, int):
                    if n - lag > 0:
                        pe.wait_ge(b_free, n - lag)
                else:
                    pe.wait_ge(b_free, n - lag)

            def queries_keys(h, n, par):
                pe.wait_ge(w_ready, h + 1)
                for c in range(QB):
                    wait_bank(n + c, 0 if c == 0 else 1)
                    for k in range(RC):
                        ins = three_pass(pe, tb[(par + c) % 2][:, :], [t[:, k, :] for t in w_h],
                                         [t[:, k, c * BANK:(c + 1) * BANK] for t in cqT], k == 0, k == RC - 1)
                    ins.then_inc(b_full, 1)
                for c, (k0, w) in enumerate(SB):
                    wait_bank(n + QB + c)
                    for k in range(KC):
                        ins = three_pass(pe, tb[(par + QB + c) % 2][:, 0:w], [t[:, RC + k, :] for t in w_h],
                                         [t[:, k, k0:k0 + w] for t in ckvT], k == 0, k == KC - 1)
                    ins.then_inc(b_full, 1)

            def values(n, par):
                for c, (k0, w) in enumerate(SB):
                    wait_bank(n + c, 0 if c == 0 else 1)
                    for i in range(w // P):
                        keys = slice(k0 + i * P, k0 + (i + 1) * P)
                        for k in range(KC):
                            ins = three_pass(pe, tb[(par + c) % 2][:, i * P:(i + 1) * P], [t[:, k, keys] for t in ckvT],
                                             [t[:, RC + KC + k, :] for t in w_h], k == 0, k == KC - 1)
                    ins.then_inc(b_full, 1)

            def scores(h, t, st, c):
                k0, w = SB[c]
                q = ds(t * P, P) if not isinstance(t, int) else slice(t * P, (t + 1) * P)
                pe.wait_ge(s_free, st * NS + c + 1)
                out, keys = s_ps[:, c, 0:w], slice(k0, k0 + w)
                pe.matmul(out, qT[0][:, q], kT[0][:, keys], start=True, stop=False)
                pe.matmul(out, qT[0][:, q], kT[1][:, keys], start=False, stop=False)
                pe.matmul(out, qT[1][:, q], kT[0][:, keys], start=False, stop=False)
                r = qrT[:, ds(h, 1), q].rearrange("p a t -> p (a t)") if not isinstance(h, int) else qrT[:, h, q]
                pe.matmul(out, r, krT[0][:, keys], start=False, stop=False)
                pe.matmul(out, r, krT[1][:, keys], start=False, stop=True).then_inc(s_full, 1)

            def transpose_probs(n, c):
                k0, w = SB[c]
                wait_bank(n + c, 0 if c == 0 else 1)
                for i in range(w // P):
                    ins = pe.transpose(tb[c % 2][:, i * P:(i + 1) * P], prob[:, k0 + i * P:k0 + (i + 1) * P], ident[:, :])
                ins.then_inc(b_full, 1)

            def output(n, st):
                pe.wait_ge(o_ready, st + 1)
                for c, (k0, w) in enumerate(SB):
                    pe.wait_ge(b_free, n + c + 1)
                    for i in range(c * KPB, c * KPB + w // P):
                        pe.matmul(o_ps[:, 0:2 * VD], pT[0][:, i, :], v[:, i, :, :].rearrange("p s d -> p (s d)"),
                                  start=(i == 0), stop=False)
                        ins = pe.matmul(o_ps[:, 0:VD], pT[1][:, i, :], v[:, i, 0, :], start=False, stop=(i == KT - 1))
                ins.then_inc(o_full, 1)

            def head(h, last):
                values(head_fill(h, F_V), 0)
                pe.wait_ge(b_free, head_fill(h, F_V) + VF)
                for c in range(NS):
                    scores(h, 0, h * NT, c)
                with pe.Fori(1, NT) as t:
                    n = head_fill(h, F_T) + (t - 1) * NS
                    for c in range(NS):
                        scores(h, t, h * NT + t, c)
                        transpose_probs(n, c)
                    output(n, h * NT + t - 1)
                n = head_fill(h, F_QK)
                if not last:
                    queries_keys(h + 1, n, 0)
                    n = head_fill(h, F_LAST)
                pe.wait_ge(s_free, (h * NT + NT + 1) * NS)
                for c in range(NS):
                    transpose_probs(n, c)
                output(n, h * NT + NT - 1)

            queries_keys(0, 0, 0)
            with pe.Fori(0, LAST) as h:
                head(h, False)
            head(LAST, True)


SLOTS = SEQ
PBLK = SLOTS // BLK
LAST_BLOCK = SEQ * TOPK // BLK + EXPERTS - 2
NBMAX = LAST_BLOCK + 5
BIG = 1e30
KNEG, IOTA, EOFF, THR, NCONST = 0, NBMAX, 2 * NBMAX, 2 * NBMAX + EXPERTS, 2 * NBMAX + EXPERTS + PBLK
SLOT_OF, BLOCKS_OF, FIRST_OF, NTABLE = 0, NBMAX, NBMAX + EXPERTS, NBMAX + 2 * EXPERTS


def route(nc, io, keep):
    ctx = ExitStack()
    with ctx:
        sb = lambda name, shape, dt=F32: ctx.enter_context(nc.sbuf_tensor(f"route_{name}", shape, dt))
        sem = lambda name: ctx.enter_context(nc.semaphore(f"route_{name}"))
        ident, g2b = keep["ident"], keep["g2b"]

        w_st = sb("w_st", [P, DC, D])
        w_o = [sb(f"w_o{s}", [P, DC, D], F16) for s in ("hi", "lo")]
        w_r = sb("w_r", [P, DC, 4 + EXPERTS])
        b_r = sb("b_r", [P, 4 + EXPERTS])
        at = sb("at", [P, 2, D])
        xt = sb("xt", [P, 2, D])
        aT = [sb(f"aT{s}", [P, 2, DC, P], F16) for s in ("hi", "lo")]
        yg = sb("yg", [P, D])
        x1 = sb("x1_t", [P, 2, D])
        h2 = sb("h2_t", [P, 2, D])
        h2T = sb("h2T", [P, 2, DC, P])
        sq = sb("sq", [P, D], BF16)
        g1b = sb("g1b", [P, D])
        A2b = sb("A2b", [P, D])
        B2b = sb("B2b", [P, D])
        rowb = sb("rowb", [P, 4, D])
        n2b = sb("n2b", [P, D])
        ss = sb("ss", [P, 2])
        rms = sb("rms", [P, 2])
        small = sb("small", [P, 8])
        eps_t = sb("eps_t", [P, 1])
        cst = sb("cst", [P, NCONST])
        tri = sb("tri", [P, P], F16)
        tri_f = sb("tri_f", [P, P])
        ones = sb("ones", [P, P], F16)
        tok = sb("tok", [P, TOPK, NT, 2], I32)
        lg = sb("lg", [P, NT, 4 + EXPERTS])

        w = {n: sb("r_" + n, shape, dt) for n, shape, dt in (
            ("dest_i", [P, TOPK * NT], I32), ("dest", [P, TOPK * NT], F32), ("ex", [P, NT, 5], F32),
            ("M", [P, NT, EXPERTS], F16), ("M1", [P, NT, EXPERTS], F16), ("M2", [P, NT, EXPERTS], F16),
            ("per_row", [P, 7 * NT], F32), ("eq", [P, NT, PER_GROUP], F32), ("ohg", [P, NT, GROUPS_E], F32),
            ("sel", [P, NT, PER_GROUP], F32), ("oh1", [P, NT, PER_GROUP], F32), ("oh2", [P, NT, PER_GROUP], F32),
            ("big", [P, NT * EXPERTS], F32), ("big2", [P, NBMAX * EXPERTS], F32), ("rank", [P, NT, EXPERTS], F32),
            ("per_e", [P, 3, EXPERTS], F32), ("tab_f", [P, 2, NBMAX], F32))}

        tb = [ctx.enter_context(nc.psum_tensor(f"route_rt{i}", [P, BANK], F32)) for i in range(2)]
        y_ps = [ctx.enter_context(nc.psum_tensor(f"route_y_ps{i}", [P, D], F32)) for i in range(2)]
        lg_ps = [ctx.enter_context(nc.psum_tensor(f"route_lg_ps{i}", [P, BANK], F32)) for i in range(2)]

        w_in = [sem(f"w_in{i}") for i in range(2)]
        small_in = sem("small_in")
        w_hi = sem("w_hi")
        w_ready = sem("w_ready")
        at_in = [sem(f"at_in{i}") for i in range(2)]
        xt_in = [sem(f"xt_in{i}") for i in range(2)]
        rows_ready = sem("rows_ready")
        t_full = sem("t_full")
        t_hi = sem("t_hi")
        t_free = [sem(f"t_free{i}") for i in range(2)]
        aT_ready = sem("aT_ready")
        y_full = sem("y_full")
        x1_ready = sem("x1_ready")
        rms_ready = sem("rms_ready")
        sq_done = sem("sq_done")
        h2_ready = sem("h2_ready")
        h2T_ready = sem("h2T_ready")
        lg_full = sem("lg_full")
        lg_ready = sem("lg_ready")
        x1_out = [sem(f"x1_out{i}") for i in range(2)]
        h2_out = [sem(f"h2_out{i}") for i in range(2)]
        dve_step = sem("dve_step")
        sp_passed = sem("sp_passed")
        slots_empty = sem("slots_empty")
        exp_in = sem("exp_in")
        exp_out = sem("exp_out")
        m_ready = sem("m_ready")
        rank_full = sem("rank_full")
        dest_ready = sem("dest_ready")
        slots_out = sem("slots_out")

        def at_fill(n):
            return 2 * n if isinstance(n, int) and n < 2 else 4 * n - 4

        def h2_fill(n):
            if isinstance(n, int) and n >= NT - 2:
                return 4 * NT - 4 + 2 * (n - NT + 2)
            return 4 * n + 6

        mod_b = io["mod_b"].rearrange("(a n) -> a n", a=1)
        block = ctx.enter_context(nc.Block())

        @block.sync
        def _(sp):
            sp.dma_start(at[:, 0, :], io["attn"][0:P, :]).then_inc(at_in[0], 16)
            w_v = io["w_o"].rearrange("(k p) n -> p k n", p=P)
            for i in range(2):
                sp.dma_start(w_st[:, 4 * i:4 * i + 4, :], w_v[:, 4 * i:4 * i + 4, :]).then_inc(w_in[i], 16)
            sp.dma_start(at[:, 1, :], io["attn"][P:2 * P, :]).then_inc(at_in[1], 16)
            for i, dst in enumerate((g1b, B2b, A2b, g2b)):
                sp.dma_start(dst[:, :], io["mod_rows"][:, i * D:(i + 1) * D].broadcast_to([P, D])).then_inc(small_in, 16)
                sp.dma_start(rowb[:, i, :], mod_b[:, (i + 2) * D:(i + 3) * D].broadcast_to([P, D])).then_inc(small_in, 16)
            sp.dma_start(n2b[:, :], io["norm2_g"].rearrange("(a n) -> a n", a=1).broadcast_to([P, D])).then_inc(small_in, 16)
            for n in range(2):
                sp.dma_start(xt[:, n, :], io["xc"][n * P:(n + 1) * P, :]).then_inc(xt_in[n], 16)
            sp.dma_start(b_r[:, :], io["b_r"].rearrange("(a n) -> a n", a=1).broadcast_to([P, 4 + EXPERTS])).then_inc(small_in, 16)
            sp.dma_start(w_r[:, :, :], io["w_r"].rearrange("(k p) n -> p k n", p=P)).then_inc(small_in, 16)
            sp.dma_start(cst[:, :], io["row_consts"].broadcast_to([P, NCONST])).then_inc(small_in, 16)
            sp.dma_start(tri_f[:, :], io["tri"]).then_inc(small_in, 16)
            sp.dma_start(tok[:, :, :, :], io["tok"]).then_inc(small_in, 16)
            sp.dma_start(io["slots"].rearrange("(p n) o -> p (n o)", p=P), io["empty_slots"]).then_inc(slots_empty, 16)

            def rows(n):
                return ds(n * P, P) if not isinstance(n, int) else slice(n * P, (n + 1) * P)

            def load_attn(n, par):
                wait_alone(sp, t_full, at_fill(n - 2) + 2, sp_passed)
                sp.dma_start(at[:, par, :], io["attn"][rows(n), :]).then_inc(at_in[par], 16)

            def store_x1(n, par):
                wait_alone(sp, x1_ready, n + 1, sp_passed)
                sp.dma_start(io["x1"][rows(n), :], x1[:, par, :]).then_inc(x1_out[par], 16)

            def load_x(n, par):
                sp.dma_start(xt[:, par, :], io["xc"][rows(n), :]).then_inc(xt_in[par], 16)

            def store_h2(n, par):
                wait_alone(sp, h2_ready, n + 1, sp_passed)
                sp.dma_start(io["h2"][rows(n), :], h2[:, par, :]).then_inc(h2_out[par], 16)

            def step(t, par, attn=True, x=True):
                if attn:
                    load_attn(t + 2, par)
                store_x1(t - 1, 1 - par)
                if x:
                    load_x(t + 1, 1 - par)
                store_h2(t - 1, 1 - par)

            load_attn(2, 0)
            step(1, 1)
            with sp.Fori(0, (NT - 4) // 2) as i:
                step(2 * i + 2, 0)
                step(2 * i + 3, 1)
            step(NT - 2, 0, attn=False)
            step(NT - 1, 1, attn=False, x=False)
            step(NT, 0, attn=False, x=False)
            for i in range(2):
                sp.wait_ge(x1_out[i], 8 * NT)
                sp.wait_ge(h2_out[i], 8 * NT)

        @block.gpsimd
        def _(pool):
            pool.wait_ge(slots_empty, 16)
            pool.wait_ge(small_in, 16 * 14)
            for k in range(TOPK):
                pool.wait_ge(dest_ready, k + 1)
                for t in range(NT):
                    pool.indirect_dma_start(io["slots"], bass.IndirectOffsetOnAxis(ap=w["dest_i"][:, k * NT + t:k * NT + t + 1], axis=0),
                                            tok[:, k, t, :], None).then_inc(slots_out, 16)
            pool.wait_ge(slots_out, 16 * TOPK * NT)

        @block.scalar
        def _(act):
            act.preload_act_table(ACT.Sqrt)
            for i in range(2):
                act.wait_ge(w_in[i], 16)
                act.activation(w_o[0][:, 4 * i:4 * i + 4, :], w_st[:, 4 * i:4 * i + 4, :], ACT.Copy, scale=WS).then_inc(w_hi, 1)

            def attn_hi(n, par):
                for i in range(2):
                    act.wait_ge(t_full, at_fill(n) + i + 1)
                    act.activation(aT[0][:, par, 4 * i:4 * i + 4, :], tb[i][:, :].rearrange("p (k t) -> p k t", k=4),
                                   ACT.Copy).then_inc(t_hi, 1)

            def norm(n, par):
                act.wait_ge(x1_ready, n + 1)
                act.activation(sq[:, :], x1[:, par, :], ACT.Square, accum_out=ss[:, par:par + 1]).then_inc(sq_done, 1)
                act.wait_ge(sq_done, n + 1)
                act.activation(rms[:, par:par + 1], ss[:, par:par + 1], ACT.Sqrt, bias=eps_t[:, :], scale=1.0 / D).then_inc(rms_ready, 1)

            def h2_copies(n, par):
                for i in range(2):
                    act.wait_ge(t_full, h2_fill(n) + i + 1)
                    act.activation(h2T[:, par, 4 * i:4 * i + 4, :], tb[i][:, :].rearrange("p (k t) -> p k t", k=4),
                                   ACT.Copy).then_inc(t_free[i], 1)

            def step(t, par):
                attn_hi(t + 1, 1 - par)
                norm(t - 1, 1 - par)
                h2_copies(t - 1, 1 - par)

            attn_hi(0, 0)
            attn_hi(1, 1)
            act.wait_ge(rows_ready, 1)
            with act.Fori(0, (NT - 2) // 2) as i:
                step(2 * i + 1, 1)
                step(2 * i + 2, 0)
            for n in (NT - 2, NT - 1):
                norm(n, n % 2)
                h2_copies(n, n % 2)
            act.preload_act_table(ACT.Exp)
            act.wait_ge(exp_in, 1)
            act.activation(w["ex"][:, :, :], w["ex"][:, :, :], ACT.Exp).then_inc(exp_out, 1)

        @block.vector
        def _(dve):
            step = Steps(dve, dve_step)
            dve.memset(eps_t[:, :], EPS)
            step.did(dve.memset(ones[:, :], 1.0))
            for i in range(2):
                dve.wait_ge(w_hi, i + 1)
                c = slice(4 * i, 4 * i + 4)
                dve.scalar_tensor_tensor(out=w_o[1][:, c, :], in0=w_st[:, c, :], scalar=WS, in1=w_o[0][:, c, :],
                                         op0=ALU.mult, op1=ALU.subtract).then_inc(w_ready, 1)

            def attn_lo(n, par):
                for i in range(2):
                    dve.wait_ge(t_hi, 2 * n + i + 1)
                    dve.tensor_tensor(aT[1][:, par, 4 * i:4 * i + 4, :], tb[i][:, :].rearrange("p (k t) -> p k t", k=4),
                                      aT[0][:, par, 4 * i:4 * i + 4, :], ALU.subtract).then_inc(t_free[i], 1)

            attn_lo(0, 0)
            attn_lo(1, 1)
            dve.wait_ge(small_in, 16 * 14)
            for i, dst in enumerate((g1b, B2b, A2b, g2b)):
                step.did(dve.tensor_tensor(dst[:, :], dst[:, :], rowb[:, i, :], ALU.add))
            step.did(dve.tensor_copy(tri[:, :], tri_f[:, :]))
            step.settle()
            step.did(dve.tensor_scalar(g1b[:, :], g1b[:, :], 1 / WS, None, ALU.mult))
            dve.scalar_tensor_tensor(out=A2b[:, :], in0=A2b[:, :], scalar=1.0, in1=n2b[:, :], op0=ALU.add, op1=ALU.mult).then_inc(rows_ready, 1)
            step.settle()
            dve.wait_ge(rows_ready, 1)

            def residual(n, par):
                dve.wait_ge(y_full, n + 1)
                step.did(dve.tensor_tensor(yg[:, :], y_ps[par][:, :], g1b[:, :], ALU.mult))
                dve.wait_ge(xt_in[par], 8 * (n - par) + 16)
                if not (isinstance(n, int) and n < 2):
                    dve.wait_ge(x1_out[par], 8 * (n - par))
                step.settle()
                dve.tensor_tensor(x1[:, par, :], yg[:, :], xt[:, par, :], ALU.add).then_inc(x1_ready, 1)

            def norm(n, par):
                r, m, u, v = (small[:, 4 * par + i:4 * par + i + 1] for i in range(4))
                dve.wait_ge(rms_ready, n + 1)
                step.did(dve.reciprocal(r, rms[:, par:par + 1]))
                step.did(dve.tensor_scalar(m, ss[:, par:par + 1], 1.0 / D, EPS, ALU.mult, ALU.add))
                step.settle()
                step.did(dve.scalar_tensor_tensor(out=u, in0=r, scalar=r, in1=m, op0=ALU.mult, op1=ALU.mult))
                step.settle()
                step.did(dve.tensor_scalar(v, u, -0.5, 1.5, ALU.mult, ALU.add))
                step.settle()
                step.did(dve.tensor_tensor(u, r, v, ALU.mult))
                if not (isinstance(n, int) and n < 2):
                    dve.wait_ge(h2_out[par], 8 * (n - par))
                step.settle()
                step.did(dve.scalar_tensor_tensor(out=h2[:, par, :], in0=x1[:, par, :], scalar=u, in1=A2b[:, :], op0=ALU.mult, op1=ALU.mult))
                step.settle()
                dve.tensor_tensor(h2[:, par, :], h2[:, par, :], B2b[:, :], ALU.add).then_inc(h2_ready, 1)

            def logits(n, par):
                dve.wait_ge(lg_full, n + 1)
                dst = lg[:, ds(n, 1), :].rearrange("p a n -> p (a n)") if not isinstance(n, int) else lg[:, n, :]
                dve.tensor_tensor(dst, lg_ps[par][:, 0:4 + EXPERTS], b_r[:, :], ALU.add).then_inc(lg_ready, 1)

            def body(t, par):
                residual(t - 1, 1 - par)
                attn_lo(t + 1, 1 - par)
                norm(t - 1, 1 - par)
                logits(t - 1, 1 - par)

            PER = 7
            body(1, 1)
            body(2, 0)
            with dve.Fori(1, (NT - 2) // 2) as i:
                step.enter((i - 1) * (2 * PER), 2 * PER)
                body(2 * i + 1, 1)
                body(2 * i + 2, 0)
            step.leave((NT - 2) // 2 - 1)
            for n in (NT - 2, NT - 1):
                residual(n, n % 2)
                norm(n, n % 2)
                logits(n, n % 2)
            dve.wait_ge(lg_ready, NT)
            slots_of_tokens(dve, step, lg, cst, keep, w, dict(
                exp_in=exp_in, exp_out=exp_out, m_ready=m_ready, rank_full=rank_full, dest_ready=dest_ready), y_ps)

        @block.tensor
        def _(pe):
            def transposes(src, fill0, count, first=False):
                for i in range(2):
                    if not first:
                        pe.wait_ge(t_free[i], count)
                    for u in range(4):
                        k = 4 * i + u
                        ins = pe.transpose(tb[i][:, u * P:(u + 1) * P], src[:, k * P:(k + 1) * P], ident[:, :])
                    ins.then_inc(t_full, 1)

            def attn_T(n, par, first=False):
                pe.wait_ge(at_in[par], 8 * (n - par) + 16)
                f = at_fill(n)
                transposes(at[:, par, :], f, n if isinstance(n, int) and n < 2 else 2 * n - 2, first)

            def product(n, par):
                pe.wait_ge(t_free[1], n + 1 if isinstance(n, int) and n < 2 else 2 * n - 1)
                pe.wait_ge(t_free[0], n + 1 if isinstance(n, int) and n < 2 else 2 * n - 1)
                if not (isinstance(n, int) and n < 2):
                    pe.wait_ge(x1_ready, n - 1)
                for k in range(DC):
                    for c in range(2):
                        ins = three_pass(pe, y_ps[par][:, c * BANK:(c + 1) * BANK], [t[:, par, k, :] for t in aT],
                                         [t[:, k, c * BANK:(c + 1) * BANK] for t in w_o], k == 0, k == DC - 1)
                ins.then_inc(y_full, 1)

            def router(n, par):
                pe.wait_ge(h2_ready, n + 1)
                late = isinstance(n, int) and n >= NT - 2
                cnt = (2 * NT - 2 + (n - NT + 2)) if late else 2 * n + 3
                transposes(h2[:, par, :], h2_fill(n), cnt)
                for i in range(2):
                    pe.wait_ge(t_free[i], cnt + 1)
                if not (isinstance(n, int) and n < 2):
                    pe.wait_ge(lg_ready, n - 1)
                for k in range(DC):
                    ins = pe.matmul(lg_ps[par][:, 0:4 + EXPERTS], h2T[:, par, k, :], w_r[:, k, :], start=(k == 0), stop=(k == DC - 1))
                ins.then_inc(lg_full, 1)

            pe.wait_ge(small_in, 16 * 14)
            attn_T(0, 0, first=True)
            attn_T(1, 1)
            pe.wait_ge(w_ready, 2)
            product(0, 0)

            def step(t, par):
                attn_T(t + 1, 1 - par)
                product(t, par)
                router(t - 1, 1 - par)

            step(1, 1)
            step(2, 0)
            with pe.Fori(1, (NT - 2) // 2) as i:
                step(2 * i + 1, 1)
                step(2 * i + 2, 0)
            product(NT - 1, 1)
            router(NT - 2, 0)
            router(NT - 1, 1)
            M = w["M"]
            pe.wait_ge(m_ready, 1)
            pe.matmul(y_ps[0][:, 0:BANK], tri[:, :], M[:, :, :].rearrange("p t e -> p (t e)"), start=True, stop=False)
            for t in range(NT - 1):
                ins = pe.matmul(y_ps[0][:, (t + 1) * EXPERTS:NT * EXPERTS].rearrange("p (t e) -> p t e", e=EXPERTS), ones[:, :],
                                M[:, t:t + 1, :].broadcast_to([P, NT - 1 - t, EXPERTS]), start=False, stop=(t == NT - 2))
            for t in range(NT):
                ins = pe.matmul(y_ps[1][:, 0:EXPERTS], ones[:, :], M[:, t, :], start=(t == 0), stop=(t == NT - 1))
            ins.then_inc(rank_full, 1)


def slots_of_tokens(dve, step, lg, cst, keep, w, s, y_ps):
    PG, E = PER_GROUP, EXPERTS
    iota = lambda o, n: cst[:, o:o + n]
    W = w["per_row"]
    gm, gi, e1, e2, i1, i2, z = (W[:, NT * i:NT * (i + 1)] for i in range(7))
    b3 = lambda a, n: a.unsqueeze(2).broadcast_to([P, NT, n])
    row3 = lambda o, n: iota(o, n).unsqueeze(1).broadcast_to([P, NT, n])
    G4 = lg[:, :, 0:4]
    eq, ohg, sel, oh1, oh2 = w["eq"], w["ohg"], w["sel"], w["oh1"], w["oh2"]
    M1, M2, M, big = w["M1"], w["M2"], w["M"], w["big"]
    ex = w["ex"]

    def first_max(src, n, m, idx, onehot):
        step.did(dve.tensor_reduce(m, src, AX.X, ALU.max))
        step.settle()
        step.did(dve.tensor_tensor(eq[:, :, 0:n], src, b3(m, n), ALU.is_equal))
        step.settle()
        step.did(dve.tensor_tensor(eq[:, :, 0:n], eq[:, :, 0:n], row3(KNEG, n), ALU.mult))
        step.settle()
        step.did(dve.tensor_reduce(idx, eq[:, :, 0:n], AX.X, ALU.min))
        step.settle()
        step.did(dve.tensor_tensor(onehot, b3(idx, n), row3(KNEG, n), ALU.is_equal))
        step.settle()

    first_max(G4, 4, gm, gi, ohg[:, :, :])
    g4 = big[:, :].rearrange("p (t g i) -> p t g i", g=4, i=PG)
    step.did(dve.tensor_tensor(g4, lg[:, :, 4:4 + E].rearrange("p t (g i) -> p t g i", g=4),
                               ohg[:, :, :].unsqueeze(3).broadcast_to([P, NT, 4, PG]), ALU.mult))
    step.settle()
    step.did(dve.tensor_reduce(sel[:, :, :], g4.rearrange("p t g i -> p t i g"), AX.X, ALU.add))
    step.settle()
    first_max(sel[:, :, :], PG, e1, i1, oh1[:, :, :])
    step.did(dve.scalar_tensor_tensor(out=sel[:, :, :], in0=oh1[:, :, :], scalar=-BIG, in1=sel[:, :, :], op0=ALU.mult, op1=ALU.add))
    step.settle()
    first_max(sel[:, :, :], PG, e2, i2, oh2[:, :, :])
    for m, oh in ((M1, oh1), (M2, oh2)):
        step.did(dve.tensor_tensor(m[:, :, :].rearrange("p t (g i) -> p t g i", g=4), ohg[:, :, :].unsqueeze(3).broadcast_to([P, NT, 4, PG]),
                                   oh[:, :, :].unsqueeze(2).broadcast_to([P, NT, 4, PG]), ALU.mult))
    step.settle()
    dve.tensor_tensor(M[:, :, :], M1[:, :, :], M2[:, :, :], ALU.add).then_inc(s["m_ready"], 1)
    step.did(dve.tensor_tensor(ex[:, :, 0:4], G4, b3(gm, 4), ALU.subtract))
    step.did(dve.tensor_tensor(ex[:, :, 4], e2, e1, ALU.subtract))
    step.settle()
    dve.nop().then_inc(s["exp_in"], 1)
    dve.wait_ge(s["rank_full"], 1)
    rank = w["rank"]
    step.did(dve.tensor_tensor(rank[:, :, :], y_ps[0][:, 0:NT * E].rearrange("p (t e) -> p t e", e=E), row3(EOFF, E), ALU.add))
    step.settle()
    dest = w["dest"]
    b4 = big[:, :].rearrange("p (t e) -> p t e", e=E)
    for k, m in enumerate((M1, M2)):
        step.did(dve.tensor_tensor(b4, rank[:, :, :], m[:, :, :], ALU.mult))
        step.settle()
        step.did(dve.tensor_reduce(dest[:, k * NT:(k + 1) * NT], b4, AX.X, ALU.add))
        step.settle()
        dve.tensor_copy(w["dest_i"][:, k * NT:(k + 1) * NT], dest[:, k * NT:(k + 1) * NT]).then_inc(s["dest_ready"], 1)
    cnt, nb, be = (w["per_e"][:, i, :] for i in range(3))
    step.did(dve.tensor_copy(cnt, y_ps[1][:, 0:E]))
    step.settle()
    big2 = w["big2"]
    v = big2[:, 0:E * PBLK].rearrange("p (e m) -> p e m", m=PBLK)
    step.did(dve.tensor_tensor(v, cnt.unsqueeze(2).broadcast_to([P, E, PBLK]),
                               iota(THR, PBLK).unsqueeze(1).broadcast_to([P, E, PBLK]), ALU.is_gt))
    step.settle()
    step.did(dve.tensor_reduce(nb, v, AX.X, ALU.add))
    step.settle()
    step.did(dve.tensor_scalar(nb, nb, 1.0, None, ALU.max))
    step.settle()
    v = big2[:, 0:E * E].rearrange("p (e m) -> p e m", m=E)
    ie = iota(IOTA, E)
    step.did(dve.tensor_tensor(v, ie.unsqueeze(1).broadcast_to([P, E, E]), ie.unsqueeze(2).broadcast_to([P, E, E]), ALU.is_le))
    step.settle()
    step.did(dve.tensor_tensor(v, v, nb.unsqueeze(1).broadcast_to([P, E, E]), ALU.mult))
    step.settle()
    step.did(dve.tensor_reduce(be, v, AX.X, ALU.add))
    step.settle()
    v = big2[:, :].rearrange("p (j e) -> p j e", e=E)
    ends = be.unsqueeze(1).broadcast_to([P, NBMAX, E])
    tab_f = w["tab_f"]
    step.did(dve.tensor_tensor(v, ends, iota(IOTA, NBMAX).unsqueeze(2).broadcast_to([P, NBMAX, E]), ALU.is_le))
    step.settle()
    step.did(dve.tensor_reduce(tab_f[:, 0, :], v, AX.X, ALU.add))
    step.settle()
    step.did(dve.tensor_tensor(v, v, ends, ALU.mult))
    step.settle()
    step.did(dve.tensor_reduce(tab_f[:, 1, :], v, AX.X, ALU.max))
    step.did(dve.tensor_scalar(tab_f[:, 0, :], tab_f[:, 0, :], float(E - 1), None, ALU.min))
    step.settle()
    step.did(dve.tensor_tensor(tab_f[:, 1, :], iota(IOTA, NBMAX), tab_f[:, 1, :], ALU.subtract))
    step.settle()
    step.did(dve.tensor_scalar(tab_f[:, 1, :], tab_f[:, 1, :], float(BLK), None, ALU.mult))
    step.settle()
    step.did(dve.scalar_tensor_tensor(out=tab_f[:, 1, :], in0=tab_f[:, 0, :], scalar=float(SLOTS), in1=tab_f[:, 1, :], op0=ALU.mult, op1=ALU.add))
    step.settle()
    step.did(dve.tensor_scalar(tab_f[:, 1, :], tab_f[:, 1, :], float(E * SLOTS - BLK), None, ALU.min))
    step.settle()
    step.did(dve.tensor_tensor(be, be, nb, ALU.subtract))
    step.settle()
    for o, src in ((SLOT_OF, tab_f[:, 1, :]), (BLOCKS_OF, nb), (FIRST_OF, be)):
        step.did(dve.tensor_copy(keep["tables"][:, o:o + src.shape[1]], src))
    dve.wait_ge(s["exp_out"], 1)
    t_ = ex[:, :, 4]
    g1, g2 = keep["gates"][:, 0:NT], keep["gates"][:, NT:2 * NT]
    step.did(dve.tensor_reduce(z, ex[:, :, 0:4], AX.X, ALU.add))
    step.settle()
    step.did(dve.scalar_tensor_tensor(out=z, in0=t_, scalar=1.0, in1=z, op0=ALU.add, op1=ALU.mult))
    step.settle()
    step.did(dve.reciprocal(g1, z))
    step.settle()
    step.did(dve.tensor_tensor(g2, t_, g1, ALU.mult))
    step.settle()


def experts(nc, io, keep):
    ctx = ExitStack()
    with ctx:
        sb = lambda name, shape, dt=F32: ctx.enter_context(nc.sbuf_tensor(f"experts_{name}", shape, dt))
        sem = lambda name: ctx.enter_context(nc.semaphore(f"experts_{name}"))
        bank = lambda name: ctx.enter_context(nc.psum_tensor(f"experts_{name}", [P, BANK], F32))
        ident, tables = keep["ident"], keep["tables"]

        raw = {"gate": sb("gate_raw", [P, DC, FF]), "up": sb("up_raw", [P, DC, FF]), "down": sb("down_raw", [P, FC, D])}
        w = {n: [sb(f"{n}_{s}", [P, 2] + list(r.shape[1:]), F16) for s in ("hi", "lo")] for n, r in raw.items()}
        src = {n: io[f"w_{n}"] for n in raw}
        slots = sb("slots", [P, NTABLE, 2], I32)
        source = sb("source", [P, 1], I32)
        target = sb("target", [P, 1], I32)
        xe = sb("xe", [P, D])
        xT = [sb(f"xT{s}", [P, DC, P], F16) for s in ("hi", "lo")]
        act_g = sb("act_g", [P, FF])
        hid = sb("hid", [P, FF])
        hidT = [sb(f"hidT{s}", [P, FC, P], F16) for s in ("hi", "lo")]
        y_out = sb("y_out", [P, D])

        g_ps, u_ps, h_ps = bank("g_ps"), bank("u_ps"), bank("h_ps")
        x_ps = [bank(f"x_ps{i}") for i in range(2)]
        y_ps = [bank(f"ye_ps{i}") for i in range(2)]

        w_in = {n: sem(f"{n}_in") for n in raw}
        w_hi = {n: sem(f"{n}_hi") for n in raw}
        w_ready = {n: sem(f"{n}_ready") for n in raw}
        slots_in = sem("slots_in")
        picked = sem("picked")
        y_gone = sem("y_gone")
        xe_in = sem("xe_in")
        x_full = sem("x_full")
        x_hi = sem("x_hi")
        x_ready = sem("x_ready")
        g_full = sem("g_full")
        act_ready = sem("act_ready")
        u_full = sem("u_full")
        hid_ready = sem("hid_ready")
        h_full = sem("h_full")
        h_hi = sem("h_hi")
        h_ready = sem("h_ready")
        y_full = sem("y_full")
        y_left = sem("y_left")
        y_right = sem("y_right")
        y_stored = sem("y_stored")
        sp_passed = sem("sp_passed")
        pool_passed = sem("pool_passed")

        def over_experts(eng, first, body, before=None):
            first()

            def one(e, par, last):
                if before:
                    before(e, par, last)
                index = lambda o: tables[0:1, ds(o + e, 1)] if not isinstance(e, int) else tables[0:1, o + e:o + e + 1]
                count = eng.value_load(index(BLOCKS_OF), min_val=1, max_val=PBLK)
                start = eng.value_load(index(FIRST_OF), min_val=0, max_val=LAST_BLOCK)
                body(e, par, count, start, last)

            with eng.Fori(0, EXPERTS // 2 - 1) as ee:
                one(2 * ee, 0, False)
                one(2 * ee + 1, 1, False)
            one(EXPERTS - 2, 0, False)
            one(EXPERTS - 1, 1, True)

        halves = {n: (slice(0, r.shape[1] // 2), slice(r.shape[1] // 2, r.shape[1])) for n, r in raw.items()}
        SPLIT_A = (("gate", 0), ("gate", 1), ("up", 0))
        SPLIT_B = (("up", 1), ("down", 0), ("down", 1))
        block = ctx.enter_context(nc.Block())

        @block.sync
        def _(sp):
            def load(n, e):
                s = src[n][ds(e, 1)] if not isinstance(e, int) else src[n][e:e + 1]
                sp.dma_start(raw[n][:, :, :], s.rearrange("a (k p) n -> p (a k) n", p=P)).then_inc(w_in[n], 16)

            def first():
                for n in raw:
                    load(n, 0)
                for n in raw:
                    sp.wait_ge(w_ready[n], 2)
                    load(n, 1)

            first()
            with sp.Fori(0, EXPERTS - 2) as e:
                for n in raw:
                    wait_alone(sp, w_ready[n], 2 * e + 4, sp_passed)
                    load(n, e + 2)

        @block.gpsimd
        def _(pool):
            def load_slots(j):
                slot = pool.value_load(tables[0:1, ds(SLOT_OF + j, 1)] if not isinstance(j, int) else tables[0:1, j:j + 1],
                                       min_val=0, max_val=EXPERTS * SLOTS - BLK)
                dst = slots[:, ds(j, 1), :] if not isinstance(j, int) else slots[:, j:j + 1, :]
                pool.dma_start(dst.rearrange("p a n -> p (a n)"), io["slots"][ds(slot, BLK), :]).then_inc(slots_in, 16)

            def pick(dst, j, column, n):
                src = slots[:, ds(j, 1), column] if not isinstance(j, int) else slots[:, j:j + 1, column]
                pool.tensor_copy(dst[:, :], src).then_inc(picked, 1)
                wait_alone(pool, picked, n + 1, pool_passed)

            def gather(j, n):
                pick(source, j, 0, n)
                pool.indirect_dma_start(xe[:, :], None, io["h2"], bass.IndirectOffsetOnAxis(ap=source[:, 0:1], axis=0)).then_inc(xe_in, 16)

            def first():
                for j in range(3):
                    load_slots(j)
                    pool.wait_ge(slots_in, 16 * j + 16)
                gather(0, 0)
                pool.wait_ge(x_full, 2)
                gather(1, 1)

            def body(e, par, count, start, last):
                with pool.Fori(0, count) as i:
                    j = start + i
                    load_slots(j + 3)
                    wait_alone(pool, x_full, 2 * j + 4, pool_passed)
                    wait_alone(pool, xe_in, 16 * j + 32, pool_passed)
                    gather(j + 2, 2 * j + 2)
                    pool.wait_ge(y_left, j + 2)
                    wait_alone(pool, y_right, j + 2, pool_passed)
                    pick(target, j, 1, 2 * j + 3)
                    pool.indirect_dma_start(io["y"], bass.IndirectOffsetOnAxis(ap=target[:, 0:1], axis=0), y_out[:, :], None).then_inc(y_stored, 16)
                    wait_alone(pool, y_stored, 16 * j + 16, pool_passed)
                    wait_alone(pool, slots_in, 16 * j + 64, y_gone)

            over_experts(pool, first, body)

        @block.scalar
        def _(act):
            act.sem_inc(y_left, 1)
            act.preload_act_table(ACT.Silu)

            def split(e, par, n, part):
                if part == 0:
                    act.wait_ge(w_in[n], 16 * e + 16)
                k = halves[n][part]
                act.activation(w[n][0][:, par, k, :], raw[n][:, k, :], ACT.Copy, scale=WS).then_inc(w_hi[n], 1)

            def rows_hi(j, i):
                act.wait_ge(x_full, 2 * j + i + 1)
                act.activation(xT[0][:, 4 * i:4 * i + 4, :], x_ps[i][:, :].rearrange("p (k t) -> p k t", k=4), ACT.Copy).then_inc(x_hi, 1)

            def first():
                for n, part in SPLIT_A + SPLIT_B:
                    split(0, 0, n, part)
                for i in range(2):
                    rows_hi(0, i)

            def before(e, par, last):
                if not last:
                    for n, part in SPLIT_A:
                        split(e + 1, 1 - par, n, part)

            def blk(j, more=None):
                act.wait_ge(g_full, j + 1)
                act.wait_ge(hid_ready, j + 1)
                act.activation(act_g[:, :], g_ps[:, :], ACT.Silu, scale=1 / WS).then_inc(act_ready, 1)
                rows_hi(j + 1, 0)
                act.wait_ge(h_full, j + 2)
                act.activation(hidT[0][:, :, :], h_ps[:, :].rearrange("p (k t) -> p k t", k=FC), ACT.Copy).then_inc(h_hi, 1)
                rows_hi(j + 1, 1)
                if more:
                    more()
                act.wait_ge(y_full, j + 2)
                act.wait_ge(y_gone, j + 1)
                act.activation(y_out[:, 0:BANK], y_ps[0][:, :], ACT.Copy, scale=1 / WS).then_inc(y_left, 1)

            def body(e, par, count, start, last):
                def more():
                    for n, part in SPLIT_B:
                        split(e + 1, 1 - par, n, part)
                blk(start, None if last else more)
                with act.If(count > 1):
                    with act.Fori(1, count) as k:
                        blk(start + k)

            act.sem_inc(y_gone, 1)
            over_experts(act, first, body, before)

        @block.vector
        def _(dve):
            for signal in (hid_ready, h_ready, y_right):
                dve.sem_inc(signal, 1)
            def split(e, par, n, part):
                dve.wait_ge(w_hi[n], 2 * e + part + 1)
                k = halves[n][part]
                dve.scalar_tensor_tensor(out=w[n][1][:, par, k, :], in0=raw[n][:, k, :], scalar=WS, in1=w[n][0][:, par, k, :],
                                         op0=ALU.mult, op1=ALU.subtract).then_inc(w_ready[n], 1)

            def rows_lo(j, i):
                dve.wait_ge(x_hi, 2 * j + i + 1)
                dve.tensor_tensor(xT[1][:, 4 * i:4 * i + 4, :], x_ps[i][:, :].rearrange("p (k t) -> p k t", k=4),
                                  xT[0][:, 4 * i:4 * i + 4, :], ALU.subtract).then_inc(x_ready, 1)

            def first():
                for n, part in SPLIT_A + SPLIT_B:
                    split(0, 0, n, part)
                for i in range(2):
                    rows_lo(0, i)

            def before(e, par, last):
                if not last:
                    for n, part in SPLIT_A:
                        split(e + 1, 1 - par, n, part)

            def blk(j, more=None):
                dve.wait_ge(u_full, j + 1)
                dve.wait_ge(act_ready, j + 1)
                dve.wait_ge(h_full, j + 1)
                dve.scalar_tensor_tensor(out=hid[:, :], in0=u_ps[:, :], scalar=1 / WS, in1=act_g[:, :],
                                         op0=ALU.mult, op1=ALU.mult).then_inc(hid_ready, 1)
                rows_lo(j + 1, 0)
                dve.wait_ge(h_hi, j + 1)
                dve.tensor_tensor(hidT[1][:, :, :], h_ps[:, :].rearrange("p (k t) -> p k t", k=FC), hidT[0][:, :, :],
                                  ALU.subtract).then_inc(h_ready, 1)
                rows_lo(j + 1, 1)
                if more:
                    more()
                dve.wait_ge(y_full, j + 2)
                dve.wait_ge(y_gone, j + 1)
                dve.tensor_scalar(y_out[:, BANK:D], y_ps[1][:, :], 1 / WS, None, ALU.mult).then_inc(y_right, 1)

            def body(e, par, count, start, last):
                def more():
                    for n, part in SPLIT_B:
                        split(e + 1, 1 - par, n, part)
                blk(start, None if last else more)
                with dve.If(count > 1):
                    with dve.Fori(1, count) as k:
                        blk(start + k)

            over_experts(dve, first, body, before)

        @block.tensor
        def _(pe):
            for signal in (y_full, h_full):
                pe.sem_inc(signal, 1)
            def transpose_rows(j, i):
                for u in range(4):
                    k = 4 * i + u
                    ins = pe.transpose(x_ps[i][:, u * P:(u + 1) * P], xe[:, k * P:(k + 1) * P], ident[:, :])
                ins.then_inc(x_full, 1)

            def first():
                pe.wait_ge(xe_in, 16)
                transpose_rows(0, 0)
                transpose_rows(0, 1)

            def body(e, par, count, start, last):
                with pe.Fori(0, count) as i:
                    j = start + i
                    pe.wait_ge(x_ready, 2 * j + 2)
                    pe.wait_ge(hid_ready, j + 1)
                    for n, out, full in (("gate", g_ps, g_full), ("up", u_ps, u_full)):
                        pe.wait_ge(w_ready[n], 2 * e + 2)
                        for k in range(DC):
                            ins = three_pass(pe, out[:, :], [t[:, k, :] for t in xT], [t[:, par, k, :] for t in w[n]], k == 0, k == DC - 1)
                        ins.then_inc(full, 1)
                    pe.wait_ge(xe_in, 16 * j + 32)
                    transpose_rows(j + 1, 0)
                    pe.wait_ge(hid_ready, j + 2)
                    for k in range(FC):
                        ins = pe.transpose(h_ps[:, k * P:(k + 1) * P], hid[:, k * P:(k + 1) * P], ident[:, :])
                    ins.then_inc(h_full, 1)
                    transpose_rows(j + 1, 1)
                    pe.wait_ge(h_hi, j + 1)
                    pe.wait_ge(y_left, j + 1)
                    pe.wait_ge(y_right, j + 1)
                    pe.wait_ge(w_ready["down"], 2 * e + 2)
                    for part, k, low in [(0, k, low) for k in range(FC) for low in range(2)] + [(1, k, 0) for k in range(FC)]:
                        if part == 1 and k == 0:
                            pe.wait_ge(h_ready, j + 2)
                        for c in range(2):
                            ins = pe.matmul(y_ps[c][:, :], hidT[part][:, k, :], w["down"][low][:, par, k, c * BANK:(c + 1) * BANK],
                                            start=(part == 0 and k == 0 and low == 0), stop=(part == 1 and k == FC - 1))
                    ins.then_inc(y_full, 1)

            over_experts(pe, first, body)


def combine(nc, io, keep):
    ctx = ExitStack()
    with ctx:
        sb = lambda name, shape, dt=F32: ctx.enter_context(nc.sbuf_tensor(f"combine_{name}", shape, dt))
        sem = lambda name: ctx.enter_context(nc.semaphore(f"combine_{name}"))
        gates, g2b = keep["gates"], keep["g2b"]
        ya = sb("ya", [P, 2, D])
        yb = sb("yb", [P, 2, D])
        xr = sb("xr", [P, 2, D])
        res = sb("res", [P, 2, D])
        sq = sb("sq", [P, D], BF16)
        fg = sb("fg", [P, D])
        ss = sb("ss", [P, 2])
        rms = sb("rms", [P, 2])
        rstd = sb("rstd", [P, 2])
        eps_t = sb("eps_t", [P, 1])


        fg_in = sem("fg_in")
        ya_in = [sem(f"ya_in{i}") for i in range(2)]
        yb_in = [sem(f"yb_in{i}") for i in range(2)]
        xr_in = [sem(f"xr_in{i}") for i in range(2)]
        out_done = [sem(f"out_done{i}") for i in range(2)]
        ya_scaled = sem("ya_scaled")
        x2_ready = sem("x2_ready")
        sq_done = sem("sq_done")
        rms_ready = sem("rms_ready")
        res_ready = sem("res_ready")
        eps_ready = sem("eps_ready")
        dve_step = sem("dve_step")
        sp_passed = sem("sp_passed")
        block = ctx.enter_context(nc.Block())

        @block.sync
        def _(sp):
            for signal in (out_done[0], out_done[1]):
                sp.sem_inc(signal, 1)
            sp.dma_start(fg[:, :], io["final_g"].rearrange("(a n) -> a n", a=1).broadcast_to([P, D])).then_inc(fg_in, 16)

            def load(t, par):
                rows = lambda o: ds(t * P + o, P) if not isinstance(t, int) else slice(t * P + o, t * P + o + P)
                sp.dma_start(ya[:, par, :], io["y"][rows(0), :]).then_inc(ya_in[par], 16)
                sp.dma_start(yb[:, par, :], io["y"][rows(SEQ), :]).then_inc(yb_in[par], 16)
                sp.dma_start(xr[:, par, :], io["x1"][rows(0), :]).then_inc(xr_in[par], 16)

            load(0, 0)
            load(1, 1)
            with sp.Fori(0, NT // 2 - 1) as i:
                for par in range(2):
                    t = 2 * i + par
                    wait_alone(sp, res_ready, t + 1, sp_passed)
                    sp.dma_start(io["out"][ds(t * P, P), :], res[:, par, :]).then_inc(out_done[par], 16)
                    load(t + 2, par)
            for t in (NT - 2, NT - 1):
                sp.wait_ge(res_ready, t + 1)
                sp.dma_start(io["out"][t * P:(t + 1) * P, :], res[:, t % 2, :]).then_inc(out_done[t % 2], 16)
            for par in range(2):
                sp.wait_ge(out_done[par], 8 * NT + 1)

        @block.scalar
        def _(act):
            act.sem_inc(rms_ready, 1)
            act.preload_act_table(ACT.Sqrt)
            act.wait_ge(eps_ready, 1)
            with act.Fori(0, NT // 2) as i:
                for par in range(2):
                    t = 2 * i + par
                    act.wait_ge(ya_in[par], 16 * i + 16)
                    act.activation(ya[:, par, :], ya[:, par, :], ACT.Copy, scale=gates[:, ds(t, 1)]).then_inc(ya_scaled, 1)
                    act.wait_ge(x2_ready, t + 1)
                    act.wait_ge(rms_ready, t + 1)
                    act.activation(sq[:, :], xr[:, par, :], ACT.Square, accum_out=ss[:, par:par + 1]).then_inc(sq_done, 1)
                    act.wait_ge(sq_done, t + 1)
                    act.activation(rms[:, par:par + 1], ss[:, par:par + 1], ACT.Sqrt, bias=eps_t[:, :], scale=1.0 / D).then_inc(rms_ready, 1)

        @block.vector
        def _(dve):
            step = Steps(dve, dve_step)
            dve.memset(eps_t[:, :], EPS).then_inc(eps_ready, 1)
            dve.wait_ge(fg_in, 16)
            PER = 5
            with dve.Fori(0, NT // 2) as i:
                step.enter(i * (2 * PER), 2 * PER)
                for par in range(2):
                    t = 2 * i + par
                    y = yb[:, par, :]
                    dve.wait_ge(ya_scaled, t + 1)
                    dve.wait_ge(yb_in[par], 16 * i + 16)
                    step.did(dve.scalar_tensor_tensor(out=y, in0=y, scalar=gates[:, ds(NT + t, 1)], in1=ya[:, par, :],
                                                      op0=ALU.mult, op1=ALU.add))
                    step.settle()
                    step.did(dve.tensor_tensor(y, y, g2b[:, :], ALU.mult))
                    dve.wait_ge(xr_in[par], 16 * i + 16)
                    step.settle()
                    step.did(dve.tensor_tensor(xr[:, par, :], xr[:, par, :], y, ALU.add))
                    step.settle()
                    dve.nop().then_inc(x2_ready, 1)
                    dve.wait_ge(rms_ready, t + 2)
                    step.did(dve.reciprocal(rstd[:, par:par + 1], rms[:, par:par + 1]))
                    dve.wait_ge(out_done[par], 16 * i + 1)
                    step.settle()
                    step.did(dve.scalar_tensor_tensor(out=res[:, par, :], in0=xr[:, par, :], scalar=rstd[:, par:par + 1],
                                                      in1=fg[:, :], op0=ALU.mult, op1=ALU.mult))
                    step.settle()
                    dve.nop().then_inc(res_ready, 1)
            step.leave(NT // 2)




def build(nc, io):
    scratch = lambda name, shape, dt=F32: nc.dram_tensor(name, shape, dt, kind="Internal").ap()
    io["mod_rows"] = scratch("mod_rows", (1, 4 * D))
    io["attn"] = scratch("attn", (SEQ, HEADS * VD))
    io["x1"] = scratch("x1", (SEQ, D))
    io["h2"] = scratch("h2", (SEQ, D))
    io["slots"] = scratch("slots", (EXPERTS * SLOTS, 2), I32)
    io["y"] = scratch("y", (TOPK * SEQ + BLK, D))
    with ExitStack() as whole:
        ident = whole.enter_context(nc.sbuf_tensor("ident", [P, P], F32))
        with ExitStack() as latents:
            sb = lambda name, shape: latents.enter_context(nc.sbuf_tensor(name, shape, F16))
            keep = {
                "ident": ident,
                "cqT": [sb(f"cqT_{s}", [P, RC, SEQ]) for s in ("hi", "lo")],
                "ckvT": [sb(f"ckvT_{s}", [P, KC, KEYS]) for s in ("hi", "lo")],
                "krT": [sb(f"krT_{s}", [P, KEYS]) for s in ("hi", "lo")],
                "qrT": sb("qrT", [P, HEADS, SEQ]),
            }
            project(nc, io, keep)
            attend(nc, io, keep)
        sb = lambda name, shape, dt=F32: whole.enter_context(nc.sbuf_tensor(name, shape, dt))
        keep = {"ident": ident, "g2b": sb("g2b", [P, D]), "gates": sb("gates", [P, TOPK * NT]),
                "tables": sb("tables", [P, NTABLE], I32)}
        route(nc, io, keep)
        experts(nc, io, keep)
        combine(nc, io, keep)


def rotary_tables():
    n = ROPE // 4
    freq = (np.float32(ROPE_THETA) ** (-np.arange(n, dtype=np.float32) / np.float32(n))).astype(np.float32)
    t = np.arange(SEQ)
    row, col = (t // GRID_W).astype(np.float32), (t % GRID_W).astype(np.float32)
    angle = np.concatenate([row[:, None] * freq, col[:, None] * freq], -1)
    tile = lambda a: np.ascontiguousarray(a.astype(np.float32).reshape(KT, P, HALF).transpose(1, 0, 2))
    return (tile(np.concatenate([np.cos(angle), np.ones((CTX, HALF))])),
            tile(np.concatenate([np.sin(angle), np.zeros((CTX, HALF))])))


def constants():
    cos, sin = rotary_tables()
    e, s = np.arange(EXPERTS), np.arange(EXPERTS * SLOTS // P)
    token = np.arange(SEQ, dtype=np.int32).reshape(NT, P).T
    return {
        "ident": np.eye(P, dtype=np.float32), "cos": cos, "sin": sin,
        "tri": np.triu(np.ones((P, P), np.float32), 1),
        "row_consts": np.concatenate([np.arange(NBMAX) - NBMAX, np.arange(NBMAX), e * SLOTS, np.arange(PBLK) * BLK])[None].astype(np.float32),
        "tok": np.stack([np.stack([token, token + k * SEQ], -1) for k in range(TOPK)], 1).astype(np.int32),
        "empty_slots": np.broadcast_to(np.stack([0 * s, TOPK * SEQ + s % BLK], -1).reshape(-1), (P, 2 * len(s))).astype(np.int32),
    }


def kernel(**inputs):
    import concourse.bacc as bacc
    from concourse.bass_utils import run_bass_kernel_spmd

    a = {k: np.asarray(v) for k, v in inputs.items()}
    w_uq = a["mla_w_uq"][0].reshape(Q_RANK, HEADS, QK)
    w_ukv = a["mla_w_ukv"][0].reshape(KV_RANK, HEADS, KV)
    arrays = {
        "xc": np.concatenate([a["x"][0], a["ctx"][0]]), "c": a["c"][0], "c_ctx": a["c_ctx"],
        "mod_w": a["mod_w"][0], "mod_b": a["mod_b"][0], "norm1_g": a["norm1_g"][0], "norm2_g": a["norm2_g"][0],
        "final_g": a["final_g"], "g_q": a["mla_g_q"][0], "g_kv": a["mla_g_kv"][0],
        "w_dq": a["mla_w_dq"][0], "w_dkv": a["mla_w_dkv"][0],
        "w_uq_rope": w_uq[:, :, NOPE:].reshape(Q_RANK, HEADS * ROPE),
        "w_uq": w_uq[:, :, :NOPE].transpose(1, 0, 2),
        "w_uk": w_ukv[:, :, :NOPE].transpose(1, 0, 2), "w_uv": w_ukv[:, :, NOPE:].transpose(1, 0, 2),
        "w_o": a["mla_w_o"][0],
        "w_r": np.concatenate([a["moe_w_grp"][0], a["moe_w_rt"][0]], 1),
        "b_r": np.concatenate([a["moe_b_grp"][0], a["moe_b_rt"][0]]),
        "w_gate": a["moe_w_gate"][0], "w_up": a["moe_w_up"][0], "w_down": a["moe_w_down"][0],
        **constants(),
    }
    arrays = {f"in_{k}": np.ascontiguousarray(v) for k, v in arrays.items()}
    nc = bacc.Bacc("TRN2", target_bir_lowering=False, num_devices=1)
    io = {k[3:]: nc.dram_tensor(k, v.shape, mybir.dt.from_np(v.dtype), kind="ExternalInput").ap() for k, v in arrays.items()}
    io["out"] = nc.dram_tensor("out", (SEQ, D), F32, kind="ExternalOutput").ap()
    build(nc, io)
    r = run_bass_kernel_spmd(nc, [arrays], core_ids=[0])
    return r.results[0]["out"].reshape(1, SEQ, D)
```

```python
from contextlib import ExitStack

import numpy as np

import concourse.bass as bass
from concourse import mybir
from concourse.alu_op_type import AluOpType as ALU

F32, F16, BF16, I32 = mybir.dt.float32, mybir.dt.float16, mybir.dt.bfloat16, mybir.dt.int32
ACT = mybir.ActivationFunctionType
AX = mybir.AxisListType
ds = bass.ds

P = 128
D = 1024
SEQ, CTX = 2048, 256
KEYS = SEQ + CTX
GRID_W = 64
EPS = 1e-6
ROPE_THETA = 10000.0
HEADS, Q_RANK, KV_RANK, NOPE, ROPE, VD = 8, 512, 256, 128, 64, 128
HALF = ROPE // 2
QK = NOPE + ROPE
KV = NOPE + VD
SOFTMAX_SCALE = float(QK) ** -0.5
GROUPS_E, PER_GROUP = 4, 8
EXPERTS = GROUPS_E * PER_GROUP
TOPK = 2
FF = 512
BLK = 128

DC = D // P
RC = Q_RANK // P
KC = KV_RANK // P
FC = FF // P
BANK = 512
G = 256
TG = G // P
NG = KEYS // G
NGL = SEQ // G
NT = SEQ // P
KT = KEYS // P
WS = 64.0
LOG_P_SCALE = 6.931471805599453


class Steps:

    def __init__(self, eng, sem):
        self.eng, self.sem, self.base, self.n = eng, sem, 0, 0

    def did(self, ins):
        ins.then_inc(self.sem, 1)
        self.n += 1

    def settle(self):
        if not isinstance(self.base, int) or self.base + self.n:
            self.eng.wait_ge(self.sem, self.base + self.n)

    def enter(self, before, per):
        self.outer, self.per = self.base + self.n, per
        self.base, self.n = self.outer + before, 0

    def leave(self, count):
        assert self.n == self.per, (self.n, self.per)
        self.base, self.n = self.outer + count * self.per, 0


def wait_alone(eng, sem, value, passed):
    eng.wait_ge(sem, value)
    eng.sem_inc(passed, 1)


def three_pass(pe, out, lhs, rhs, first, last):
    pe.matmul(out, lhs[0], rhs[0], start=first, stop=False)
    pe.matmul(out, lhs[0], rhs[1], start=False, stop=False)
    return pe.matmul(out, lhs[1], rhs[0], start=False, stop=last)


def project(nc, io, keep):
    ctx = ExitStack()
    with ctx:
        sb = lambda name, shape, dt=F32: ctx.enter_context(nc.sbuf_tensor(f"project_{name}", shape, dt))
        sem = lambda name: ctx.enter_context(nc.semaphore(f"project_{name}"))
        bank = lambda name: ctx.enter_context(nc.psum_tensor(f"project_{name}", [P, BANK], F32))

        cqT, ckvT, krT, qrT, ident = keep["cqT"], keep["ckvT"], keep["krT"], keep["qrT"], keep["ident"]

        x_t = sb("x_t", [P, TG, D])
        junk = sb("junk", [P, D], BF16)
        hT = [sb(f"hT{s}", [P, 2, DC, G], F16) for s in ("hi", "lo")]
        f_t = sb("f_t", [P, 2, BANK])
        w_dq = [sb(f"w_dq{s}", [P, DC, Q_RANK], F16) for s in ("hi", "lo")]
        w_dkv = [sb(f"w_dkv{s}", [P, DC, KV_RANK + ROPE], F16) for s in ("hi", "lo")]
        w_qr = [sb(f"w_qr{s}", [P, RC, HEADS * ROPE], F16) for s in ("hi", "lo")]
        stage = sb("stage", [P, DC, BANK])
        cqn = sb("cqn", [P, TG, Q_RANK])
        ckn = sb("ckn", [P, TG, KV_RANK])
        k_raw = sb("k_raw", [P, TG, ROPE])
        k_rot = sb("k_rot", [P, TG, 2 * ROPE])
        q_raw = sb("q_raw", [P, HEADS, ROPE])
        q_rot = sb("q_rot", [P, TG, HEADS, 2 * ROPE])
        rt = [sb(f"rt{i}", [P, HEADS, HALF]) for i in range(4)]
        cos_t = sb("cos_t", [P, KT, HALF])
        sin_t = sb("sin_t", [P, KT, HALF])
        mod_acc = sb("mod_acc", [P, BANK])
        mod_row = sb("mod_row", [1, BANK])
        ones = sb("ones", [P, 1])
        cond_in = sb("cond_in", [P, DC, 2])
        cond = sb("cond", [P, DC, 2])
        modb_col = sb("modb_col", [P, 2 * DC])
        g1_col = sb("g1_col", [P, DC])
        gq_col = sb("gq_col", [P, RC])
        gkv_col = sb("gkv_col", [P, KC])
        shsc = sb("shsc", [P, 2 * DC, 2])
        aff = sb("aff", [P, DC, 2])
        ssum = sb("ssum", [P, 6])
        rms = sb("rms", [P, 6])
        rstd = sb("rstd", [P, 6])
        eps_t = sb("eps_t", [P, 1])
        mod_two = q_rot[:, :, :, :].rearrange("p j h r -> p (j h r)").rearrange("p (i n) -> p i n", i=4)
        as_stage = lambda t: t.rearrange("p h t -> p (h t)").bitcast(F32).rearrange("p (k n) -> p k n", k=DC)
        early = [as_stage(qrT[:, 4 * i:4 * i + 4, :]) for i in range(2)] + [as_stage(t[:, :, :]) for t in cqT]

        tb = [bank(f"tb{i}") for i in range(2)]
        cq_ps = [bank(f"cq_ps{i}") for i in range(TG)]
        ck_ps = [bank(f"ck_ps{i}") for i in range(TG)]
        qr_ps, mr_ps = bank("qr_ps"), bank("mr_ps")
        two_ps = cq_ps + ck_ps

        small_in = sem("small_in")
        ident_in = sem("ident_in")
        rope_in = sem("rope_in")
        slot_in = [sem(f"slot_in{i}") for i in range(5)]
        x_in = sem("x_in")
        cond_ready = sem("cond_ready")
        mod_read = sem("mod_read")
        two_ready = sem("two_ready")
        cols_full = sem("cols_full")
        aff_ready = sem("aff_ready")
        w_hi = sem("w_hi")
        w_ready = sem("w_ready")
        stats = sem("stats")
        rms_ready = sem("rms_ready")
        dve_step = sem("dve_step")
        xn_ready = sem("xn_ready")
        t_full = sem("t_full")
        t_copied = sem("t_copied")
        t_free = sem("t_free")
        cq_full = sem("cq_full")
        ck_full = sem("ck_full")
        cqn_ready = sem("cqn_ready")
        ckn_ready = sem("ckn_ready")
        k_rot_ready = sem("k_rot_ready")
        qr_full = sem("qr_full")
        q_raw_ready = sem("q_raw_ready")
        q_rot_ready = sem("q_rot_ready")
        acc_ready = sem("acc_ready")
        mr_full = sem("mr_full")
        mod_row_ready = sem("mod_row_ready")
        mod_row_out = sem("mod_row_out")
        ones_ready = sem("ones_ready")
        sp_passed = sem("sp_passed")

        slots = [stage] + early
        mod_v = io["mod_w"].rearrange("(k p) n -> p k n", p=P)
        loads = [(1, "mod0"), (2, "mod1"), (3, "mod2"), (0, "dq"), (4, "mod3"), (1, "dkv"), (2, "qr")]
        weights = {
            "dq": (io["w_dq"].rearrange("(k p) n -> p k n", p=P), w_dq, DC, Q_RANK),
            "dkv": (io["w_dkv"].rearrange("(k p) n -> p k n", p=P), w_dkv, DC, KV_RANK + ROPE),
            "qr": (io["w_uq_rope"].rearrange("(k p) n -> p k n", p=P), w_qr, RC, HEADS * ROPE),
        }
        seen = [0] * len(slots)
        nth = {}
        for s, what in loads:
            seen[s] += 1
            nth[what] = (s, seen[s])

        def slot_view(what):
            s = slots[nth[what][0]]
            if what.startswith("mod"):
                return s[:, :, :]
            _, _, k, n = weights[what]
            return s[:, :, :].rearrange("p k n -> p (k n)")[:, 0:k * n].rearrange("p (k n) -> p k n", k=k)

        def wait_slot(eng, what):
            s, n = nth[what]
            eng.wait_ge(slot_in[s], 16 * n)

        PASS = 12
        T_CQ, T_CKV, T_KR, T_X, T_QR = 0, 2, 3, 4, 8

        def fill(g, what):
            if isinstance(g, int):
                if g == 0:
                    return 4 + what - T_X
                if g >= NGL:
                    return PASS * NGL - 4 + (what - 4 if what == T_QR else what)
            return PASS * g - 4 + what

        CTX_FILL = PASS * NGL - 4 + 8

        block = ctx.enter_context(nc.Block())

        @block.sync
        def _(sp):
            sp.sem_inc(mod_row_out, 1)
            for dst, src in ((cond_in[:, :, 0], io["c"]), (cond_in[:, :, 1], io["c_ctx"])):
                sp.dma_start(dst, src.rearrange("(k p) -> p k", p=P), allow_slow_non_contiguous=True).then_inc(small_in, 16)
            for dst, src in ((modb_col, io["mod_b"][0:2 * D]), (g1_col, io["norm1_g"]),
                             (gq_col, io["g_q"]), (gkv_col, io["g_kv"])):
                sp.dma_start(dst[:, :], src.rearrange("(k p) -> p k", p=P), allow_slow_non_contiguous=True).then_inc(small_in, 16)

            def load(what):
                src = mod_v[:, :, int(what[3]) * BANK:(int(what[3]) + 1) * BANK] if what.startswith("mod") else weights[what][0]
                sp.dma_start(slot_view(what), src).then_inc(slot_in[nth[what][0]], 16)

            load("mod0")
            load("mod1")
            sp.dma_start(ident[:, :], io["ident"]).then_inc(ident_in, 16)
            sp.dma_start(x_t[:, :, :], io["xc"][0:G, :].rearrange("(j p) d -> p j d", p=P)).then_inc(x_in, 16)
            load("mod2")
            load("dq")
            load("mod3")
            for what, used in (("dkv", 1), ("qr", 2)):
                sp.wait_ge(mod_read, used)
                load(what)
            sp.dma_start(cos_t[:, :, :], io["cos"]).then_inc(rope_in, 16)
            sp.dma_start(sin_t[:, :, :], io["sin"]).then_inc(rope_in, 16)
            sp.wait_ge(w_ready, 1)

            def step(g, transposed):
                cols = ds(2 * D + g * BANK, BANK) if not isinstance(g, int) else slice(2 * D + g * BANK, 2 * D + (g + 1) * BANK)
                rows = ds(g * G + G, G) if not isinstance(g, int) else slice(g * G + G, g * G + 2 * G)
                out = ds(g * BANK, BANK) if not isinstance(g, int) else slice(g * BANK, (g + 1) * BANK)
                sp.dma_start(stage[:, :, :], mod_v[:, :, cols]).then_inc(slot_in[0], 16)
                wait_alone(sp, t_full, transposed, sp_passed)
                sp.dma_start(x_t[:, :, :], io["xc"][rows, :].rearrange("(j p) d -> p j d", p=P)).then_inc(x_in, 16)
                wait_alone(sp, mod_row_ready, g + 1, sp_passed)
                sp.dma_start(io["mod_rows"][:, out], mod_row[0:1, :]).then_inc(mod_row_out, 16)
                wait_alone(sp, acc_ready, g + 1, sp_passed)

            step(0, 4)
            step(1, fill(0, T_X) + 4)
            with sp.Fori(2, NGL) as g:
                step(g, fill(g - 1, T_X) + 4)
            sp.wait_ge(mod_row_out, 16 * NGL + 1)

        @block.scalar
        def _(act):
            act.preload_act_table(ACT.Silu)
            act.wait_ge(small_in, 6 * 16)
            act.activation(cond[:, :, :], cond_in[:, :, :], ACT.Silu).then_inc(cond_ready, 1)
            act.preload_act_table(ACT.Sqrt)

            def weight_hi(what):
                wait_slot(act, what)
                act.activation(weights[what][1][0][:, :, :], slot_view(what), ACT.Copy, scale=WS).then_inc(w_hi, 1)

            def mod_rows_copy(i):
                act.wait_ge(mod_read, i + 1)
                act.activation(mod_two[0:2, i, :], two_ps[i][0:2, :], ACT.Copy).then_inc(two_ready, 1)

            stat = Steps(act, stats)

            def squares(src, i):
                stat.settle()
                stat.did(act.activation(junk[:, 0:src.shape[1]], src, ACT.Square, accum_out=ssum[:, i:i + 1]))

            def root(lo, hi, n, scale):
                stat.settle()
                act.activation(rms[:, lo:hi], ssum[:, lo:hi], ACT.Sqrt, bias=eps_t[:, :], scale=1.0 / (n * scale * scale)).then_inc(rms_ready, 1)

            def prep():
                for j in range(TG):
                    squares(x_t[:, j, :], j)
                root(0, TG, D, 1.0)

            def hi_part(hi, i, chunks):
                stat.settle()
                act.activation(hi, f_t[:, i, :].rearrange("p (k t) -> p k t", k=chunks), ACT.Copy).then_inc(t_copied, 1)

            def h_fills(n0, c, half, par):
                for i in (2 * half, 2 * half + 1):
                    act.wait_ge(t_full, n0 + i + 1)
                    for u in range(2):
                        k = 2 * i + u
                        stat.did(act.activation(f_t[:, i % 2, u * G:(u + 1) * G], tb[i % 2][:, u * G:(u + 1) * G],
                                                ACT.Identity, bias=shsc[:, k, c:c + 1], scale=aff[:, k, c:c + 1]))
                    hi_part(hT[0][:, par, 2 * i:2 * i + 2, :], i % 2, 2)

            def q_stats(g, j):
                act.wait_ge(cq_full, TG * g + j + 1)
                squares(cq_ps[j][:, :], 2 + j)
                root(2 + j, 3 + j, Q_RANK, WS)

            def kv_stats(g, j):
                act.wait_ge(ck_full, TG * g + j + 1)
                act.activation(k_raw[:, j, :], ck_ps[j][:, KV_RANK:KV_RANK + ROPE], ACT.Copy, scale=1 / WS)
                squares(ck_ps[j][:, 0:KV_RANK], 4 + j)
                root(4 + j, 5 + j, KV_RANK, WS)

            def q_fills(n0, g):
                for i in range(2):
                    act.wait_ge(t_full, n0 + i + 1)
                    for u in range(2):
                        stat.did(act.activation(f_t[:, i, u * G:(u + 1) * G], tb[i][:, u * G:(u + 1) * G],
                                                ACT.Copy, scale=gq_col[:, 2 * i + u:2 * i + u + 1]))
                    hi_part(cqT[0][:, 2 * i:2 * i + 2, ds(g * G, G)], i, 2)

            def kv_fills(n0, g):
                act.wait_ge(t_full, n0 + 1)
                for u in range(KC):
                    stat.did(act.activation(f_t[:, 0, u * G:(u + 1) * G], tb[0][:, u * G:(u + 1) * G],
                                            ACT.Copy, scale=gkv_col[:, u:u + 1]))
                hi_part(ckvT[0][:, :, ds(g * G, G)], 0, KC)
                act.wait_ge(t_full, n0 + 2)
                act.activation(krT[0][:, ds(g * G, G)], tb[1][:, 0:G], ACT.Copy).then_inc(t_copied, 1)

            def q_copy(g, j):
                act.wait_ge(qr_full, TG * g + j + 1)
                act.wait_ge(q_rot_ready, TG * g + j + 1)
                act.activation(q_raw[:, :, :], qr_ps[:, :].rearrange("p (h r) -> p h r", h=HEADS), ACT.Copy,
                               scale=1 / WS).then_inc(q_raw_ready, 1)

            def qr_fills(n0, g):
                for j in range(TG):
                    for u in range(2):
                        act.wait_ge(t_full, n0 + 2 * j + u + 1)
                        act.activation(qrT[:, 4 * u:4 * u + 4, ds(g * G + j * P, P)],
                                       tb[u][:, :].rearrange("p (h t) -> p h t", h=4), ACT.Copy).then_inc(t_copied, 1)

            mod_rows_copy(0)
            mod_rows_copy(1)
            act.wait_ge(ones_ready, 2)
            act.wait_ge(x_in, 16)
            prep()
            weight_hi("dq")
            mod_rows_copy(2)
            weight_hi("dkv")
            mod_rows_copy(3)
            act.wait_ge(aff_ready, 1)
            for half in range(2):
                h_fills(0, 0, half, 0)
            weight_hi("qr")

            def group(g, par, c_next=0):
                old = not (isinstance(g, int) and g == 0)
                latent = not (isinstance(g, int) and g == NGL)
                if latent:
                    act.wait_ge(x_in, 16 * g + 32)
                    prep()
                    q_stats(g, 0)
                if old:
                    q_fills(fill(g, T_CQ), g - 1)
                kv_stats(g, 0)
                if old:
                    kv_fills(fill(g, T_CKV), g - 1)
                if latent:
                    q_stats(g, 1)
                    h_fills(fill(g, T_X), c_next, 0, par)
                kv_stats(g, 1)
                if latent:
                    act.wait_ge(mr_full, g + 2)
                    act.wait_ge(mod_row_out, 16 * g + 1)
                    act.activation(mod_row[0:1, :], mr_ps[0:1, :], ACT.Copy).then_inc(mod_row_ready, 1)
                if old:
                    q_copy(g - 1, 0)
                if latent:
                    h_fills(fill(g, T_X), c_next, 1, par)
                if old:
                    q_copy(g - 1, 1)
                    qr_fills(fill(g, T_QR), g - 1)

            PER = 3 * TG + 2 * (2 + 1 + 4)
            group(0, 1)
            group(1, 0)
            with act.Fori(1, NGL // 2 - 1) as i:
                stat.enter((i - 1) * (2 * PER), 2 * PER)
                group(2 * i, 1)
                group(2 * i + 1, 0)
            stat.leave(NGL // 2 - 2)
            group(NGL - 2, 1)
            group(NGL - 1, 0, 1)
            group(NGL, 1)
            kv_fills(CTX_FILL, NGL)

        @block.vector
        def _(dve):
            dve.sem_inc(q_rot_ready, 1)
            step = Steps(dve, dve_step)
            dve.memset(ones[:, :], 1.0).then_inc(ones_ready, 1)
            dve.memset(eps_t[:, :], EPS).then_inc(ones_ready, 1)
            def inverse_rms(n, lo, hi):
                dve.wait_ge(rms_ready, n + 1)
                step.did(dve.reciprocal(rstd[:, lo:hi], rms[:, lo:hi]))
                step.settle()

            def prep(n):
                inverse_rms(n, 0, TG)
                for j in range(TG):
                    dve.tensor_scalar(x_t[:, j, :], x_t[:, j, :], rstd[:, j:j + 1], None, ALU.mult).then_inc(xn_ready, 1)

            def split(src, hi, lo):
                dve.tensor_tensor(lo, src, hi, ALU.subtract).then_inc(t_free, 1)

            def h_fills(n0, par, half):
                for i in (2 * half, 2 * half + 1):
                    dve.wait_ge(t_copied, n0 + i + 1)
                    split(f_t[:, i % 2, :].rearrange("p (k t) -> p k t", k=2),
                          hT[0][:, par, 2 * i:2 * i + 2, :], hT[1][:, par, 2 * i:2 * i + 2, :])

            def split_weight(n, what):
                dve.wait_ge(w_hi, n + 1)
                hi, lo = (t[:, :, :] for t in weights[what][1])
                dve.scalar_tensor_tensor(out=lo, in0=slot_view(what), scalar=WS, in1=hi,
                                         op0=ALU.mult, op1=ALU.subtract).then_inc(w_ready, 1)

            prep(0)
            split_weight(0, "dq")
            split_weight(1, "dkv")
            dve.wait_ge(small_in, 6 * 16)
            dve.wait_ge(cols_full, 1)
            step.did(dve.tensor_tensor(shsc[:, :, :], mr_ps[:, 0:4 * DC].rearrange("p (k c) -> p k c", c=2),
                                       modb_col[:, :].unsqueeze(2).broadcast_to([P, 2 * DC, 2]), ALU.add))
            step.settle()
            dve.scalar_tensor_tensor(out=aff[:, :, :], in0=shsc[:, DC:2 * DC, :], scalar=1.0,
                                     in1=g1_col[:, :].unsqueeze(2).broadcast_to([P, DC, 2]),
                                     op0=ALU.add, op1=ALU.mult).then_inc(aff_ready, 1)
            for half in range(2):
                h_fills(0, 0, half)
            split_weight(2, "qr")
            dve.wait_ge(rope_in, 32)

            def q_normed(n, j):
                inverse_rms(n, 2 + j, 3 + j)
                dve.tensor_scalar(cqn[:, j, :], cq_ps[j][:, :], rstd[:, 2 + j:3 + j], 1 / WS, ALU.mult, ALU.mult).then_inc(cqn_ready, 1)

            def kv_normed(n, j):
                inverse_rms(n, 4 + j, 5 + j)
                dve.tensor_scalar(ckn[:, j, :], ck_ps[j][:, 0:KV_RANK], rstd[:, 4 + j:5 + j], 1 / WS, ALU.mult, ALU.mult).then_inc(ckn_ready, 1)

            def rotate(x, cs, sn, out, dup, n, ready):
                x1, x2 = x[:, :, 0:HALF], x[:, :, HALF:ROPE]
                a, b, c, d = (t[:, 0:n, :] for t in rt)
                for o, x_, w in ((a, x1, cs), (b, x2, sn), (c, x1, sn), (d, x2, cs)):
                    step.did(dve.tensor_tensor(o, x_, w, ALU.mult))
                step.settle()
                step.did(dve.tensor_tensor(out[:, :, 0:HALF], a, b, ALU.subtract))
                step.did(dve.tensor_tensor(out[:, :, HALF:ROPE], c, d, ALU.add))
                step.settle()
                dve.tensor_copy(dup, out).then_inc(ready, 1)

            def rotate_keys(g):
                rotate(k_raw[:, :, :], cos_t[:, ds(g * TG, TG), :], sin_t[:, ds(g * TG, TG), :],
                       k_rot[:, :, 0:ROPE], k_rot[:, :, ROPE:2 * ROPE], TG, k_rot_ready)

            def q_fills(n0, g):
                for i in range(2):
                    dve.wait_ge(t_copied, n0 + i + 1)
                    split(f_t[:, i, :].rearrange("p (k t) -> p k t", k=2),
                          cqT[0][:, 2 * i:2 * i + 2, ds(g * G, G)], cqT[1][:, 2 * i:2 * i + 2, ds(g * G, G)])

            def kv_fills(n0, g):
                dve.wait_ge(t_copied, n0 + 1)
                split(f_t[:, 0, :].rearrange("p (k t) -> p k t", k=KC),
                      ckvT[0][:, :, ds(g * G, G)], ckvT[1][:, :, ds(g * G, G)])
                dve.wait_ge(t_copied, n0 + 2)
                dve.tensor_tensor(krT[1][:, ds(g * G, G)], tb[1][:, 0:G], krT[0][:, ds(g * G, G)],
                                  ALU.subtract).then_inc(t_free, 1)

            def gate_columns(g, k0, k1):
                if k0 == 0:
                    dve.wait_ge(slot_in[0], 16 * g + 32)
                    dve.wait_ge(mr_full, g + 1)
                for k in range(k0, k1):
                    if k == 0:
                        step.did(dve.tensor_scalar(mod_acc[:, :], stage[:, 0, :], cond[:, 0, 0:1], None, ALU.mult))
                        continue
                    step.settle()
                    ins = dve.scalar_tensor_tensor(out=mod_acc[:, :], in0=stage[:, k, :], scalar=cond[:, k, 0:1],
                                                   in1=mod_acc[:, :], op0=ALU.mult, op1=ALU.add)
                    if k < DC - 1:
                        step.did(ins)
                    else:
                        ins.then_inc(acc_ready, 1)

            def rotate_queries(g, j):
                dve.wait_ge(q_raw_ready, TG * g + j + 1)
                cs = cos_t[:, ds(g * TG + j, 1), :].broadcast_to([P, HEADS, HALF])
                sn = sin_t[:, ds(g * TG + j, 1), :].broadcast_to([P, HEADS, HALF])
                rotate(q_raw[:, :, :], cs, sn, q_rot[:, j, :, 0:ROPE], q_rot[:, j, :, ROPE:2 * ROPE], HEADS, q_rot_ready)

            def qr_fills(n0, g):
                for j in range(TG):
                    for u in range(2):
                        dve.wait_ge(t_copied, n0 + 2 * j + u + 1)
                        lo = qrT[ROPE:P, 4 * u:4 * u + 4, ds(g * G + j * P, P)]
                        dve.tensor_tensor(lo, tb[u][ROPE:P, :].rearrange("p (h t) -> p h t", h=4), lo,
                                          ALU.subtract).then_inc(t_free, 1)

            ROOTS = 1 + 2 * TG

            def group(g, par):
                old = not (isinstance(g, int) and g == 0)
                latent = not (isinstance(g, int) and g == NGL)
                n = 1 + ROOTS * g
                if latent:
                    prep(n)
                    gate_columns(g, 0, 4)
                if old:
                    q_fills(fill(g, T_CQ), g - 1)
                if latent:
                    q_normed(n + 1, 0)
                    gate_columns(g, 4, DC)
                if old:
                    kv_fills(fill(g, T_CKV), g - 1)
                kv_normed(n + 2 if latent else n, 0)
                if latent:
                    h_fills(fill(g, T_X), par, 0)
                    q_normed(n + 3, 1)
                kv_normed(n + 4 if latent else n + 1, 1)
                rotate_keys(g)
                if old:
                    rotate_queries(g - 1, 0)
                if latent:
                    h_fills(fill(g, T_X), par, 1)
                if old:
                    rotate_queries(g - 1, 1)
                    qr_fills(fill(g, T_QR), g - 1)

            PER = 1 + (DC - 1) + 2 * TG + 6 + 6 * TG
            group(0, 1)
            group(1, 0)
            with dve.Fori(1, NGL // 2) as i:
                step.enter((i - 1) * (2 * PER), 2 * PER)
                group(2 * i, 1)
                group(2 * i + 1, 0)
            step.leave(NGL // 2 - 1)
            group(NGL, 0)
            kv_fills(CTX_FILL, NGL)

        @block.tensor
        def _(pe):
            pe.sem_inc(mr_full, 1)
            pe.wait_ge(cond_ready, 1)
            for i in range(4):
                wait_slot(pe, f"mod{i}")
                for k in range(DC):
                    ins = pe.matmul(two_ps[i][0:2, :], cond[:, k, :], slots[nth[f"mod{i}"][0]][:, k, :],
                                    start=(k == 0), stop=(k == DC - 1))
                ins.then_inc(mod_read, 1)
            pe.wait_ge(ident_in, 16)
            pe.wait_ge(two_ready, 4)
            for i in range(4):
                for cc in range(4):
                    col = 4 * i + cc
                    ins = pe.transpose(mr_ps[:, 2 * col:2 * col + 2], mod_two[0:2, i, cc * P:(cc + 1) * P], ident[0:2, 0:2])
            ins.then_inc(cols_full, 1)

            def transpose_x(n0, half, first=False):
                for i in (2 * half, 2 * half + 1):
                    if not (first and i < 2):
                        pe.wait_ge(t_free, n0 + i - 1)
                    for u in range(2):
                        k = 2 * i + u
                        for j in range(TG):
                            ins = pe.transpose(tb[i % 2][:, u * G + j * P:u * G + (j + 1) * P], x_t[:, j, k * P:(k + 1) * P], ident[:, :])
                    ins.then_inc(t_full, 1)

            def q_down(g, j, par):
                tok = slice(j * P, (j + 1) * P)
                if not isinstance(g, int) or g > 0:
                    pe.wait_ge(cqn_ready, TG * g + j - TG + 1)
                for k in range(DC):
                    ins = three_pass(pe, cq_ps[j][:, :], [t[:, par, k, tok] for t in hT], [t[:, k, :] for t in w_dq],
                                     k == 0, k == DC - 1)
                ins.then_inc(cq_full, 1)

            def kv_down(g, j, par):
                tok = slice(j * P, (j + 1) * P)
                if not isinstance(g, int) or g > 0:
                    pe.wait_ge(ckn_ready, TG * g + j - TG + 1)
                for k in range(DC):
                    ins = three_pass(pe, ck_ps[j][:, 0:KV_RANK + ROPE], [t[:, par, k, tok] for t in hT],
                                     [t[:, k, :] for t in w_dkv], k == 0, k == DC - 1)
                ins.then_inc(ck_full, 1)

            def transpose_q(g, n0):
                pe.wait_ge(cqn_ready, TG * g + TG)
                for i in range(2):
                    pe.wait_ge(t_free, n0 + i - 1)
                    for u in range(2):
                        for j in range(TG):
                            ins = pe.transpose(tb[i][:, u * G + j * P:u * G + (j + 1) * P],
                                               cqn[:, j, (2 * i + u) * P:(2 * i + u + 1) * P], ident[:, :])
                    ins.then_inc(t_full, 1)

            def transpose_kv(g, n0):
                pe.wait_ge(ckn_ready, TG * g + TG)
                pe.wait_ge(t_free, n0 - 1)
                for u in range(KC):
                    for j in range(TG):
                        ins = pe.transpose(tb[0][:, u * G + j * P:u * G + (j + 1) * P], ckn[:, j, u * P:(u + 1) * P], ident[:, :])
                ins.then_inc(t_full, 1)
                pe.wait_ge(k_rot_ready, g + 1)
                pe.wait_ge(t_free, n0)
                for j in range(TG):
                    ins = pe.transpose(tb[1][:, j * P:(j + 1) * P], k_rot[:, j, :], ident[:, :])
                ins.then_inc(t_full, 1)

            def q_up(g, j):
                if not (isinstance(g, int) and g == 0 and j == 0):
                    pe.wait_ge(q_raw_ready, TG * g + j)
                for k in range(RC):
                    ins = three_pass(pe, qr_ps[:, :], [t[:, k, ds(g * G + j * P, P)] for t in cqT], [t[:, k, :] for t in w_qr],
                                     k == 0, k == RC - 1)
                ins.then_inc(qr_full, 1)

            def transpose_qr(g, n0):
                for j in range(TG):
                    pe.wait_ge(q_rot_ready, TG * g + j + 2)
                    for u in range(2):
                        pe.wait_ge(t_free, n0 + 2 * j + u - 1)
                        for v in range(4):
                            ins = pe.transpose(tb[u][:, v * P:(v + 1) * P], q_rot[:, j, 4 * u + v, :], ident[:, :])
                        ins.then_inc(t_full, 1)

            def group(g, par):
                old = not (isinstance(g, int) and g == 0)
                latent = not (isinstance(g, int) and g == NGL)
                pe.wait_ge(t_free, 4 if not old else fill(g - 1, T_X) + 4)
                if latent:
                    q_down(g, 0, par)
                if old:
                    transpose_q(g - 1, fill(g, T_CQ))
                kv_down(g, 0, par)
                if old:
                    transpose_kv(g - 1, fill(g, T_CKV))
                if latent:
                    q_down(g, 1, par)
                    pe.wait_ge(xn_ready, TG * g + 2 * TG)
                    transpose_x(fill(g, T_X), 0)
                kv_down(g, 1, par)
                if latent:
                    pe.wait_ge(acc_ready, g + 1)
                    if old:
                        pe.wait_ge(mod_row_ready, g)
                    pe.matmul(mr_ps[0:1, :], ones[:, :], mod_acc[:, :], start=True, stop=True).then_inc(mr_full, 1)
                if old:
                    if isinstance(g, int) and g == 1:
                        pe.wait_ge(w_ready, 3)
                    pe.wait_ge(t_free, fill(g, T_CQ) + 2)
                    q_up(g - 1, 0)
                if latent:
                    transpose_x(fill(g, T_X), 1)
                if old:
                    q_up(g - 1, 1)
                    transpose_qr(g - 1, fill(g, T_QR))

            pe.wait_ge(xn_ready, TG)
            for half in range(2):
                transpose_x(0, half, first=True)
            pe.wait_ge(w_ready, 2)
            group(0, 0)
            group(1, 1)
            with pe.Fori(1, NGL // 2) as i:
                group(2 * i, 0)
                group(2 * i + 1, 1)
            group(NGL, 0)
            transpose_kv(NGL, CTX_FILL)


SB = [(c * BANK, min(BANK, KEYS - c * BANK)) for c in range(-(-KEYS // BANK))]
NS = len(SB)
QB = SEQ // BANK
KPB = BANK // P


def attend(nc, io, keep):
    ctx = ExitStack()
    with ctx:
        sb = lambda name, shape, dt=F32: ctx.enter_context(nc.sbuf_tensor(f"attend_{name}", shape, dt))
        sem = lambda name: ctx.enter_context(nc.semaphore(f"attend_{name}"))
        cqT, ckvT, krT, qrT, ident = keep["cqT"], keep["ckvT"], keep["krT"], keep["qrT"], keep["ident"]

        NW = RC + 2 * KC
        w_raw = sb("w_raw", [P, NW, P])
        w_h = [sb(f"w_h{s}", [P, NW, P], F16) for s in ("hi", "lo")]
        qT = [sb(f"qT{s}", [P, SEQ], F16) for s in ("hi", "lo")]
        kT = [sb(f"kT{s}", [P, KEYS], F16) for s in ("hi", "lo")]
        v = sb("v", [P, KT, 2, VD], F16)
        prob = sb("prob", [P, KEYS])
        pT = [sb(f"pT{s}", [P, KT, P], F16) for s in ("hi", "lo")]
        o_lo = sb("o_lo", [P, VD])
        o_out = sb("o_out", [P, VD])
        mx = sb("mx", [P, NS])
        neg_max = sb("neg_max", [P, 2])
        rsum = sb("rsum", [P, NS])
        inv = sb("inv", [P, 2])

        s_ps = ctx.enter_context(nc.psum_tensor("attend_s_ps", [P, NS, BANK], F32))
        tb = [ctx.enter_context(nc.psum_tensor(f"attend_tp{i}", [P, BANK], F32)) for i in range(2)]
        o_ps = ctx.enter_context(nc.psum_tensor("attend_o_ps", [P, BANK], F32))

        w_in = sem("w_in")
        w_hi = sem("w_hi")
        w_ready = sem("w_ready")
        b_full = sem("b_full")
        b_copied = sem("b_copied")
        b_free = sem("b_free")
        s_full = sem("s_full")
        s_free = sem("s_free")
        max_step = sem("max_step")
        max_ready = sem("max_ready")
        inv_ready = sem("inv_ready")
        o_full = sem("o_full")
        o_lo_ready = sem("o_lo_ready")
        o_ready = sem("o_ready")
        o_stored = sem("o_stored")
        sp_passed = sem("sp_passed2")

        QKF = QB + NS
        PER = QKF + NS + NS + (NT - 1) * NS

        def qk_fill(h):
            return 0 if isinstance(h, int) and h == 0 else PER * h - NS

        def step_fill(h, t):
            return PER * h - NS + QKF + t * NS + (0 if isinstance(t, int) and t == 0 else NS)

        def v_fill(h):
            return PER * h - NS + QKF + NS

        END_FILL = PER * HEADS - NS
        LAST = HEADS - 1

        block = ctx.enter_context(nc.Block())

        @block.sync
        def _(sp):
            sp.sem_inc(o_stored, 1)
            def load(h):
                for dst, src, k in ((w_raw[:, 0:RC, :], io["w_uq"], RC), (w_raw[:, RC:RC + KC, :], io["w_uk"], KC),
                                    (w_raw[:, RC + KC:NW, :], io["w_uv"], KC)):
                    src = src[ds(h, 1)] if not isinstance(h, int) else src[h:h + 1]
                    sp.dma_start(dst, src.rearrange("a (k p) n -> p (a k) n", p=P)).then_inc(w_in, 16)

            load(0)
            sp.wait_ge(w_ready, 1)
            load(1)

            def stores(h):
                with sp.Fori(0, NT) as t:
                    wait_alone(sp, o_ready, h * NT + t + 2, sp_passed)
                    sp.dma_start(io["attn"][ds(t * P, P), ds(h * VD, VD)], o_out[:, :]).then_inc(o_stored, 16)

            with sp.Fori(0, HEADS - 2) as h:
                wait_alone(sp, w_ready, h + 2, sp_passed)
                load(h + 2)
                stores(h)
            with sp.Fori(HEADS - 2, HEADS) as h:
                stores(h)
            sp.wait_ge(o_stored, 16 * HEADS * NT + 1)

        @block.scalar
        def _(act):
            act.preload_act_table(ACT.Exp)

            def copy_fill(n, bank_, dst, width, scale):
                act.wait_ge(b_full, n + 1)
                src = bank_[:, 0:width]
                if len(dst.shape) == 3:
                    src = src.rearrange("p (k t) -> p k t", t=P)
                act.activation(dst, src, ACT.Copy, scale=scale).then_inc(b_copied, 1)

            def split_weights(h):
                act.wait_ge(w_in, 48 * h + 48)
                act.activation(w_h[0][:, :, :], w_raw[:, :, :], ACT.Copy, scale=WS).then_inc(w_hi, 1)

            def queries_keys(n, par):
                for c in range(QB):
                    copy_fill(n + c, tb[(par + c) % 2], qT[0][:, c * BANK:(c + 1) * BANK], BANK, 1 / WS)
                for c, (k0, w) in enumerate(SB):
                    copy_fill(n + QB + c, tb[(par + QB + c) % 2], kT[0][:, k0:k0 + w], w, 1 / WS)

            def values(n, par):
                for c, (k0, w) in enumerate(SB):
                    copy_fill(n + c, tb[(par + c) % 2], v[:, c * KPB:c * KPB + w // P, 0, :], w, 1 / WS)

            def exps(step):
                act.wait_ge(max_ready, step + 1)
                for c, (k0, w) in enumerate(SB):
                    act.activation(prob[:, k0:k0 + w], s_ps[:, c, 0:w], ACT.Exp, bias=neg_max[:, 1:2], scale=SOFTMAX_SCALE,
                                   accum_out=rsum[:, c:c + 1]).then_inc(s_free, 1)

            def transposed(n, low=None):
                for c, (k0, w) in enumerate(SB):
                    copy_fill(n + c, tb[c % 2], pT[0][:, c * KPB:c * KPB + w // P, :], w, 1.0)
                    if c == 0 and low is not None:
                        low_output(low)

            def low_output(step):
                act.wait_ge(o_full, step + 1)
                act.wait_ge(inv_ready, step + 1)
                act.activation(o_lo[:, :], o_ps[:, VD:2 * VD], ACT.Copy, scale=inv[:, 1:2]).then_inc(o_lo_ready, 1)

            def head(h, first=False, last=False):
                queries_keys(qk_fill(h), 0)
                if not first:
                    transposed(step_fill(h, 0), h * NT - 2)
                exps(h * NT)
                values(v_fill(h), 0)
                if not last:
                    split_weights(h + 1)
                t0 = 1
                if first:
                    transposed(step_fill(h, 1))
                    exps(1)
                    t0 = 2
                with act.Fori(t0, NT) as t:
                    transposed(step_fill(h, t), h * NT + t - 2)
                    exps(h * NT + t)

            act.sem_inc(s_free, NS)
            split_weights(0)
            head(0, first=True)
            with act.Fori(1, LAST) as h:
                head(h)
            head(LAST, last=True)
            transposed(END_FILL, HEADS * NT - 2)
            low_output(HEADS * NT - 1)

        @block.vector
        def _(dve):
            dve.sem_inc(o_ready, 1)
            step = Steps(dve, max_step)

            def split_fill(n, bank_, hi, lo, width, scale):
                dve.wait_ge(b_copied, n + 1)
                src = bank_[:, 0:width]
                if len(hi.shape) == 3:
                    src = src.rearrange("p (k t) -> p k t", t=P)
                if scale == 1.0:
                    ins = dve.tensor_tensor(lo, src, hi, ALU.subtract)
                else:
                    ins = dve.scalar_tensor_tensor(out=lo, in0=src, scalar=scale, in1=hi, op0=ALU.mult, op1=ALU.subtract)
                ins.then_inc(b_free, 1)

            def split_weights(h):
                dve.wait_ge(w_hi, h + 1)
                dve.scalar_tensor_tensor(out=w_h[1][:, :, :], in0=w_raw[:, :, :], scalar=WS, in1=w_h[0][:, :, :],
                                         op0=ALU.mult, op1=ALU.subtract).then_inc(w_ready, 1)

            def queries_keys(n, par):
                for c in range(QB):
                    s = slice(c * BANK, (c + 1) * BANK)
                    split_fill(n + c, tb[(par + c) % 2], qT[0][:, s], qT[1][:, s], BANK, 1 / WS)
                for c, (k0, w) in enumerate(SB):
                    s = slice(k0, k0 + w)
                    split_fill(n + QB + c, tb[(par + QB + c) % 2], kT[0][:, s], kT[1][:, s], w, 1 / WS)

            def values(n, par):
                for c, (k0, w) in enumerate(SB):
                    s = slice(c * KPB, c * KPB + w // P)
                    split_fill(n + c, tb[(par + c) % 2], v[:, s, 0, :], v[:, s, 1, :], w, 1 / WS)

            def chunk_max(st, c):
                dve.wait_ge(s_full, st * NS + c + 1)
                step.did(dve.tensor_reduce(mx[:, c:c + 1], s_ps[:, c, 0:SB[c][1]], AX.X, ALU.max))

            def row_max():
                step.settle()
                step.did(dve.tensor_reduce(neg_max[:, 0:1], mx[:, :], AX.X, ALU.max))
                step.settle()
                dve.tensor_scalar(neg_max[:, 1:2], neg_max[:, 0:1], -SOFTMAX_SCALE, LOG_P_SCALE, ALU.mult, ALU.add).then_inc(max_ready, 1)

            def inverse(st):
                dve.wait_ge(s_free, (st + 2) * NS)
                step.did(dve.tensor_reduce(inv[:, 0:1], rsum[:, :], AX.X, ALU.add))
                step.settle()
                dve.reciprocal(inv[:, 1:2], inv[:, 0:1]).then_inc(inv_ready, 1)

            def output(st):
                dve.wait_ge(o_lo_ready, st + 1)
                dve.wait_ge(o_stored, st * 16 + 1)
                dve.scalar_tensor_tensor(out=o_out[:, :], in0=o_ps[:, 0:VD], scalar=inv[:, 1:2], in1=o_lo[:, :],
                                         op0=ALU.mult, op1=ALU.add).then_inc(o_ready, 1)

            def low_fill(n, c):
                k0, w = SB[c]
                s = slice(c * KPB, c * KPB + w // P)
                split_fill(n + c, tb[c % 2], pT[0][:, s, :], pT[1][:, s, :], w, 1.0)

            def step_of(h, t, st, output_due=True):
                for c in range(NS):
                    chunk_max(st, c)
                    if c == NS - 1:
                        row_max()
                    low_fill(step_fill(h, t), c)
                    if c == 0:
                        if output_due:
                            output(st - 2)
                        inverse(st - 1)

            STEP = NS + 2

            def head(h, first=False, last=False):
                queries_keys(qk_fill(h), 0)
                if first:
                    for c in range(NS):
                        chunk_max(0, c)
                    row_max()
                else:
                    step_of(h, 0, h * NT)
                values(v_fill(h), 0)
                if not last:
                    split_weights(h + 1)
                t0 = 1
                if first:
                    step_of(h, 1, 1, output_due=False)
                    t0 = 2
                with dve.Fori(t0, NT) as t:
                    step.enter((t - t0) * STEP, STEP)
                    step_of(h, t, h * NT + t)
                step.leave(NT - t0)

            split_weights(0)
            head(0, first=True)
            with dve.Fori(1, LAST) as h:
                step.enter((h - 1) * (STEP * NT), STEP * NT)
                outer = step.outer
                head(h)
            step.base, step.n = outer + (LAST - 1) * STEP * NT, 0
            head(LAST, last=True)
            for c in range(NS):
                low_fill(END_FILL, c)
                if c == 0:
                    output(HEADS * NT - 2)
                    inverse(HEADS * NT - 1)
            output(HEADS * NT - 1)

        @block.tensor
        def _(pe):
            def wait_bank(n, lag=1):
                if isinstance(n, int):
                    if n - lag > 0:
                        pe.wait_ge(b_free, n - lag)
                else:
                    pe.wait_ge(b_free, n - lag)

            def queries_keys(h, n, par):
                pe.wait_ge(w_ready, h + 1)
                for c in range(QB):
                    wait_bank(n + c, 0 if c == 0 else 1)
                    for k in range(RC):
                        ins = three_pass(pe, tb[(par + c) % 2][:, :], [t[:, k, :] for t in w_h],
                                         [t[:, k, c * BANK:(c + 1) * BANK] for t in cqT], k == 0, k == RC - 1)
                    ins.then_inc(b_full, 1)
                for c, (k0, w) in enumerate(SB):
                    wait_bank(n + QB + c)
                    for k in range(KC):
                        ins = three_pass(pe, tb[(par + QB + c) % 2][:, 0:w], [t[:, RC + k, :] for t in w_h],
                                         [t[:, k, k0:k0 + w] for t in ckvT], k == 0, k == KC - 1)
                    ins.then_inc(b_full, 1)

            def values(n, par):
                for c, (k0, w) in enumerate(SB):
                    wait_bank(n + c, 0 if c == 0 else 1)
                    for i in range(w // P):
                        keys = slice(k0 + i * P, k0 + (i + 1) * P)
                        for k in range(KC):
                            ins = three_pass(pe, tb[(par + c) % 2][:, i * P:(i + 1) * P], [t[:, k, keys] for t in ckvT],
                                             [t[:, RC + KC + k, :] for t in w_h], k == 0, k == KC - 1)
                    ins.then_inc(b_full, 1)

            def scores(h, t, st, c):
                k0, w = SB[c]
                q = ds(t * P, P) if not isinstance(t, int) else slice(t * P, (t + 1) * P)
                pe.wait_ge(s_free, st * NS + c + 1)
                out, keys = s_ps[:, c, 0:w], slice(k0, k0 + w)
                pe.matmul(out, qT[0][:, q], kT[0][:, keys], start=True, stop=False)
                pe.matmul(out, qT[0][:, q], kT[1][:, keys], start=False, stop=False)
                pe.matmul(out, qT[1][:, q], kT[0][:, keys], start=False, stop=False)
                r = qrT[:, ds(h, 1), q].rearrange("p a t -> p (a t)") if not isinstance(h, int) else qrT[:, h, q]
                pe.matmul(out, r, krT[0][:, keys], start=False, stop=False)
                pe.matmul(out, r, krT[1][:, keys], start=False, stop=True).then_inc(s_full, 1)

            def transpose_probs(n, c):
                k0, w = SB[c]
                wait_bank(n + c, 0 if c == 0 else 1)
                for i in range(w // P):
                    ins = pe.transpose(tb[c % 2][:, i * P:(i + 1) * P], prob[:, k0 + i * P:k0 + (i + 1) * P], ident[:, :])
                ins.then_inc(b_full, 1)

            def output(n, st):
                pe.wait_ge(o_ready, st + 1)
                for c, (k0, w) in enumerate(SB):
                    pe.wait_ge(b_free, n + c + 1)
                    for i in range(c * KPB, c * KPB + w // P):
                        pe.matmul(o_ps[:, 0:2 * VD], pT[0][:, i, :], v[:, i, :, :].rearrange("p s d -> p (s d)"),
                                  start=(i == 0), stop=False)
                        ins = pe.matmul(o_ps[:, 0:VD], pT[1][:, i, :], v[:, i, 0, :], start=False, stop=(i == KT - 1))
                ins.then_inc(o_full, 1)

            def step_of(h, t, st):
                for c in range(NS):
                    scores(h, t, st, c)
                    transpose_probs(step_fill(h, t), c)
                output(step_fill(h, t), st - 1)

            def head(h, first=False):
                queries_keys(h, qk_fill(h), 0)
                pe.wait_ge(b_free, qk_fill(h) + QKF)
                if first:
                    for c in range(NS):
                        scores(h, 0, 0, c)
                else:
                    step_of(h, 0, h * NT)
                values(v_fill(h), 0)
                with pe.Fori(1, NT) as t:
                    step_of(h, t, h * NT + t)

            head(0, first=True)
            with pe.Fori(1, HEADS) as h:
                head(h)
            pe.wait_ge(s_free, (HEADS * NT + 1) * NS)
            for c in range(NS):
                transpose_probs(END_FILL, c)
            output(END_FILL, HEADS * NT - 1)


SLOTS = SEQ
PBLK = SLOTS // BLK
LAST_BLOCK = SEQ * TOPK // BLK + EXPERTS - 2
NBMAX = LAST_BLOCK + 5
BIG = 1e30
KNEG, IOTA, EOFF, THR, NCONST = 0, NBMAX, 2 * NBMAX, 2 * NBMAX + EXPERTS, 2 * NBMAX + EXPERTS + PBLK
SLOT_OF, BLOCKS_OF, FIRST_OF, NTABLE = 0, NBMAX, NBMAX + EXPERTS, NBMAX + 2 * EXPERTS


def route(nc, io, keep):
    ctx = ExitStack()
    with ctx:
        sb = lambda name, shape, dt=F32: ctx.enter_context(nc.sbuf_tensor(f"route_{name}", shape, dt))
        sem = lambda name: ctx.enter_context(nc.semaphore(f"route_{name}"))
        ident, g2b = keep["ident"], keep["g2b"]

        w_st = sb("w_st", [P, DC, D])
        w_o = [sb(f"w_o{s}", [P, DC, D], F16) for s in ("hi", "lo")]
        w_r = sb("w_r", [P, DC, 4 + EXPERTS])
        b_r = sb("b_r", [P, 4 + EXPERTS])
        at = sb("at", [P, 2, D])
        xt = sb("xt", [P, 2, D])
        aT = [sb(f"aT{s}", [P, 2, DC, P], F16) for s in ("hi", "lo")]
        yg = sb("yg", [P, D])
        x1 = sb("x1_t", [P, 2, D])
        h2 = sb("h2_t", [P, 2, D])
        h2T = sb("h2T", [P, 2, DC, P])
        sq = sb("sq", [P, D], BF16)
        g1b = sb("g1b", [P, D])
        A2b = sb("A2b", [P, D])
        B2b = sb("B2b", [P, D])
        rowb = sb("rowb", [P, 4, D])
        n2b = sb("n2b", [P, D])
        ss = sb("ss", [P, 2])
        rms = sb("rms", [P, 2])
        small = sb("small", [P, 8])
        eps_t = sb("eps_t", [P, 1])
        cst = sb("cst", [P, NCONST])
        tri = sb("tri", [P, P], F16)
        tri_f = sb("tri_f", [P, P])
        ones = sb("ones", [P, P], F16)
        tok = sb("tok", [P, TOPK, NT, 2], I32)
        lg = sb("lg", [P, NT, 4 + EXPERTS])

        w = {n: sb("r_" + n, shape, dt) for n, shape, dt in (
            ("dest_i", [P, TOPK * NT], I32), ("dest", [P, TOPK * NT], F32), ("ex", [P, NT, 5], F32),
            ("M", [P, NT, EXPERTS], F16), ("M1", [P, NT, EXPERTS], F16), ("M2", [P, NT, EXPERTS], F16),
            ("per_row", [P, 7 * NT], F32), ("eq", [P, NT, PER_GROUP], F32), ("ohg", [P, NT, GROUPS_E], F32),
            ("sel", [P, NT, PER_GROUP], F32), ("oh1", [P, NT, PER_GROUP], F32), ("oh2", [P, NT, PER_GROUP], F32),
            ("big", [P, NT * EXPERTS], F32), ("big2", [P, NBMAX * EXPERTS], F32), ("rank", [P, NT, EXPERTS], F32),
            ("per_e", [P, 3, EXPERTS], F32), ("tab_f", [P, 2, NBMAX], F32))}

        tb = [ctx.enter_context(nc.psum_tensor(f"route_rt{i}", [P, BANK], F32)) for i in range(2)]
        y_ps = [ctx.enter_context(nc.psum_tensor(f"route_y_ps{i}", [P, D], F32)) for i in range(2)]
        lg_ps = [ctx.enter_context(nc.psum_tensor(f"route_lg_ps{i}", [P, BANK], F32)) for i in range(2)]

        w_in = [sem(f"w_in{i}") for i in range(2)]
        small_in = sem("small_in")
        w_hi = sem("w_hi")
        w_ready = sem("w_ready")
        at_in = [sem(f"at_in{i}") for i in range(2)]
        xt_in = [sem(f"xt_in{i}") for i in range(2)]
        rows_ready = sem("rows_ready")
        t_full = sem("t_full")
        t_hi = sem("t_hi")
        t_free = [sem(f"t_free{i}") for i in range(2)]
        aT_ready = sem("aT_ready")
        y_full = sem("y_full")
        x1_ready = sem("x1_ready")
        rms_ready = sem("rms_ready")
        sq_done = sem("sq_done")
        h2_ready = sem("h2_ready")
        h2T_ready = sem("h2T_ready")
        lg_full = sem("lg_full")
        lg_ready = sem("lg_ready")
        x1_out = [sem(f"x1_out{i}") for i in range(2)]
        h2_out = [sem(f"h2_out{i}") for i in range(2)]
        dve_step = sem("dve_step")
        sp_passed = sem("sp_passed")
        slots_empty = sem("slots_empty")
        exp_in = sem("exp_in")
        exp_out = sem("exp_out")
        m_ready = sem("m_ready")
        rank_full = sem("rank_full")
        dest_ready = sem("dest_ready")
        slots_out = sem("slots_out")

        def at_fill(n):
            return 2 * n if isinstance(n, int) and n < 2 else 4 * n - 4

        def h2_fill(n):
            if isinstance(n, int) and n >= NT - 2:
                return 4 * NT - 4 + 2 * (n - NT + 2)
            return 4 * n + 6

        mod_b = io["mod_b"].rearrange("(a n) -> a n", a=1)
        block = ctx.enter_context(nc.Block())

        @block.sync
        def _(sp):
            sp.dma_start(at[:, 0, :], io["attn"][0:P, :]).then_inc(at_in[0], 16)
            w_v = io["w_o"].rearrange("(k p) n -> p k n", p=P)
            for i in range(2):
                sp.dma_start(w_st[:, 4 * i:4 * i + 4, :], w_v[:, 4 * i:4 * i + 4, :]).then_inc(w_in[i], 16)
            sp.dma_start(at[:, 1, :], io["attn"][P:2 * P, :]).then_inc(at_in[1], 16)
            for i, dst in enumerate((g1b, B2b, A2b, g2b)):
                sp.dma_start(dst[:, :], io["mod_rows"][:, i * D:(i + 1) * D].broadcast_to([P, D])).then_inc(small_in, 16)
                sp.dma_start(rowb[:, i, :], mod_b[:, (i + 2) * D:(i + 3) * D].broadcast_to([P, D])).then_inc(small_in, 16)
            sp.dma_start(n2b[:, :], io["norm2_g"].rearrange("(a n) -> a n", a=1).broadcast_to([P, D])).then_inc(small_in, 16)
            for n in range(2):
                sp.dma_start(xt[:, n, :], io["xc"][n * P:(n + 1) * P, :]).then_inc(xt_in[n], 16)
            sp.dma_start(b_r[:, :], io["b_r"].rearrange("(a n) -> a n", a=1).broadcast_to([P, 4 + EXPERTS])).then_inc(small_in, 16)
            sp.dma_start(w_r[:, :, :], io["w_r"].rearrange("(k p) n -> p k n", p=P)).then_inc(small_in, 16)
            sp.dma_start(cst[:, :], io["row_consts"].broadcast_to([P, NCONST])).then_inc(small_in, 16)
            sp.dma_start(tri_f[:, :], io["tri"]).then_inc(small_in, 16)
            sp.dma_start(tok[:, :, :, :], io["tok"]).then_inc(small_in, 16)
            sp.dma_start(io["slots"].rearrange("(p n) o -> p (n o)", p=P), io["empty_slots"]).then_inc(slots_empty, 16)

            def rows(n):
                return ds(n * P, P) if not isinstance(n, int) else slice(n * P, (n + 1) * P)

            def load_attn(n, par):
                wait_alone(sp, t_full, at_fill(n - 2) + 2, sp_passed)
                sp.dma_start(at[:, par, :], io["attn"][rows(n), :]).then_inc(at_in[par], 16)

            def store_x1(n, par):
                wait_alone(sp, x1_ready, n + 1, sp_passed)
                sp.dma_start(io["x1"][rows(n), :], x1[:, par, :]).then_inc(x1_out[par], 16)

            def load_x(n, par):
                sp.dma_start(xt[:, par, :], io["xc"][rows(n), :]).then_inc(xt_in[par], 16)

            def store_h2(n, par):
                wait_alone(sp, h2_ready, n + 1, sp_passed)
                sp.dma_start(io["h2"][rows(n), :], h2[:, par, :]).then_inc(h2_out[par], 16)

            def step(t, par, attn=True, x=True):
                if attn:
                    load_attn(t + 2, par)
                store_x1(t - 1, 1 - par)
                if x:
                    load_x(t + 1, 1 - par)
                store_h2(t - 1, 1 - par)

            load_attn(2, 0)
            step(1, 1)
            with sp.Fori(0, (NT - 4) // 2) as i:
                step(2 * i + 2, 0)
                step(2 * i + 3, 1)
            step(NT - 2, 0, attn=False)
            step(NT - 1, 1, attn=False, x=False)
            step(NT, 0, attn=False, x=False)
            for i in range(2):
                sp.wait_ge(x1_out[i], 8 * NT)
                sp.wait_ge(h2_out[i], 8 * NT)

        @block.gpsimd
        def _(pool):
            pool.wait_ge(slots_empty, 16)
            pool.wait_ge(small_in, 16 * 14)
            for k in range(TOPK):
                pool.wait_ge(dest_ready, k + 1)
                for t in range(NT):
                    pool.indirect_dma_start(io["slots"], bass.IndirectOffsetOnAxis(ap=w["dest_i"][:, k * NT + t:k * NT + t + 1], axis=0),
                                            tok[:, k, t, :], None).then_inc(slots_out, 16)
            pool.wait_ge(slots_out, 16 * TOPK * NT)

        @block.scalar
        def _(act):
            act.preload_act_table(ACT.Sqrt)
            for i in range(2):
                act.wait_ge(w_in[i], 16)
                act.activation(w_o[0][:, 4 * i:4 * i + 4, :], w_st[:, 4 * i:4 * i + 4, :], ACT.Copy, scale=WS).then_inc(w_hi, 1)

            def attn_hi(n, par):
                for i in range(2):
                    act.wait_ge(t_full, at_fill(n) + i + 1)
                    act.activation(aT[0][:, par, 4 * i:4 * i + 4, :], tb[i][:, :].rearrange("p (k t) -> p k t", k=4),
                                   ACT.Copy).then_inc(t_hi, 1)

            def norm(n, par):
                act.wait_ge(x1_ready, n + 1)
                act.activation(sq[:, :], x1[:, par, :], ACT.Square, accum_out=ss[:, par:par + 1]).then_inc(sq_done, 1)
                act.wait_ge(sq_done, n + 1)
                act.activation(rms[:, par:par + 1], ss[:, par:par + 1], ACT.Sqrt, bias=eps_t[:, :], scale=1.0 / D).then_inc(rms_ready, 1)

            def h2_copies(n, par):
                for i in range(2):
                    act.wait_ge(t_full, h2_fill(n) + i + 1)
                    act.activation(h2T[:, par, 4 * i:4 * i + 4, :], tb[i][:, :].rearrange("p (k t) -> p k t", k=4),
                                   ACT.Copy).then_inc(t_free[i], 1)

            def step(t, par):
                attn_hi(t + 1, 1 - par)
                norm(t - 1, 1 - par)
                h2_copies(t - 1, 1 - par)

            attn_hi(0, 0)
            attn_hi(1, 1)
            act.wait_ge(rows_ready, 1)
            with act.Fori(0, (NT - 2) // 2) as i:
                step(2 * i + 1, 1)
                step(2 * i + 2, 0)
            for n in (NT - 2, NT - 1):
                norm(n, n % 2)
                h2_copies(n, n % 2)
            act.preload_act_table(ACT.Exp)
            act.wait_ge(exp_in, 1)
            act.activation(w["ex"][:, :, :], w["ex"][:, :, :], ACT.Exp).then_inc(exp_out, 1)

        @block.vector
        def _(dve):
            step = Steps(dve, dve_step)
            dve.memset(eps_t[:, :], EPS)
            step.did(dve.memset(ones[:, :], 1.0))
            for i in range(2):
                dve.wait_ge(w_hi, i + 1)
                c = slice(4 * i, 4 * i + 4)
                dve.scalar_tensor_tensor(out=w_o[1][:, c, :], in0=w_st[:, c, :], scalar=WS, in1=w_o[0][:, c, :],
                                         op0=ALU.mult, op1=ALU.subtract).then_inc(w_ready, 1)

            def attn_lo(n, par):
                for i in range(2):
                    dve.wait_ge(t_hi, 2 * n + i + 1)
                    dve.tensor_tensor(aT[1][:, par, 4 * i:4 * i + 4, :], tb[i][:, :].rearrange("p (k t) -> p k t", k=4),
                                      aT[0][:, par, 4 * i:4 * i + 4, :], ALU.subtract).then_inc(t_free[i], 1)

            attn_lo(0, 0)
            attn_lo(1, 1)
            dve.wait_ge(small_in, 16 * 14)
            for i, dst in enumerate((g1b, B2b, A2b, g2b)):
                step.did(dve.tensor_tensor(dst[:, :], dst[:, :], rowb[:, i, :], ALU.add))
            step.did(dve.tensor_copy(tri[:, :], tri_f[:, :]))
            step.settle()
            step.did(dve.tensor_scalar(g1b[:, :], g1b[:, :], 1 / WS, None, ALU.mult))
            dve.scalar_tensor_tensor(out=A2b[:, :], in0=A2b[:, :], scalar=1.0, in1=n2b[:, :], op0=ALU.add, op1=ALU.mult).then_inc(rows_ready, 1)
            step.settle()
            dve.wait_ge(rows_ready, 1)

            def residual(n, par):
                dve.wait_ge(y_full, n + 1)
                step.did(dve.tensor_tensor(yg[:, :], y_ps[par][:, :], g1b[:, :], ALU.mult))
                dve.wait_ge(xt_in[par], 8 * (n - par) + 16)
                if not (isinstance(n, int) and n < 2):
                    dve.wait_ge(x1_out[par], 8 * (n - par))
                step.settle()
                dve.tensor_tensor(x1[:, par, :], yg[:, :], xt[:, par, :], ALU.add).then_inc(x1_ready, 1)

            def norm(n, par):
                r, m, u, v = (small[:, 4 * par + i:4 * par + i + 1] for i in range(4))
                dve.wait_ge(rms_ready, n + 1)
                step.did(dve.reciprocal(r, rms[:, par:par + 1]))
                step.did(dve.tensor_scalar(m, ss[:, par:par + 1], 1.0 / D, EPS, ALU.mult, ALU.add))
                step.settle()
                step.did(dve.scalar_tensor_tensor(out=u, in0=r, scalar=r, in1=m, op0=ALU.mult, op1=ALU.mult))
                step.settle()
                step.did(dve.tensor_scalar(v, u, -0.5, 1.5, ALU.mult, ALU.add))
                step.settle()
                step.did(dve.tensor_tensor(u, r, v, ALU.mult))
                if not (isinstance(n, int) and n < 2):
                    dve.wait_ge(h2_out[par], 8 * (n - par))
                step.settle()
                step.did(dve.scalar_tensor_tensor(out=h2[:, par, :], in0=x1[:, par, :], scalar=u, in1=A2b[:, :], op0=ALU.mult, op1=ALU.mult))
                step.settle()
                dve.tensor_tensor(h2[:, par, :], h2[:, par, :], B2b[:, :], ALU.add).then_inc(h2_ready, 1)

            def logits(n, par):
                dve.wait_ge(lg_full, n + 1)
                dst = lg[:, ds(n, 1), :].rearrange("p a n -> p (a n)") if not isinstance(n, int) else lg[:, n, :]
                dve.tensor_tensor(dst, lg_ps[par][:, 0:4 + EXPERTS], b_r[:, :], ALU.add).then_inc(lg_ready, 1)

            def body(t, par):
                residual(t - 1, 1 - par)
                attn_lo(t + 1, 1 - par)
                norm(t - 1, 1 - par)
                logits(t - 1, 1 - par)

            PER = 7
            body(1, 1)
            body(2, 0)
            with dve.Fori(1, (NT - 2) // 2) as i:
                step.enter((i - 1) * (2 * PER), 2 * PER)
                body(2 * i + 1, 1)
                body(2 * i + 2, 0)
            step.leave((NT - 2) // 2 - 1)
            for n in (NT - 2, NT - 1):
                residual(n, n % 2)
                norm(n, n % 2)
                logits(n, n % 2)
            dve.wait_ge(lg_ready, NT)
            slots_of_tokens(dve, step, lg, cst, keep, w, dict(
                exp_in=exp_in, exp_out=exp_out, m_ready=m_ready, rank_full=rank_full, dest_ready=dest_ready), y_ps)

        @block.tensor
        def _(pe):
            def transposes(src, fill0, count, first=False):
                for i in range(2):
                    if not first:
                        pe.wait_ge(t_free[i], count)
                    for u in range(4):
                        k = 4 * i + u
                        ins = pe.transpose(tb[i][:, u * P:(u + 1) * P], src[:, k * P:(k + 1) * P], ident[:, :])
                    ins.then_inc(t_full, 1)

            def attn_T(n, par, first=False):
                pe.wait_ge(at_in[par], 8 * (n - par) + 16)
                f = at_fill(n)
                transposes(at[:, par, :], f, n if isinstance(n, int) and n < 2 else 2 * n - 2, first)

            def product(n, par):
                pe.wait_ge(t_free[1], n + 1 if isinstance(n, int) and n < 2 else 2 * n - 1)
                pe.wait_ge(t_free[0], n + 1 if isinstance(n, int) and n < 2 else 2 * n - 1)
                if not (isinstance(n, int) and n < 2):
                    pe.wait_ge(x1_ready, n - 1)
                for k in range(DC):
                    for c in range(2):
                        ins = three_pass(pe, y_ps[par][:, c * BANK:(c + 1) * BANK], [t[:, par, k, :] for t in aT],
                                         [t[:, k, c * BANK:(c + 1) * BANK] for t in w_o], k == 0, k == DC - 1)
                ins.then_inc(y_full, 1)

            def router(n, par):
                pe.wait_ge(h2_ready, n + 1)
                late = isinstance(n, int) and n >= NT - 2
                cnt = (2 * NT - 2 + (n - NT + 2)) if late else 2 * n + 3
                transposes(h2[:, par, :], h2_fill(n), cnt)
                for i in range(2):
                    pe.wait_ge(t_free[i], cnt + 1)
                if not (isinstance(n, int) and n < 2):
                    pe.wait_ge(lg_ready, n - 1)
                for k in range(DC):
                    ins = pe.matmul(lg_ps[par][:, 0:4 + EXPERTS], h2T[:, par, k, :], w_r[:, k, :], start=(k == 0), stop=(k == DC - 1))
                ins.then_inc(lg_full, 1)

            pe.wait_ge(small_in, 16 * 14)
            attn_T(0, 0, first=True)
            attn_T(1, 1)
            pe.wait_ge(w_ready, 2)
            product(0, 0)

            def step(t, par):
                attn_T(t + 1, 1 - par)
                product(t, par)
                router(t - 1, 1 - par)

            step(1, 1)
            step(2, 0)
            with pe.Fori(1, (NT - 2) // 2) as i:
                step(2 * i + 1, 1)
                step(2 * i + 2, 0)
            product(NT - 1, 1)
            router(NT - 2, 0)
            router(NT - 1, 1)
            M = w["M"]
            pe.wait_ge(m_ready, 1)
            pe.matmul(y_ps[0][:, 0:BANK], tri[:, :], M[:, :, :].rearrange("p t e -> p (t e)"), start=True, stop=False)
            for t in range(NT - 1):
                ins = pe.matmul(y_ps[0][:, (t + 1) * EXPERTS:NT * EXPERTS].rearrange("p (t e) -> p t e", e=EXPERTS), ones[:, :],
                                M[:, t:t + 1, :].broadcast_to([P, NT - 1 - t, EXPERTS]), start=False, stop=(t == NT - 2))
            for t in range(NT):
                ins = pe.matmul(y_ps[1][:, 0:EXPERTS], ones[:, :], M[:, t, :], start=(t == 0), stop=(t == NT - 1))
            ins.then_inc(rank_full, 1)


def slots_of_tokens(dve, step, lg, cst, keep, w, s, y_ps):
    PG, E = PER_GROUP, EXPERTS
    iota = lambda o, n: cst[:, o:o + n]
    W = w["per_row"]
    gm, gi, e1, e2, i1, i2, z = (W[:, NT * i:NT * (i + 1)] for i in range(7))
    b3 = lambda a, n: a.unsqueeze(2).broadcast_to([P, NT, n])
    row3 = lambda o, n: iota(o, n).unsqueeze(1).broadcast_to([P, NT, n])
    G4 = lg[:, :, 0:4]
    eq, ohg, sel, oh1, oh2 = w["eq"], w["ohg"], w["sel"], w["oh1"], w["oh2"]
    M1, M2, M, big = w["M1"], w["M2"], w["M"], w["big"]
    ex = w["ex"]

    def first_max(src, n, m, idx, onehot):
        step.did(dve.tensor_reduce(m, src, AX.X, ALU.max))
        step.settle()
        step.did(dve.tensor_tensor(eq[:, :, 0:n], src, b3(m, n), ALU.is_equal))
        step.settle()
        step.did(dve.tensor_tensor(eq[:, :, 0:n], eq[:, :, 0:n], row3(KNEG, n), ALU.mult))
        step.settle()
        step.did(dve.tensor_reduce(idx, eq[:, :, 0:n], AX.X, ALU.min))
        step.settle()
        step.did(dve.tensor_tensor(onehot, b3(idx, n), row3(KNEG, n), ALU.is_equal))
        step.settle()

    first_max(G4, 4, gm, gi, ohg[:, :, :])
    g4 = big[:, :].rearrange("p (t g i) -> p t g i", g=4, i=PG)
    step.did(dve.tensor_tensor(g4, lg[:, :, 4:4 + E].rearrange("p t (g i) -> p t g i", g=4),
                               ohg[:, :, :].unsqueeze(3).broadcast_to([P, NT, 4, PG]), ALU.mult))
    step.settle()
    step.did(dve.tensor_reduce(sel[:, :, :], g4.rearrange("p t g i -> p t i g"), AX.X, ALU.add))
    step.settle()
    first_max(sel[:, :, :], PG, e1, i1, oh1[:, :, :])
    step.did(dve.scalar_tensor_tensor(out=sel[:, :, :], in0=oh1[:, :, :], scalar=-BIG, in1=sel[:, :, :], op0=ALU.mult, op1=ALU.add))
    step.settle()
    first_max(sel[:, :, :], PG, e2, i2, oh2[:, :, :])
    for m, oh in ((M1, oh1), (M2, oh2)):
        step.did(dve.tensor_tensor(m[:, :, :].rearrange("p t (g i) -> p t g i", g=4), ohg[:, :, :].unsqueeze(3).broadcast_to([P, NT, 4, PG]),
                                   oh[:, :, :].unsqueeze(2).broadcast_to([P, NT, 4, PG]), ALU.mult))
    step.settle()
    dve.tensor_tensor(M[:, :, :], M1[:, :, :], M2[:, :, :], ALU.add).then_inc(s["m_ready"], 1)
    step.did(dve.tensor_tensor(ex[:, :, 0:4], G4, b3(gm, 4), ALU.subtract))
    step.did(dve.tensor_tensor(ex[:, :, 4], e2, e1, ALU.subtract))
    step.settle()
    dve.nop().then_inc(s["exp_in"], 1)
    dve.wait_ge(s["rank_full"], 1)
    rank = w["rank"]
    step.did(dve.tensor_tensor(rank[:, :, :], y_ps[0][:, 0:NT * E].rearrange("p (t e) -> p t e", e=E), row3(EOFF, E), ALU.add))
    step.settle()
    dest = w["dest"]
    b4 = big[:, :].rearrange("p (t e) -> p t e", e=E)
    for k, m in enumerate((M1, M2)):
        step.did(dve.tensor_tensor(b4, rank[:, :, :], m[:, :, :], ALU.mult))
        step.settle()
        step.did(dve.tensor_reduce(dest[:, k * NT:(k + 1) * NT], b4, AX.X, ALU.add))
        step.settle()
        dve.tensor_copy(w["dest_i"][:, k * NT:(k + 1) * NT], dest[:, k * NT:(k + 1) * NT]).then_inc(s["dest_ready"], 1)
    cnt, nb, be = (w["per_e"][:, i, :] for i in range(3))
    step.did(dve.tensor_copy(cnt, y_ps[1][:, 0:E]))
    step.settle()
    big2 = w["big2"]
    v = big2[:, 0:E * PBLK].rearrange("p (e m) -> p e m", m=PBLK)
    step.did(dve.tensor_tensor(v, cnt.unsqueeze(2).broadcast_to([P, E, PBLK]),
                               iota(THR, PBLK).unsqueeze(1).broadcast_to([P, E, PBLK]), ALU.is_gt))
    step.settle()
    step.did(dve.tensor_reduce(nb, v, AX.X, ALU.add))
    step.settle()
    step.did(dve.tensor_scalar(nb, nb, 1.0, None, ALU.max))
    step.settle()
    v = big2[:, 0:E * E].rearrange("p (e m) -> p e m", m=E)
    ie = iota(IOTA, E)
    step.did(dve.tensor_tensor(v, ie.unsqueeze(1).broadcast_to([P, E, E]), ie.unsqueeze(2).broadcast_to([P, E, E]), ALU.is_le))
    step.settle()
    step.did(dve.tensor_tensor(v, v, nb.unsqueeze(1).broadcast_to([P, E, E]), ALU.mult))
    step.settle()
    step.did(dve.tensor_reduce(be, v, AX.X, ALU.add))
    step.settle()
    v = big2[:, :].rearrange("p (j e) -> p j e", e=E)
    ends = be.unsqueeze(1).broadcast_to([P, NBMAX, E])
    tab_f = w["tab_f"]
    step.did(dve.tensor_tensor(v, ends, iota(IOTA, NBMAX).unsqueeze(2).broadcast_to([P, NBMAX, E]), ALU.is_le))
    step.settle()
    step.did(dve.tensor_reduce(tab_f[:, 0, :], v, AX.X, ALU.add))
    step.settle()
    step.did(dve.tensor_tensor(v, v, ends, ALU.mult))
    step.settle()
    step.did(dve.tensor_reduce(tab_f[:, 1, :], v, AX.X, ALU.max))
    step.did(dve.tensor_scalar(tab_f[:, 0, :], tab_f[:, 0, :], float(E - 1), None, ALU.min))
    step.settle()
    step.did(dve.tensor_tensor(tab_f[:, 1, :], iota(IOTA, NBMAX), tab_f[:, 1, :], ALU.subtract))
    step.settle()
    step.did(dve.tensor_scalar(tab_f[:, 1, :], tab_f[:, 1, :], float(BLK), None, ALU.mult))
    step.settle()
    step.did(dve.scalar_tensor_tensor(out=tab_f[:, 1, :], in0=tab_f[:, 0, :], scalar=float(SLOTS), in1=tab_f[:, 1, :], op0=ALU.mult, op1=ALU.add))
    step.settle()
    step.did(dve.tensor_scalar(tab_f[:, 1, :], tab_f[:, 1, :], float(E * SLOTS - BLK), None, ALU.min))
    step.settle()
    step.did(dve.tensor_tensor(be, be, nb, ALU.subtract))
    step.settle()
    for o, src in ((SLOT_OF, tab_f[:, 1, :]), (BLOCKS_OF, nb), (FIRST_OF, be)):
        step.did(dve.tensor_copy(keep["tables"][:, o:o + src.shape[1]], src))
    dve.wait_ge(s["exp_out"], 1)
    t_ = ex[:, :, 4]
    g1, g2 = keep["gates"][:, 0:NT], keep["gates"][:, NT:2 * NT]
    step.did(dve.tensor_reduce(z, ex[:, :, 0:4], AX.X, ALU.add))
    step.settle()
    step.did(dve.scalar_tensor_tensor(out=z, in0=t_, scalar=1.0, in1=z, op0=ALU.add, op1=ALU.mult))
    step.settle()
    step.did(dve.reciprocal(g1, z))
    step.settle()
    step.did(dve.tensor_tensor(g2, t_, g1, ALU.mult))
    step.settle()


def experts(nc, io, keep):
    ctx = ExitStack()
    with ctx:
        sb = lambda name, shape, dt=F32: ctx.enter_context(nc.sbuf_tensor(f"experts_{name}", shape, dt))
        sem = lambda name: ctx.enter_context(nc.semaphore(f"experts_{name}"))
        bank = lambda name: ctx.enter_context(nc.psum_tensor(f"experts_{name}", [P, BANK], F32))
        ident, tables = keep["ident"], keep["tables"]

        raw = {"gate": sb("gate_raw", [P, DC, FF]), "up": sb("up_raw", [P, DC, FF]), "down": sb("down_raw", [P, FC, D])}
        w = {n: [sb(f"{n}_{s}", [P, 2] + list(r.shape[1:]), F16) for s in ("hi", "lo")] for n, r in raw.items()}
        src = {n: io[f"w_{n}"] for n in raw}
        slots = sb("slots", [P, NTABLE, 2], I32)
        source = sb("source", [P, 1], I32)
        target = sb("target", [P, 1], I32)
        xe = sb("xe", [P, D])
        xT = [sb(f"xT{s}", [P, DC, P], F16) for s in ("hi", "lo")]
        act_g = sb("act_g", [P, FF])
        hid = sb("hid", [P, FF])
        hidT = [sb(f"hidT{s}", [P, FC, P], F16) for s in ("hi", "lo")]
        y_out = sb("y_out", [P, D])

        g_ps, u_ps, h_ps = bank("g_ps"), bank("u_ps"), bank("h_ps")
        x_ps = [bank(f"x_ps{i}") for i in range(2)]
        y_ps = [bank(f"ye_ps{i}") for i in range(2)]

        w_in = {n: sem(f"{n}_in") for n in raw}
        w_hi = {n: sem(f"{n}_hi") for n in raw}
        w_ready = {n: sem(f"{n}_ready") for n in raw}
        slots_in = sem("slots_in")
        picked = sem("picked")
        y_gone = sem("y_gone")
        xe_in = sem("xe_in")
        x_full = sem("x_full")
        x_hi = sem("x_hi")
        x_ready = sem("x_ready")
        g_full = sem("g_full")
        act_ready = sem("act_ready")
        u_full = sem("u_full")
        hid_ready = sem("hid_ready")
        h_full = sem("h_full")
        h_hi = sem("h_hi")
        h_ready = sem("h_ready")
        y_full = sem("y_full")
        y_left = sem("y_left")
        y_right = sem("y_right")
        y_stored = sem("y_stored")
        sp_passed = sem("sp_passed")
        pool_passed = sem("pool_passed")

        def over_experts(eng, first, body, before=None):
            first()

            def one(e, par, last):
                if before:
                    before(e, par, last)
                index = lambda o: tables[0:1, ds(o + e, 1)] if not isinstance(e, int) else tables[0:1, o + e:o + e + 1]
                count = eng.value_load(index(BLOCKS_OF), min_val=1, max_val=PBLK)
                start = eng.value_load(index(FIRST_OF), min_val=0, max_val=LAST_BLOCK)
                body(e, par, count, start, last)

            with eng.Fori(0, EXPERTS // 2 - 1) as ee:
                one(2 * ee, 0, False)
                one(2 * ee + 1, 1, False)
            one(EXPERTS - 2, 0, False)
            one(EXPERTS - 1, 1, True)

        halves = {n: (slice(0, r.shape[1] // 2), slice(r.shape[1] // 2, r.shape[1])) for n, r in raw.items()}
        SPLIT_A = (("gate", 0), ("gate", 1), ("up", 0))
        SPLIT_B = (("up", 1), ("down", 0), ("down", 1))
        block = ctx.enter_context(nc.Block())

        @block.sync
        def _(sp):
            def load(n, e):
                s = src[n][ds(e, 1)] if not isinstance(e, int) else src[n][e:e + 1]
                sp.dma_start(raw[n][:, :, :], s.rearrange("a (k p) n -> p (a k) n", p=P)).then_inc(w_in[n], 16)

            def first():
                for n in raw:
                    load(n, 0)
                for n in raw:
                    sp.wait_ge(w_ready[n], 2)
                    load(n, 1)

            first()
            with sp.Fori(0, EXPERTS - 2) as e:
                for n in raw:
                    wait_alone(sp, w_ready[n], 2 * e + 4, sp_passed)
                    load(n, e + 2)

        @block.gpsimd
        def _(pool):
            def load_slots(j):
                slot = pool.value_load(tables[0:1, ds(SLOT_OF + j, 1)] if not isinstance(j, int) else tables[0:1, j:j + 1],
                                       min_val=0, max_val=EXPERTS * SLOTS - BLK)
                dst = slots[:, ds(j, 1), :] if not isinstance(j, int) else slots[:, j:j + 1, :]
                pool.dma_start(dst.rearrange("p a n -> p (a n)"), io["slots"][ds(slot, BLK), :]).then_inc(slots_in, 16)

            def pick(dst, j, column, n):
                src = slots[:, ds(j, 1), column] if not isinstance(j, int) else slots[:, j:j + 1, column]
                pool.tensor_copy(dst[:, :], src).then_inc(picked, 1)
                wait_alone(pool, picked, n + 1, pool_passed)

            def gather(j, n):
                pick(source, j, 0, n)
                pool.indirect_dma_start(xe[:, :], None, io["h2"], bass.IndirectOffsetOnAxis(ap=source[:, 0:1], axis=0)).then_inc(xe_in, 16)

            def first():
                for j in range(3):
                    load_slots(j)
                    pool.wait_ge(slots_in, 16 * j + 16)
                gather(0, 0)
                pool.wait_ge(x_full, 2)
                gather(1, 1)

            def body(e, par, count, start, last):
                with pool.Fori(0, count) as i:
                    j = start + i
                    load_slots(j + 3)
                    wait_alone(pool, x_full, 2 * j + 4, pool_passed)
                    wait_alone(pool, xe_in, 16 * j + 32, pool_passed)
                    gather(j + 2, 2 * j + 2)
                    pool.wait_ge(y_left, j + 2)
                    wait_alone(pool, y_right, j + 2, pool_passed)
                    pick(target, j, 1, 2 * j + 3)
                    pool.indirect_dma_start(io["y"], bass.IndirectOffsetOnAxis(ap=target[:, 0:1], axis=0), y_out[:, :], None).then_inc(y_stored, 16)
                    wait_alone(pool, y_stored, 16 * j + 16, pool_passed)
                    wait_alone(pool, slots_in, 16 * j + 64, y_gone)

            over_experts(pool, first, body)

        @block.scalar
        def _(act):
            act.sem_inc(y_left, 1)
            act.preload_act_table(ACT.Silu)

            def split(e, par, n, part):
                if part == 0:
                    act.wait_ge(w_in[n], 16 * e + 16)
                k = halves[n][part]
                act.activation(w[n][0][:, par, k, :], raw[n][:, k, :], ACT.Copy, scale=WS).then_inc(w_hi[n], 1)

            def rows_hi(j, i):
                act.wait_ge(x_full, 2 * j + i + 1)
                act.activation(xT[0][:, 4 * i:4 * i + 4, :], x_ps[i][:, :].rearrange("p (k t) -> p k t", k=4), ACT.Copy).then_inc(x_hi, 1)

            def first():
                for n, part in SPLIT_A + SPLIT_B:
                    split(0, 0, n, part)
                for i in range(2):
                    rows_hi(0, i)

            def before(e, par, last):
                if not last:
                    for n, part in SPLIT_A:
                        split(e + 1, 1 - par, n, part)

            def blk(j, more=None):
                act.wait_ge(g_full, j + 1)
                act.wait_ge(hid_ready, j + 1)
                act.activation(act_g[:, :], g_ps[:, :], ACT.Silu, scale=1 / WS).then_inc(act_ready, 1)
                rows_hi(j + 1, 0)
                act.wait_ge(h_full, j + 2)
                act.activation(hidT[0][:, :, :], h_ps[:, :].rearrange("p (k t) -> p k t", k=FC), ACT.Copy).then_inc(h_hi, 1)
                rows_hi(j + 1, 1)
                if more:
                    more()
                act.wait_ge(y_full, j + 2)
                act.wait_ge(y_gone, j + 1)
                act.activation(y_out[:, 0:BANK], y_ps[0][:, :], ACT.Copy, scale=1 / WS).then_inc(y_left, 1)

            def body(e, par, count, start, last):
                def more():
                    for n, part in SPLIT_B:
                        split(e + 1, 1 - par, n, part)
                blk(start, None if last else more)
                with act.If(count > 1):
                    with act.Fori(1, count) as k:
                        blk(start + k)

            act.sem_inc(y_gone, 1)
            over_experts(act, first, body, before)

        @block.vector
        def _(dve):
            for signal in (hid_ready, h_ready, y_right):
                dve.sem_inc(signal, 1)
            def split(e, par, n, part):
                dve.wait_ge(w_hi[n], 2 * e + part + 1)
                k = halves[n][part]
                dve.scalar_tensor_tensor(out=w[n][1][:, par, k, :], in0=raw[n][:, k, :], scalar=WS, in1=w[n][0][:, par, k, :],
                                         op0=ALU.mult, op1=ALU.subtract).then_inc(w_ready[n], 1)

            def rows_lo(j, i):
                dve.wait_ge(x_hi, 2 * j + i + 1)
                dve.tensor_tensor(xT[1][:, 4 * i:4 * i + 4, :], x_ps[i][:, :].rearrange("p (k t) -> p k t", k=4),
                                  xT[0][:, 4 * i:4 * i + 4, :], ALU.subtract).then_inc(x_ready, 1)

            def first():
                for n, part in SPLIT_A + SPLIT_B:
                    split(0, 0, n, part)
                for i in range(2):
                    rows_lo(0, i)

            def before(e, par, last):
                if not last:
                    for n, part in SPLIT_A:
                        split(e + 1, 1 - par, n, part)

            def blk(j, more=None):
                dve.wait_ge(u_full, j + 1)
                dve.wait_ge(act_ready, j + 1)
                dve.wait_ge(h_full, j + 1)
                dve.scalar_tensor_tensor(out=hid[:, :], in0=u_ps[:, :], scalar=1 / WS, in1=act_g[:, :],
                                         op0=ALU.mult, op1=ALU.mult).then_inc(hid_ready, 1)
                rows_lo(j + 1, 0)
                dve.wait_ge(h_hi, j + 1)
                dve.tensor_tensor(hidT[1][:, :, :], h_ps[:, :].rearrange("p (k t) -> p k t", k=FC), hidT[0][:, :, :],
                                  ALU.subtract).then_inc(h_ready, 1)
                rows_lo(j + 1, 1)
                if more:
                    more()
                dve.wait_ge(y_full, j + 2)
                dve.wait_ge(y_gone, j + 1)
                dve.tensor_scalar(y_out[:, BANK:D], y_ps[1][:, :], 1 / WS, None, ALU.mult).then_inc(y_right, 1)

            def body(e, par, count, start, last):
                def more():
                    for n, part in SPLIT_B:
                        split(e + 1, 1 - par, n, part)
                blk(start, None if last else more)
                with dve.If(count > 1):
                    with dve.Fori(1, count) as k:
                        blk(start + k)

            over_experts(dve, first, body, before)

        @block.tensor
        def _(pe):
            for signal in (y_full, h_full):
                pe.sem_inc(signal, 1)
            def transpose_rows(j, i):
                for u in range(4):
                    k = 4 * i + u
                    ins = pe.transpose(x_ps[i][:, u * P:(u + 1) * P], xe[:, k * P:(k + 1) * P], ident[:, :])
                ins.then_inc(x_full, 1)

            def first():
                pe.wait_ge(xe_in, 16)
                transpose_rows(0, 0)
                transpose_rows(0, 1)

            def body(e, par, count, start, last):
                with pe.Fori(0, count) as i:
                    j = start + i
                    pe.wait_ge(x_ready, 2 * j + 2)
                    pe.wait_ge(hid_ready, j + 1)
                    for n, out, full in (("gate", g_ps, g_full), ("up", u_ps, u_full)):
                        pe.wait_ge(w_ready[n], 2 * e + 2)
                        for k in range(DC):
                            ins = three_pass(pe, out[:, :], [t[:, k, :] for t in xT], [t[:, par, k, :] for t in w[n]], k == 0, k == DC - 1)
                        ins.then_inc(full, 1)
                    pe.wait_ge(xe_in, 16 * j + 32)
                    transpose_rows(j + 1, 0)
                    pe.wait_ge(hid_ready, j + 2)
                    for k in range(FC):
                        ins = pe.transpose(h_ps[:, k * P:(k + 1) * P], hid[:, k * P:(k + 1) * P], ident[:, :])
                    ins.then_inc(h_full, 1)
                    transpose_rows(j + 1, 1)
                    pe.wait_ge(h_hi, j + 1)
                    pe.wait_ge(y_left, j + 1)
                    pe.wait_ge(y_right, j + 1)
                    pe.wait_ge(w_ready["down"], 2 * e + 2)
                    for part, k, low in [(0, k, low) for k in range(FC) for low in range(2)] + [(1, k, 0) for k in range(FC)]:
                        if part == 1 and k == 0:
                            pe.wait_ge(h_ready, j + 2)
                        for c in range(2):
                            ins = pe.matmul(y_ps[c][:, :], hidT[part][:, k, :], w["down"][low][:, par, k, c * BANK:(c + 1) * BANK],
                                            start=(part == 0 and k == 0 and low == 0), stop=(part == 1 and k == FC - 1))
                    ins.then_inc(y_full, 1)

            over_experts(pe, first, body)


def combine(nc, io, keep):
    ctx = ExitStack()
    with ctx:
        sb = lambda name, shape, dt=F32: ctx.enter_context(nc.sbuf_tensor(f"combine_{name}", shape, dt))
        sem = lambda name: ctx.enter_context(nc.semaphore(f"combine_{name}"))
        gates, g2b = keep["gates"], keep["g2b"]
        ya = sb("ya", [P, 2, D])
        yb = sb("yb", [P, 2, D])
        xr = sb("xr", [P, 2, D])
        res = sb("res", [P, 2, D])
        sq = sb("sq", [P, D], BF16)
        fg = sb("fg", [P, D])
        ss = sb("ss", [P, 2])
        rms = sb("rms", [P, 2])
        rstd = sb("rstd", [P, 2])
        eps_t = sb("eps_t", [P, 1])


        fg_in = sem("fg_in")
        ya_in = [sem(f"ya_in{i}") for i in range(2)]
        yb_in = [sem(f"yb_in{i}") for i in range(2)]
        xr_in = [sem(f"xr_in{i}") for i in range(2)]
        out_done = [sem(f"out_done{i}") for i in range(2)]
        ya_scaled = sem("ya_scaled")
        x2_ready = sem("x2_ready")
        sq_done = sem("sq_done")
        rms_ready = sem("rms_ready")
        res_ready = sem("res_ready")
        eps_ready = sem("eps_ready")
        dve_step = sem("dve_step")
        sp_passed = sem("sp_passed")
        block = ctx.enter_context(nc.Block())

        @block.sync
        def _(sp):
            for signal in (out_done[0], out_done[1]):
                sp.sem_inc(signal, 1)
            sp.dma_start(fg[:, :], io["final_g"].rearrange("(a n) -> a n", a=1).broadcast_to([P, D])).then_inc(fg_in, 16)

            def load(t, par):
                rows = lambda o: ds(t * P + o, P) if not isinstance(t, int) else slice(t * P + o, t * P + o + P)
                sp.dma_start(ya[:, par, :], io["y"][rows(0), :]).then_inc(ya_in[par], 16)
                sp.dma_start(yb[:, par, :], io["y"][rows(SEQ), :]).then_inc(yb_in[par], 16)
                sp.dma_start(xr[:, par, :], io["x1"][rows(0), :]).then_inc(xr_in[par], 16)

            load(0, 0)
            load(1, 1)
            with sp.Fori(0, NT // 2 - 1) as i:
                for par in range(2):
                    t = 2 * i + par
                    wait_alone(sp, res_ready, t + 1, sp_passed)
                    sp.dma_start(io["out"][ds(t * P, P), :], res[:, par, :]).then_inc(out_done[par], 16)
                    load(t + 2, par)
            for t in (NT - 2, NT - 1):
                sp.wait_ge(res_ready, t + 1)
                sp.dma_start(io["out"][t * P:(t + 1) * P, :], res[:, t % 2, :]).then_inc(out_done[t % 2], 16)
            for par in range(2):
                sp.wait_ge(out_done[par], 8 * NT + 1)

        @block.scalar
        def _(act):
            act.sem_inc(rms_ready, 1)
            act.preload_act_table(ACT.Sqrt)
            act.wait_ge(eps_ready, 1)
            with act.Fori(0, NT // 2) as i:
                for par in range(2):
                    t = 2 * i + par
                    act.wait_ge(ya_in[par], 16 * i + 16)
                    act.activation(ya[:, par, :], ya[:, par, :], ACT.Copy, scale=gates[:, ds(t, 1)]).then_inc(ya_scaled, 1)
                    act.wait_ge(x2_ready, t + 1)
                    act.wait_ge(rms_ready, t + 1)
                    act.activation(sq[:, :], xr[:, par, :], ACT.Square, accum_out=ss[:, par:par + 1]).then_inc(sq_done, 1)
                    act.wait_ge(sq_done, t + 1)
                    act.activation(rms[:, par:par + 1], ss[:, par:par + 1], ACT.Sqrt, bias=eps_t[:, :], scale=1.0 / D).then_inc(rms_ready, 1)

        @block.vector
        def _(dve):
            step = Steps(dve, dve_step)
            dve.memset(eps_t[:, :], EPS).then_inc(eps_ready, 1)
            dve.wait_ge(fg_in, 16)
            PER = 5
            with dve.Fori(0, NT // 2) as i:
                step.enter(i * (2 * PER), 2 * PER)
                for par in range(2):
                    t = 2 * i + par
                    y = yb[:, par, :]
                    dve.wait_ge(ya_scaled, t + 1)
                    dve.wait_ge(yb_in[par], 16 * i + 16)
                    step.did(dve.scalar_tensor_tensor(out=y, in0=y, scalar=gates[:, ds(NT + t, 1)], in1=ya[:, par, :],
                                                      op0=ALU.mult, op1=ALU.add))
                    step.settle()
                    step.did(dve.tensor_tensor(y, y, g2b[:, :], ALU.mult))
                    dve.wait_ge(xr_in[par], 16 * i + 16)
                    step.settle()
                    step.did(dve.tensor_tensor(xr[:, par, :], xr[:, par, :], y, ALU.add))
                    step.settle()
                    dve.nop().then_inc(x2_ready, 1)
                    dve.wait_ge(rms_ready, t + 2)
                    step.did(dve.reciprocal(rstd[:, par:par + 1], rms[:, par:par + 1]))
                    dve.wait_ge(out_done[par], 16 * i + 1)
                    step.settle()
                    step.did(dve.scalar_tensor_tensor(out=res[:, par, :], in0=xr[:, par, :], scalar=rstd[:, par:par + 1],
                                                      in1=fg[:, :], op0=ALU.mult, op1=ALU.mult))
                    step.settle()
                    dve.nop().then_inc(res_ready, 1)
            step.leave(NT // 2)




def build(nc, io):
    scratch = lambda name, shape, dt=F32: nc.dram_tensor(name, shape, dt, kind="Internal").ap()
    io["mod_rows"] = scratch("mod_rows", (1, 4 * D))
    io["attn"] = scratch("attn", (SEQ, HEADS * VD))
    io["x1"] = scratch("x1", (SEQ, D))
    io["h2"] = scratch("h2", (SEQ, D))
    io["slots"] = scratch("slots", (EXPERTS * SLOTS, 2), I32)
    io["y"] = scratch("y", (TOPK * SEQ + BLK, D))
    with ExitStack() as whole:
        ident = whole.enter_context(nc.sbuf_tensor("ident", [P, P], F32))
        with ExitStack() as latents:
            sb = lambda name, shape: latents.enter_context(nc.sbuf_tensor(name, shape, F16))
            keep = {
                "ident": ident,
                "cqT": [sb(f"cqT_{s}", [P, RC, SEQ]) for s in ("hi", "lo")],
                "ckvT": [sb(f"ckvT_{s}", [P, KC, KEYS]) for s in ("hi", "lo")],
                "krT": [sb(f"krT_{s}", [P, KEYS]) for s in ("hi", "lo")],
                "qrT": sb("qrT", [P, HEADS, SEQ]),
            }
            project(nc, io, keep)
            attend(nc, io, keep)
        sb = lambda name, shape, dt=F32: whole.enter_context(nc.sbuf_tensor(name, shape, dt))
        keep = {"ident": ident, "g2b": sb("g2b", [P, D]), "gates": sb("gates", [P, TOPK * NT]),
                "tables": sb("tables", [P, NTABLE], I32)}
        route(nc, io, keep)
        experts(nc, io, keep)
        combine(nc, io, keep)


def rotary_tables():
    n = ROPE // 4
    freq = (np.float32(ROPE_THETA) ** (-np.arange(n, dtype=np.float32) / np.float32(n))).astype(np.float32)
    t = np.arange(SEQ)
    row, col = (t // GRID_W).astype(np.float32), (t % GRID_W).astype(np.float32)
    angle = np.concatenate([row[:, None] * freq, col[:, None] * freq], -1)
    tile = lambda a: np.ascontiguousarray(a.astype(np.float32).reshape(KT, P, HALF).transpose(1, 0, 2))
    return (tile(np.concatenate([np.cos(angle), np.ones((CTX, HALF))])),
            tile(np.concatenate([np.sin(angle), np.zeros((CTX, HALF))])))


def constants():
    cos, sin = rotary_tables()
    e, s = np.arange(EXPERTS), np.arange(EXPERTS * SLOTS // P)
    token = np.arange(SEQ, dtype=np.int32).reshape(NT, P).T
    return {
        "ident": np.eye(P, dtype=np.float32), "cos": cos, "sin": sin,
        "tri": np.triu(np.ones((P, P), np.float32), 1),
        "row_consts": np.concatenate([np.arange(NBMAX) - NBMAX, np.arange(NBMAX), e * SLOTS, np.arange(PBLK) * BLK])[None].astype(np.float32),
        "tok": np.stack([np.stack([token, token + k * SEQ], -1) for k in range(TOPK)], 1).astype(np.int32),
        "empty_slots": np.broadcast_to(np.stack([0 * s, TOPK * SEQ + s % BLK], -1).reshape(-1), (P, 2 * len(s))).astype(np.int32),
    }


def kernel(**inputs):
    import concourse.bacc as bacc
    from concourse.bass_utils import run_bass_kernel_spmd

    a = {k: np.asarray(v) for k, v in inputs.items()}
    w_uq = a["mla_w_uq"][0].reshape(Q_RANK, HEADS, QK)
    w_ukv = a["mla_w_ukv"][0].reshape(KV_RANK, HEADS, KV)
    arrays = {
        "xc": np.concatenate([a["x"][0], a["ctx"][0]]), "c": a["c"][0], "c_ctx": a["c_ctx"],
        "mod_w": a["mod_w"][0], "mod_b": a["mod_b"][0], "norm1_g": a["norm1_g"][0], "norm2_g": a["norm2_g"][0],
        "final_g": a["final_g"], "g_q": a["mla_g_q"][0], "g_kv": a["mla_g_kv"][0],
        "w_dq": a["mla_w_dq"][0], "w_dkv": a["mla_w_dkv"][0],
        "w_uq_rope": w_uq[:, :, NOPE:].reshape(Q_RANK, HEADS * ROPE),
        "w_uq": w_uq[:, :, :NOPE].transpose(1, 0, 2),
        "w_uk": w_ukv[:, :, :NOPE].transpose(1, 0, 2), "w_uv": w_ukv[:, :, NOPE:].transpose(1, 0, 2),
        "w_o": a["mla_w_o"][0],
        "w_r": np.concatenate([a["moe_w_grp"][0], a["moe_w_rt"][0]], 1),
        "b_r": np.concatenate([a["moe_b_grp"][0], a["moe_b_rt"][0]]),
        "w_gate": a["moe_w_gate"][0], "w_up": a["moe_w_up"][0], "w_down": a["moe_w_down"][0],
        **constants(),
    }
    arrays = {f"in_{k}": np.ascontiguousarray(v) for k, v in arrays.items()}
    nc = bacc.Bacc("TRN2", target_bir_lowering=False, num_devices=1)
    io = {k[3:]: nc.dram_tensor(k, v.shape, mybir.dt.from_np(v.dtype), kind="ExternalInput").ap() for k, v in arrays.items()}
    io["out"] = nc.dram_tensor("out", (SEQ, D), F32, kind="ExternalOutput").ap()
    build(nc, io)
    r = run_bass_kernel_spmd(nc, [arrays], core_ids=[0])
    return r.results[0]["out"].reshape(1, SEQ, D)
```

```python
from contextlib import ExitStack

import numpy as np

import concourse.bass as bass
from concourse import mybir
from concourse.alu_op_type import AluOpType as ALU

F32, F16, BF16, I32 = mybir.dt.float32, mybir.dt.float16, mybir.dt.bfloat16, mybir.dt.int32
ACT = mybir.ActivationFunctionType
AX = mybir.AxisListType
ds = bass.ds

P = 128
D = 1024
SEQ, CTX = 2048, 256
KEYS = SEQ + CTX
GRID_W = 64
EPS = 1e-6
ROPE_THETA = 10000.0
HEADS, Q_RANK, KV_RANK, NOPE, ROPE, VD = 8, 512, 256, 128, 64, 128
HALF = ROPE // 2
QK = NOPE + ROPE
KV = NOPE + VD
SOFTMAX_SCALE = float(QK) ** -0.5
GROUPS_E, PER_GROUP = 4, 8
EXPERTS = GROUPS_E * PER_GROUP
TOPK = 2
FF = 512
BLK = 128

DC = D // P
RC = Q_RANK // P
KC = KV_RANK // P
FC = FF // P
BANK = 512
G = 256
TG = G // P
NG = KEYS // G
NGL = SEQ // G
NT = SEQ // P
KT = KEYS // P
WS = 64.0
LOG_P_SCALE = 6.931471805599453


class Steps:

    def __init__(self, eng, sem):
        self.eng, self.sem, self.base, self.n = eng, sem, 0, 0

    def did(self, ins):
        ins.then_inc(self.sem, 1)
        self.n += 1

    def settle(self):
        if not isinstance(self.base, int) or self.base + self.n:
            self.eng.wait_ge(self.sem, self.base + self.n)

    def enter(self, before, per):
        self.outer, self.per = self.base + self.n, per
        self.base, self.n = self.outer + before, 0

    def leave(self, count):
        assert self.n == self.per, (self.n, self.per)
        self.base, self.n = self.outer + count * self.per, 0


def wait_alone(eng, sem, value, passed):
    eng.wait_ge(sem, value)
    eng.sem_inc(passed, 1)


def three_pass(pe, out, lhs, rhs, first, last):
    pe.matmul(out, lhs[0], rhs[0], start=first, stop=False)
    pe.matmul(out, lhs[0], rhs[1], start=False, stop=False)
    return pe.matmul(out, lhs[1], rhs[0], start=False, stop=last)


def project(nc, io, keep):
    ctx = ExitStack()
    with ctx:
        sb = lambda name, shape, dt=F32: ctx.enter_context(nc.sbuf_tensor(f"project_{name}", shape, dt))
        sem = lambda name: ctx.enter_context(nc.semaphore(f"project_{name}"))
        bank = lambda name: ctx.enter_context(nc.psum_tensor(f"project_{name}", [P, BANK], F32))

        cqT, ckvT, krT, qrT, ident = keep["cqT"], keep["ckvT"], keep["krT"], keep["qrT"], keep["ident"]

        x_t = sb("x_t", [P, TG, D])
        junk = sb("junk", [P, D], BF16)
        hT = [keep["shared"][:, 1, i * 2 * DC * G:(i + 1) * 2 * DC * G].rearrange("p (a k t) -> p a k t", a=2, k=DC) for i in range(2)]
        f_t = sb("f_t", [P, 2, BANK])
        w_dq = [sb(f"w_dq{s}", [P, DC, Q_RANK], F16) for s in ("hi", "lo")]
        w_dkv = [sb(f"w_dkv{s}", [P, DC, KV_RANK + ROPE], F16) for s in ("hi", "lo")]
        w_qr = [sb(f"w_qr{s}", [P, RC, HEADS * ROPE], F16) for s in ("hi", "lo")]
        stage = keep["shared"][:, 0, :].bitcast(F32).rearrange("p (k n) -> p k n", k=DC)
        cqn = sb("cqn", [P, TG, Q_RANK])
        ckn = sb("ckn", [P, TG, KV_RANK])
        k_raw = sb("k_raw", [P, TG, ROPE])
        k_rot = sb("k_rot", [P, TG, 2 * ROPE])
        q_raw = sb("q_raw", [P, HEADS, ROPE])
        q_rot = sb("q_rot", [P, TG, HEADS, 2 * ROPE])
        rt = [sb(f"rt{i}", [P, HEADS, HALF]) for i in range(4)]
        cos_t = sb("cos_t", [P, KT, HALF])
        sin_t = sb("sin_t", [P, KT, HALF])
        mod_acc = sb("mod_acc", [P, BANK])
        mod_row = sb("mod_row", [1, BANK])
        ones = sb("ones", [P, 1])
        cond_in = sb("cond_in", [P, DC, 2])
        cond = sb("cond", [P, DC, 2])
        modb_col = sb("modb_col", [P, 2 * DC])
        g1_col = sb("g1_col", [P, DC])
        gq_col = sb("gq_col", [P, RC])
        gkv_col = sb("gkv_col", [P, KC])
        shsc = sb("shsc", [P, 2 * DC, 2])
        aff = sb("aff", [P, DC, 2])
        ssum = sb("ssum", [P, 6])
        rms = sb("rms", [P, 6])
        rstd = sb("rstd", [P, 6])
        eps_t = sb("eps_t", [P, 1])
        mod_two = q_rot[:, :, :, :].rearrange("p j h r -> p (j h r)").rearrange("p (i n) -> p i n", i=4)
        as_stage = lambda t: t.rearrange("p h t -> p (h t)").bitcast(F32).rearrange("p (k n) -> p k n", k=DC)
        early = [as_stage(qrT[:, 4 * i:4 * i + 4, :]) for i in range(2)] + [as_stage(t[:, :, :]) for t in cqT]

        tb = [bank(f"tb{i}") for i in range(2)]
        cq_ps = [bank(f"cq_ps{i}") for i in range(TG)]
        ck_ps = [bank(f"ck_ps{i}") for i in range(TG)]
        qr_ps, mr_ps = bank("qr_ps"), bank("mr_ps")
        two_ps = cq_ps + ck_ps

        small_in = sem("small_in")
        ident_in = sem("ident_in")
        rope_in = sem("rope_in")
        slot_in = [sem(f"slot_in{i}") for i in range(5)]
        x_in = sem("x_in")
        cond_ready = sem("cond_ready")
        mod_read = sem("mod_read")
        two_ready = sem("two_ready")
        cols_full = sem("cols_full")
        aff_ready = sem("aff_ready")
        w_hi = sem("w_hi")
        w_ready = sem("w_ready")
        stats = sem("stats")
        rms_ready = sem("rms_ready")
        dve_step = sem("dve_step")
        xn_ready = sem("xn_ready")
        t_full = sem("t_full")
        t_copied = sem("t_copied")
        t_free = sem("t_free")
        cq_full = sem("cq_full")
        ck_full = sem("ck_full")
        cqn_ready = sem("cqn_ready")
        ckn_ready = sem("ckn_ready")
        k_rot_ready = sem("k_rot_ready")
        qr_full = sem("qr_full")
        q_raw_ready = sem("q_raw_ready")
        q_rot_ready = sem("q_rot_ready")
        acc_ready = sem("acc_ready")
        mr_full = sem("mr_full")
        mod_row_ready = sem("mod_row_ready")
        mod_row_out = sem("mod_row_out")
        ones_ready = sem("ones_ready")
        sp_passed = sem("sp_passed")

        slots = [stage] + early
        mod_v = io["mod_w"].rearrange("(k p) n -> p k n", p=P)
        loads = [(1, "mod0"), (2, "mod1"), (3, "mod2"), (0, "dq"), (4, "mod3"), (1, "dkv"), (2, "qr")]
        weights = {
            "dq": (io["w_dq"].rearrange("(k p) n -> p k n", p=P), w_dq, DC, Q_RANK),
            "dkv": (io["w_dkv"].rearrange("(k p) n -> p k n", p=P), w_dkv, DC, KV_RANK + ROPE),
            "qr": (io["w_uq_rope"].rearrange("(k p) n -> p k n", p=P), w_qr, RC, HEADS * ROPE),
        }
        seen = [0] * len(slots)
        nth = {}
        for s, what in loads:
            seen[s] += 1
            nth[what] = (s, seen[s])

        def slot_view(what):
            s = slots[nth[what][0]]
            if what.startswith("mod"):
                return s[:, :, :]
            _, _, k, n = weights[what]
            return s[:, :, :].rearrange("p k n -> p (k n)")[:, 0:k * n].rearrange("p (k n) -> p k n", k=k)

        def wait_slot(eng, what):
            s, n = nth[what]
            eng.wait_ge(slot_in[s], 16 * n)

        PASS = 12
        T_CQ, T_CKV, T_KR, T_X, T_QR = 0, 2, 3, 4, 8

        def fill(g, what):
            if isinstance(g, int):
                if g == 0:
                    return 4 + what - T_X
                if g >= NGL:
                    return PASS * NGL - 4 + (what - 4 if what == T_QR else what)
            return PASS * g - 4 + what

        CTX_FILL = PASS * NGL - 4 + 8

        block = ctx.enter_context(nc.Block())

        @block.sync
        def _(sp):
            sp.sem_inc(mod_row_out, 1)
            for dst, src in ((cond_in[:, :, 0], io["c"]), (cond_in[:, :, 1], io["c_ctx"])):
                sp.dma_start(dst, src.rearrange("(k p) -> p k", p=P), allow_slow_non_contiguous=True).then_inc(small_in, 16)
            for dst, src in ((modb_col, io["mod_b"][0:2 * D]), (g1_col, io["norm1_g"]),
                             (gq_col, io["g_q"]), (gkv_col, io["g_kv"])):
                sp.dma_start(dst[:, :], src.rearrange("(k p) -> p k", p=P), allow_slow_non_contiguous=True).then_inc(small_in, 16)

            def load(what):
                src = mod_v[:, :, int(what[3]) * BANK:(int(what[3]) + 1) * BANK] if what.startswith("mod") else weights[what][0]
                sp.dma_start(slot_view(what), src).then_inc(slot_in[nth[what][0]], 16)

            load("mod0")
            load("mod1")
            sp.dma_start(ident[:, :], io["ident"]).then_inc(ident_in, 16)
            sp.dma_start(x_t[:, :, :], io["xc"][0:G, :].rearrange("(j p) d -> p j d", p=P)).then_inc(x_in, 16)
            load("mod2")
            load("dq")
            load("mod3")
            for what, used in (("dkv", 1), ("qr", 2)):
                sp.wait_ge(mod_read, used)
                load(what)
            sp.dma_start(cos_t[:, :, :], io["cos"]).then_inc(rope_in, 16)
            sp.dma_start(sin_t[:, :, :], io["sin"]).then_inc(rope_in, 16)
            sp.wait_ge(w_ready, 1)

            def step(g, transposed):
                cols = ds(2 * D + g * BANK, BANK) if not isinstance(g, int) else slice(2 * D + g * BANK, 2 * D + (g + 1) * BANK)
                rows = ds(g * G + G, G) if not isinstance(g, int) else slice(g * G + G, g * G + 2 * G)
                out = ds(g * BANK, BANK) if not isinstance(g, int) else slice(g * BANK, (g + 1) * BANK)
                sp.dma_start(stage[:, :, :], mod_v[:, :, cols]).then_inc(slot_in[0], 16)
                wait_alone(sp, t_full, transposed, sp_passed)
                sp.dma_start(x_t[:, :, :], io["xc"][rows, :].rearrange("(j p) d -> p j d", p=P)).then_inc(x_in, 16)
                wait_alone(sp, mod_row_ready, g + 1, sp_passed)
                sp.dma_start(io["mod_rows"][:, out], mod_row[0:1, :]).then_inc(mod_row_out, 16)
                wait_alone(sp, acc_ready, g + 1, sp_passed)

            step(0, 4)
            step(1, fill(0, T_X) + 4)
            with sp.Fori(2, NGL) as g:
                step(g, fill(g - 1, T_X) + 4)
            sp.wait_ge(mod_row_out, 16 * NGL + 1)

        @block.scalar
        def _(act):
            act.preload_act_table(ACT.Silu)
            act.wait_ge(small_in, 6 * 16)
            act.activation(cond[:, :, :], cond_in[:, :, :], ACT.Silu).then_inc(cond_ready, 1)
            act.preload_act_table(ACT.Sqrt)

            def weight_hi(what):
                wait_slot(act, what)
                act.activation(weights[what][1][0][:, :, :], slot_view(what), ACT.Copy, scale=WS).then_inc(w_hi, 1)

            def mod_rows_copy(i):
                act.wait_ge(mod_read, i + 1)
                act.activation(mod_two[0:2, i, :], two_ps[i][0:2, :], ACT.Copy).then_inc(two_ready, 1)

            stat = Steps(act, stats)

            def squares(src, i):
                stat.settle()
                stat.did(act.activation(junk[:, 0:src.shape[1]], src, ACT.Square, accum_out=ssum[:, i:i + 1]))

            def root(lo, hi, n, scale):
                stat.settle()
                act.activation(rms[:, lo:hi], ssum[:, lo:hi], ACT.Sqrt, bias=eps_t[:, :], scale=1.0 / (n * scale * scale)).then_inc(rms_ready, 1)

            def prep():
                for j in range(TG):
                    squares(x_t[:, j, :], j)
                root(0, TG, D, 1.0)

            def hi_part(hi, i, chunks):
                stat.settle()
                act.activation(hi, f_t[:, i, :].rearrange("p (k t) -> p k t", k=chunks), ACT.Copy).then_inc(t_copied, 1)

            def h_fills(n0, c, half, par):
                for i in (2 * half, 2 * half + 1):
                    act.wait_ge(t_full, n0 + i + 1)
                    for u in range(2):
                        k = 2 * i + u
                        stat.did(act.activation(f_t[:, i % 2, u * G:(u + 1) * G], tb[i % 2][:, u * G:(u + 1) * G],
                                                ACT.Identity, bias=shsc[:, k, c:c + 1], scale=aff[:, k, c:c + 1]))
                    hi_part(hT[0][:, par, 2 * i:2 * i + 2, :], i % 2, 2)

            def q_stats(g, j):
                act.wait_ge(cq_full, TG * g + j + 1)
                squares(cq_ps[j][:, :], 2 + j)
                root(2 + j, 3 + j, Q_RANK, WS)

            def kv_stats(g, j):
                act.wait_ge(ck_full, TG * g + j + 1)
                act.activation(k_raw[:, j, :], ck_ps[j][:, KV_RANK:KV_RANK + ROPE], ACT.Copy, scale=1 / WS)
                squares(ck_ps[j][:, 0:KV_RANK], 4 + j)
                root(4 + j, 5 + j, KV_RANK, WS)

            def q_fills(n0, g):
                for i in range(2):
                    act.wait_ge(t_full, n0 + i + 1)
                    for u in range(2):
                        stat.did(act.activation(f_t[:, i, u * G:(u + 1) * G], tb[i][:, u * G:(u + 1) * G],
                                                ACT.Copy, scale=gq_col[:, 2 * i + u:2 * i + u + 1]))
                    hi_part(cqT[0][:, 2 * i:2 * i + 2, ds(g * G, G)], i, 2)

            def kv_fills(n0, g):
                act.wait_ge(t_full, n0 + 1)
                for u in range(KC):
                    stat.did(act.activation(f_t[:, 0, u * G:(u + 1) * G], tb[0][:, u * G:(u + 1) * G],
                                            ACT.Copy, scale=gkv_col[:, u:u + 1]))
                hi_part(ckvT[0][:, :, ds(g * G, G)], 0, KC)
                act.wait_ge(t_full, n0 + 2)
                act.activation(krT[0][:, ds(g * G, G)], tb[1][:, 0:G], ACT.Copy).then_inc(t_copied, 1)

            def q_copy(g, j):
                act.wait_ge(qr_full, TG * g + j + 1)
                act.wait_ge(q_rot_ready, TG * g + j + 1)
                act.activation(q_raw[:, :, :], qr_ps[:, :].rearrange("p (h r) -> p h r", h=HEADS), ACT.Copy,
                               scale=1 / WS).then_inc(q_raw_ready, 1)

            def qr_fills(n0, g):
                for j in range(TG):
                    for u in range(2):
                        act.wait_ge(t_full, n0 + 2 * j + u + 1)
                        act.activation(qrT[:, 4 * u:4 * u + 4, ds(g * G + j * P, P)],
                                       tb[u][:, :].rearrange("p (h t) -> p h t", h=4), ACT.Copy).then_inc(t_copied, 1)

            mod_rows_copy(0)
            mod_rows_copy(1)
            act.wait_ge(ones_ready, 2)
            act.wait_ge(x_in, 16)
            prep()
            weight_hi("dq")
            mod_rows_copy(2)
            weight_hi("dkv")
            mod_rows_copy(3)
            act.wait_ge(aff_ready, 1)
            for half in range(2):
                h_fills(0, 0, half, 0)
            weight_hi("qr")

            def group(g, par, c_next=0):
                old = not (isinstance(g, int) and g == 0)
                latent = not (isinstance(g, int) and g == NGL)
                if latent:
                    act.wait_ge(x_in, 16 * g + 32)
                    prep()
                    q_stats(g, 0)
                if old:
                    q_fills(fill(g, T_CQ), g - 1)
                kv_stats(g, 0)
                if old:
                    kv_fills(fill(g, T_CKV), g - 1)
                if latent:
                    q_stats(g, 1)
                    h_fills(fill(g, T_X), c_next, 0, par)
                kv_stats(g, 1)
                if latent:
                    act.wait_ge(mr_full, g + 2)
                    act.wait_ge(mod_row_out, 16 * g + 1)
                    act.activation(mod_row[0:1, :], mr_ps[0:1, :], ACT.Copy).then_inc(mod_row_ready, 1)
                if old:
                    q_copy(g - 1, 0)
                if latent:
                    h_fills(fill(g, T_X), c_next, 1, par)
                if old:
                    q_copy(g - 1, 1)
                    qr_fills(fill(g, T_QR), g - 1)

            PER = 3 * TG + 2 * (2 + 1 + 4)
            group(0, 1)
            group(1, 0)
            with act.Fori(1, NGL // 2 - 1) as i:
                stat.enter((i - 1) * (2 * PER), 2 * PER)
                group(2 * i, 1)
                group(2 * i + 1, 0)
            stat.leave(NGL // 2 - 2)
            group(NGL - 2, 1)
            group(NGL - 1, 0, 1)
            group(NGL, 1)
            kv_fills(CTX_FILL, NGL)

        @block.vector
        def _(dve):
            dve.sem_inc(q_rot_ready, 1)
            step = Steps(dve, dve_step)
            dve.memset(ones[:, :], 1.0).then_inc(ones_ready, 1)
            dve.memset(eps_t[:, :], EPS).then_inc(ones_ready, 1)
            def inverse_rms(n, lo, hi):
                dve.wait_ge(rms_ready, n + 1)
                step.did(dve.reciprocal(rstd[:, lo:hi], rms[:, lo:hi]))
                step.settle()

            def prep(n):
                inverse_rms(n, 0, TG)
                for j in range(TG):
                    dve.tensor_scalar(x_t[:, j, :], x_t[:, j, :], rstd[:, j:j + 1], None, ALU.mult).then_inc(xn_ready, 1)

            def split(src, hi, lo):
                dve.tensor_tensor(lo, src, hi, ALU.subtract).then_inc(t_free, 1)

            def h_fills(n0, par, half):
                for i in (2 * half, 2 * half + 1):
                    dve.wait_ge(t_copied, n0 + i + 1)
                    split(f_t[:, i % 2, :].rearrange("p (k t) -> p k t", k=2),
                          hT[0][:, par, 2 * i:2 * i + 2, :], hT[1][:, par, 2 * i:2 * i + 2, :])

            def split_weight(n, what):
                dve.wait_ge(w_hi, n + 1)
                hi, lo = (t[:, :, :] for t in weights[what][1])
                dve.scalar_tensor_tensor(out=lo, in0=slot_view(what), scalar=WS, in1=hi,
                                         op0=ALU.mult, op1=ALU.subtract).then_inc(w_ready, 1)

            prep(0)
            split_weight(0, "dq")
            split_weight(1, "dkv")
            dve.wait_ge(small_in, 6 * 16)
            dve.wait_ge(cols_full, 1)
            step.did(dve.tensor_tensor(shsc[:, :, :], mr_ps[:, 0:4 * DC].rearrange("p (k c) -> p k c", c=2),
                                       modb_col[:, :].unsqueeze(2).broadcast_to([P, 2 * DC, 2]), ALU.add))
            step.settle()
            dve.scalar_tensor_tensor(out=aff[:, :, :], in0=shsc[:, DC:2 * DC, :], scalar=1.0,
                                     in1=g1_col[:, :].unsqueeze(2).broadcast_to([P, DC, 2]),
                                     op0=ALU.add, op1=ALU.mult).then_inc(aff_ready, 1)
            for half in range(2):
                h_fills(0, 0, half)
            split_weight(2, "qr")
            dve.wait_ge(rope_in, 32)

            def q_normed(n, j):
                inverse_rms(n, 2 + j, 3 + j)
                dve.tensor_scalar(cqn[:, j, :], cq_ps[j][:, :], rstd[:, 2 + j:3 + j], 1 / WS, ALU.mult, ALU.mult).then_inc(cqn_ready, 1)

            def kv_normed(n, j):
                inverse_rms(n, 4 + j, 5 + j)
                dve.tensor_scalar(ckn[:, j, :], ck_ps[j][:, 0:KV_RANK], rstd[:, 4 + j:5 + j], 1 / WS, ALU.mult, ALU.mult).then_inc(ckn_ready, 1)

            def rotate(x, cs, sn, out, dup, n, ready):
                x1, x2 = x[:, :, 0:HALF], x[:, :, HALF:ROPE]
                a, b, c, d = (t[:, 0:n, :] for t in rt)
                for o, x_, w in ((a, x1, cs), (b, x2, sn), (c, x1, sn), (d, x2, cs)):
                    step.did(dve.tensor_tensor(o, x_, w, ALU.mult))
                step.settle()
                step.did(dve.tensor_tensor(out[:, :, 0:HALF], a, b, ALU.subtract))
                step.did(dve.tensor_tensor(out[:, :, HALF:ROPE], c, d, ALU.add))
                step.settle()
                dve.tensor_copy(dup, out).then_inc(ready, 1)

            def rotate_keys(g):
                rotate(k_raw[:, :, :], cos_t[:, ds(g * TG, TG), :], sin_t[:, ds(g * TG, TG), :],
                       k_rot[:, :, 0:ROPE], k_rot[:, :, ROPE:2 * ROPE], TG, k_rot_ready)

            def q_fills(n0, g):
                for i in range(2):
                    dve.wait_ge(t_copied, n0 + i + 1)
                    split(f_t[:, i, :].rearrange("p (k t) -> p k t", k=2),
                          cqT[0][:, 2 * i:2 * i + 2, ds(g * G, G)], cqT[1][:, 2 * i:2 * i + 2, ds(g * G, G)])

            def kv_fills(n0, g):
                dve.wait_ge(t_copied, n0 + 1)
                split(f_t[:, 0, :].rearrange("p (k t) -> p k t", k=KC),
                      ckvT[0][:, :, ds(g * G, G)], ckvT[1][:, :, ds(g * G, G)])
                dve.wait_ge(t_copied, n0 + 2)
                dve.tensor_tensor(krT[1][:, ds(g * G, G)], tb[1][:, 0:G], krT[0][:, ds(g * G, G)],
                                  ALU.subtract).then_inc(t_free, 1)

            def gate_columns(g, k0, k1):
                if k0 == 0:
                    dve.wait_ge(slot_in[0], 16 * g + 32)
                    dve.wait_ge(mr_full, g + 1)
                for k in range(k0, k1):
                    if k == 0:
                        step.did(dve.tensor_scalar(mod_acc[:, :], stage[:, 0, :], cond[:, 0, 0:1], None, ALU.mult))
                        continue
                    step.settle()
                    ins = dve.scalar_tensor_tensor(out=mod_acc[:, :], in0=stage[:, k, :], scalar=cond[:, k, 0:1],
                                                   in1=mod_acc[:, :], op0=ALU.mult, op1=ALU.add)
                    if k < DC - 1:
                        step.did(ins)
                    else:
                        ins.then_inc(acc_ready, 1)

            def rotate_queries(g, j):
                dve.wait_ge(q_raw_ready, TG * g + j + 1)
                cs = cos_t[:, ds(g * TG + j, 1), :].broadcast_to([P, HEADS, HALF])
                sn = sin_t[:, ds(g * TG + j, 1), :].broadcast_to([P, HEADS, HALF])
                rotate(q_raw[:, :, :], cs, sn, q_rot[:, j, :, 0:ROPE], q_rot[:, j, :, ROPE:2 * ROPE], HEADS, q_rot_ready)

            def qr_fills(n0, g):
                for j in range(TG):
                    for u in range(2):
                        dve.wait_ge(t_copied, n0 + 2 * j + u + 1)
                        lo = qrT[ROPE:P, 4 * u:4 * u + 4, ds(g * G + j * P, P)]
                        dve.tensor_tensor(lo, tb[u][ROPE:P, :].rearrange("p (h t) -> p h t", h=4), lo,
                                          ALU.subtract).then_inc(t_free, 1)

            ROOTS = 1 + 2 * TG

            def group(g, par):
                old = not (isinstance(g, int) and g == 0)
                latent = not (isinstance(g, int) and g == NGL)
                n = 1 + ROOTS * g
                if latent:
                    prep(n)
                    gate_columns(g, 0, 4)
                if old:
                    q_fills(fill(g, T_CQ), g - 1)
                if latent:
                    q_normed(n + 1, 0)
                    gate_columns(g, 4, DC)
                if old:
                    kv_fills(fill(g, T_CKV), g - 1)
                kv_normed(n + 2 if latent else n, 0)
                if latent:
                    h_fills(fill(g, T_X), par, 0)
                    q_normed(n + 3, 1)
                kv_normed(n + 4 if latent else n + 1, 1)
                rotate_keys(g)
                if old:
                    rotate_queries(g - 1, 0)
                if latent:
                    h_fills(fill(g, T_X), par, 1)
                if old:
                    rotate_queries(g - 1, 1)
                    qr_fills(fill(g, T_QR), g - 1)

            PER = 1 + (DC - 1) + 2 * TG + 6 + 6 * TG
            group(0, 1)
            group(1, 0)
            with dve.Fori(1, NGL // 2) as i:
                step.enter((i - 1) * (2 * PER), 2 * PER)
                group(2 * i, 1)
                group(2 * i + 1, 0)
            step.leave(NGL // 2 - 1)
            group(NGL, 0)
            kv_fills(CTX_FILL, NGL)

        @block.tensor
        def _(pe):
            pe.sem_inc(mr_full, 1)
            pe.wait_ge(cond_ready, 1)
            for i in range(4):
                wait_slot(pe, f"mod{i}")
                for k in range(DC):
                    ins = pe.matmul(two_ps[i][0:2, :], cond[:, k, :], slots[nth[f"mod{i}"][0]][:, k, :],
                                    start=(k == 0), stop=(k == DC - 1))
                ins.then_inc(mod_read, 1)
            pe.wait_ge(ident_in, 16)
            pe.wait_ge(two_ready, 4)
            for i in range(4):
                for cc in range(4):
                    col = 4 * i + cc
                    ins = pe.transpose(mr_ps[:, 2 * col:2 * col + 2], mod_two[0:2, i, cc * P:(cc + 1) * P], ident[0:2, 0:2])
            ins.then_inc(cols_full, 1)

            def transpose_x(n0, half, first=False):
                for i in (2 * half, 2 * half + 1):
                    if not (first and i < 2):
                        pe.wait_ge(t_free, n0 + i - 1)
                    for u in range(2):
                        k = 2 * i + u
                        for j in range(TG):
                            ins = pe.transpose(tb[i % 2][:, u * G + j * P:u * G + (j + 1) * P], x_t[:, j, k * P:(k + 1) * P], ident[:, :])
                    ins.then_inc(t_full, 1)

            def q_down(g, j, par):
                tok = slice(j * P, (j + 1) * P)
                if not isinstance(g, int) or g > 0:
                    pe.wait_ge(cqn_ready, TG * g + j - TG + 1)
                for k in range(DC):
                    ins = three_pass(pe, cq_ps[j][:, :], [t[:, par, k, tok] for t in hT], [t[:, k, :] for t in w_dq],
                                     k == 0, k == DC - 1)
                ins.then_inc(cq_full, 1)

            def kv_down(g, j, par):
                tok = slice(j * P, (j + 1) * P)
                if not isinstance(g, int) or g > 0:
                    pe.wait_ge(ckn_ready, TG * g + j - TG + 1)
                for k in range(DC):
                    ins = three_pass(pe, ck_ps[j][:, 0:KV_RANK + ROPE], [t[:, par, k, tok] for t in hT],
                                     [t[:, k, :] for t in w_dkv], k == 0, k == DC - 1)
                ins.then_inc(ck_full, 1)

            def transpose_q(g, n0):
                pe.wait_ge(cqn_ready, TG * g + TG)
                for i in range(2):
                    pe.wait_ge(t_free, n0 + i - 1)
                    for u in range(2):
                        for j in range(TG):
                            ins = pe.transpose(tb[i][:, u * G + j * P:u * G + (j + 1) * P],
                                               cqn[:, j, (2 * i + u) * P:(2 * i + u + 1) * P], ident[:, :])
                    ins.then_inc(t_full, 1)

            def transpose_kv(g, n0):
                pe.wait_ge(ckn_ready, TG * g + TG)
                pe.wait_ge(t_free, n0 - 1)
                for u in range(KC):
                    for j in range(TG):
                        ins = pe.transpose(tb[0][:, u * G + j * P:u * G + (j + 1) * P], ckn[:, j, u * P:(u + 1) * P], ident[:, :])
                ins.then_inc(t_full, 1)
                pe.wait_ge(k_rot_ready, g + 1)
                pe.wait_ge(t_free, n0)
                for j in range(TG):
                    ins = pe.transpose(tb[1][:, j * P:(j + 1) * P], k_rot[:, j, :], ident[:, :])
                ins.then_inc(t_full, 1)

            def q_up(g, j):
                if not (isinstance(g, int) and g == 0 and j == 0):
                    pe.wait_ge(q_raw_ready, TG * g + j)
                for k in range(RC):
                    ins = three_pass(pe, qr_ps[:, :], [t[:, k, ds(g * G + j * P, P)] for t in cqT], [t[:, k, :] for t in w_qr],
                                     k == 0, k == RC - 1)
                ins.then_inc(qr_full, 1)

            def transpose_qr(g, n0):
                for j in range(TG):
                    pe.wait_ge(q_rot_ready, TG * g + j + 2)
                    for u in range(2):
                        pe.wait_ge(t_free, n0 + 2 * j + u - 1)
                        for v in range(4):
                            ins = pe.transpose(tb[u][:, v * P:(v + 1) * P], q_rot[:, j, 4 * u + v, :], ident[:, :])
                        ins.then_inc(t_full, 1)

            def group(g, par):
                old = not (isinstance(g, int) and g == 0)
                latent = not (isinstance(g, int) and g == NGL)
                pe.wait_ge(t_free, 4 if not old else fill(g - 1, T_X) + 4)
                if latent:
                    q_down(g, 0, par)
                if old:
                    transpose_q(g - 1, fill(g, T_CQ))
                kv_down(g, 0, par)
                if old:
                    transpose_kv(g - 1, fill(g, T_CKV))
                if latent:
                    q_down(g, 1, par)
                    pe.wait_ge(xn_ready, TG * g + 2 * TG)
                    transpose_x(fill(g, T_X), 0)
                kv_down(g, 1, par)
                if latent:
                    pe.wait_ge(acc_ready, g + 1)
                    if old:
                        pe.wait_ge(mod_row_ready, g)
                    pe.matmul(mr_ps[0:1, :], ones[:, :], mod_acc[:, :], start=True, stop=True).then_inc(mr_full, 1)
                if old:
                    if isinstance(g, int) and g == 1:
                        pe.wait_ge(w_ready, 3)
                    pe.wait_ge(t_free, fill(g, T_CQ) + 2)
                    q_up(g - 1, 0)
                if latent:
                    transpose_x(fill(g, T_X), 1)
                if old:
                    q_up(g - 1, 1)
                    transpose_qr(g - 1, fill(g, T_QR))

            pe.wait_ge(xn_ready, TG)
            for half in range(2):
                transpose_x(0, half, first=True)
            pe.wait_ge(w_ready, 2)
            group(0, 0)
            group(1, 1)
            with pe.Fori(1, NGL // 2) as i:
                group(2 * i, 0)
                group(2 * i + 1, 1)
            group(NGL, 0)
            transpose_kv(NGL, CTX_FILL)


SB = [(c * BANK, min(BANK, KEYS - c * BANK)) for c in range(-(-KEYS // BANK))]
NS = len(SB)
QB = SEQ // BANK
KPB = BANK // P


def attend(nc, io, keep):
    ctx = ExitStack()
    with ctx:
        sb = lambda name, shape, dt=F32: ctx.enter_context(nc.sbuf_tensor(f"attend_{name}", shape, dt))
        sem = lambda name: ctx.enter_context(nc.semaphore(f"attend_{name}"))
        cqT, ckvT, krT, qrT, ident = keep["cqT"], keep["ckvT"], keep["krT"], keep["qrT"], keep["ident"]

        NW = RC + 2 * KC
        w_raw = sb("w_raw", [P, NW, P])
        w_o_raw = sb("w_o_raw", [P, D])
        w_o = keep["w_o"]
        w_h = [sb(f"w_h{s}", [P, NW, P], F16) for s in ("hi", "lo")]
        qT = [sb(f"qT{s}", [P, SEQ], F16) for s in ("hi", "lo")]
        kT = [sb(f"kT{s}", [P, KEYS], F16) for s in ("hi", "lo")]
        v = sb("v", [P, KT, 2, VD], F16)
        prob = sb("prob", [P, KEYS])
        pT = [sb(f"pT{s}", [P, KT, P], F16) for s in ("hi", "lo")]
        o_lo = sb("o_lo", [P, VD])
        o_out = sb("o_out", [P, VD])
        mx = sb("mx", [P, NS])
        neg_max = sb("neg_max", [P, 2])
        rsum = sb("rsum", [P, NS])
        inv = sb("inv", [P, 2])

        s_ps = ctx.enter_context(nc.psum_tensor("attend_s_ps", [P, NS, BANK], F32))
        tb = [ctx.enter_context(nc.psum_tensor(f"attend_tp{i}", [P, BANK], F32)) for i in range(2)]
        o_ps = ctx.enter_context(nc.psum_tensor("attend_o_ps", [P, BANK], F32))

        w_in = sem("w_in")
        w_hi = sem("w_hi")
        w_ready = sem("w_ready")
        b_full = sem("b_full")
        b_copied = sem("b_copied")
        b_free = sem("b_free")
        s_full = sem("s_full")
        s_free = sem("s_free")
        max_step = sem("max_step")
        max_ready = sem("max_ready")
        inv_ready = sem("inv_ready")
        o_full = sem("o_full")
        o_lo_ready = sem("o_lo_ready")
        o_ready = sem("o_ready")
        o_stored = sem("o_stored")
        sp_passed = sem("sp_passed2")

        QKF = QB + NS
        PER = QKF + NS + NS + (NT - 1) * NS

        def qk_fill(h):
            return 0 if isinstance(h, int) and h == 0 else PER * h - NS

        def step_fill(h, t):
            return PER * h - NS + QKF + t * NS + (0 if isinstance(t, int) and t == 0 else NS)

        def v_fill(h):
            return PER * h - NS + QKF + NS

        def w_o_chunk(part, h):
            return w_o[part][:, ds(h, 1), :].rearrange("p a n -> p (a n)") if not isinstance(h, int) else w_o[part][:, h, :]

        END_FILL = PER * HEADS - NS
        LAST = HEADS - 1

        block = ctx.enter_context(nc.Block())

        @block.sync
        def _(sp):
            sp.sem_inc(o_stored, 1)
            def load(h):
                for dst, src, k in ((w_raw[:, 0:RC, :], io["w_uq"], RC), (w_raw[:, RC:RC + KC, :], io["w_uk"], KC),
                                    (w_raw[:, RC + KC:NW, :], io["w_uv"], KC)):
                    src = src[ds(h, 1)] if not isinstance(h, int) else src[h:h + 1]
                    sp.dma_start(dst, src.rearrange("a (k p) n -> p (a k) n", p=P)).then_inc(w_in, 16)
                rows = ds(h * P, P) if not isinstance(h, int) else slice(h * P, h * P + P)
                sp.dma_start(w_o_raw[:, :], io["w_o"][rows, :]).then_inc(w_in, 16)

            load(0)
            sp.wait_ge(w_ready, 2)
            load(1)

            def stores(h):
                with sp.Fori(0, NT) as t:
                    wait_alone(sp, o_ready, h * NT + t + 2, sp_passed)
                    sp.dma_start(io["attn"][ds(t * P, P), ds(h * VD, VD)], o_out[:, :]).then_inc(o_stored, 16)

            with sp.Fori(0, HEADS - 2) as h:
                wait_alone(sp, w_ready, 2 * h + 4, sp_passed)
                load(h + 2)
                stores(h)
            with sp.Fori(HEADS - 2, HEADS) as h:
                stores(h)
            sp.wait_ge(o_stored, 16 * HEADS * NT + 1)

        @block.scalar
        def _(act):
            act.preload_act_table(ACT.Exp)

            def copy_fill(n, bank_, dst, width, scale):
                act.wait_ge(b_full, n + 1)
                src = bank_[:, 0:width]
                if len(dst.shape) == 3:
                    src = src.rearrange("p (k t) -> p k t", t=P)
                act.activation(dst, src, ACT.Copy, scale=scale).then_inc(b_copied, 1)

            def split_weights(h):
                act.wait_ge(w_in, 64 * h + 64)
                act.activation(w_h[0][:, :, :], w_raw[:, :, :], ACT.Copy, scale=WS).then_inc(w_hi, 1)
                act.activation(w_o_chunk(0, h), w_o_raw[:, :], ACT.Copy, scale=WS).then_inc(w_hi, 1)

            def queries_keys(n, par):
                for c in range(QB):
                    copy_fill(n + c, tb[(par + c) % 2], qT[0][:, c * BANK:(c + 1) * BANK], BANK, 1 / WS)
                for c, (k0, w) in enumerate(SB):
                    copy_fill(n + QB + c, tb[(par + QB + c) % 2], kT[0][:, k0:k0 + w], w, 1 / WS)

            def values(n, par):
                for c, (k0, w) in enumerate(SB):
                    copy_fill(n + c, tb[(par + c) % 2], v[:, c * KPB:c * KPB + w // P, 0, :], w, 1 / WS)

            def exps(step):
                act.wait_ge(max_ready, step + 1)
                for c, (k0, w) in enumerate(SB):
                    act.activation(prob[:, k0:k0 + w], s_ps[:, c, 0:w], ACT.Exp, bias=neg_max[:, 1:2], scale=SOFTMAX_SCALE,
                                   accum_out=rsum[:, c:c + 1]).then_inc(s_free, 1)

            def transposed(n, low=None):
                for c, (k0, w) in enumerate(SB):
                    copy_fill(n + c, tb[c % 2], pT[0][:, c * KPB:c * KPB + w // P, :], w, 1.0)
                    if c == 0 and low is not None:
                        low_output(low)

            def low_output(step):
                act.wait_ge(o_full, step + 1)
                act.wait_ge(inv_ready, step + 1)
                act.activation(o_lo[:, :], o_ps[:, VD:2 * VD], ACT.Copy, scale=inv[:, 1:2]).then_inc(o_lo_ready, 1)

            def head(h, first=False, last=False):
                queries_keys(qk_fill(h), 0)
                if not first:
                    transposed(step_fill(h, 0), h * NT - 2)
                exps(h * NT)
                values(v_fill(h), 0)
                if not last:
                    split_weights(h + 1)
                t0 = 1
                if first:
                    transposed(step_fill(h, 1))
                    exps(1)
                    t0 = 2
                with act.Fori(t0, NT) as t:
                    transposed(step_fill(h, t), h * NT + t - 2)
                    exps(h * NT + t)

            act.sem_inc(s_free, NS)
            split_weights(0)
            head(0, first=True)
            with act.Fori(1, LAST) as h:
                head(h)
            head(LAST, last=True)
            transposed(END_FILL, HEADS * NT - 2)
            low_output(HEADS * NT - 1)

        @block.vector
        def _(dve):
            dve.sem_inc(o_ready, 1)
            step = Steps(dve, max_step)

            def split_fill(n, bank_, hi, lo, width, scale):
                dve.wait_ge(b_copied, n + 1)
                src = bank_[:, 0:width]
                if len(hi.shape) == 3:
                    src = src.rearrange("p (k t) -> p k t", t=P)
                if scale == 1.0:
                    ins = dve.tensor_tensor(lo, src, hi, ALU.subtract)
                else:
                    ins = dve.scalar_tensor_tensor(out=lo, in0=src, scalar=scale, in1=hi, op0=ALU.mult, op1=ALU.subtract)
                ins.then_inc(b_free, 1)

            def split_weights(h):
                dve.wait_ge(w_hi, 2 * h + 2)
                for lo, raw, hi in ((w_h[1][:, :, :], w_raw[:, :, :], w_h[0][:, :, :]),
                                    (w_o_chunk(1, h), w_o_raw[:, :], w_o_chunk(0, h))):
                    dve.scalar_tensor_tensor(out=lo, in0=raw, scalar=WS, in1=hi, op0=ALU.mult, op1=ALU.subtract).then_inc(w_ready, 1)

            def queries_keys(n, par):
                for c in range(QB):
                    s = slice(c * BANK, (c + 1) * BANK)
                    split_fill(n + c, tb[(par + c) % 2], qT[0][:, s], qT[1][:, s], BANK, 1 / WS)
                for c, (k0, w) in enumerate(SB):
                    s = slice(k0, k0 + w)
                    split_fill(n + QB + c, tb[(par + QB + c) % 2], kT[0][:, s], kT[1][:, s], w, 1 / WS)

            def values(n, par):
                for c, (k0, w) in enumerate(SB):
                    s = slice(c * KPB, c * KPB + w // P)
                    split_fill(n + c, tb[(par + c) % 2], v[:, s, 0, :], v[:, s, 1, :], w, 1 / WS)

            def chunk_max(st, c):
                dve.wait_ge(s_full, st * NS + c + 1)
                step.did(dve.tensor_reduce(mx[:, c:c + 1], s_ps[:, c, 0:SB[c][1]], AX.X, ALU.max))

            def row_max():
                step.settle()
                step.did(dve.tensor_reduce(neg_max[:, 0:1], mx[:, :], AX.X, ALU.max))
                step.settle()
                dve.tensor_scalar(neg_max[:, 1:2], neg_max[:, 0:1], -SOFTMAX_SCALE, LOG_P_SCALE, ALU.mult, ALU.add).then_inc(max_ready, 1)

            def inverse(st):
                dve.wait_ge(s_free, (st + 2) * NS)
                step.did(dve.tensor_reduce(inv[:, 0:1], rsum[:, :], AX.X, ALU.add))
                step.settle()
                dve.reciprocal(inv[:, 1:2], inv[:, 0:1]).then_inc(inv_ready, 1)

            def output(st):
                dve.wait_ge(o_lo_ready, st + 1)
                dve.wait_ge(o_stored, st * 16 + 1)
                dve.scalar_tensor_tensor(out=o_out[:, :], in0=o_ps[:, 0:VD], scalar=inv[:, 1:2], in1=o_lo[:, :],
                                         op0=ALU.mult, op1=ALU.add).then_inc(o_ready, 1)

            def low_fill(n, c):
                k0, w = SB[c]
                s = slice(c * KPB, c * KPB + w // P)
                split_fill(n + c, tb[c % 2], pT[0][:, s, :], pT[1][:, s, :], w, 1.0)

            def step_of(h, t, st, output_due=True):
                for c in range(NS):
                    chunk_max(st, c)
                    if c == NS - 1:
                        row_max()
                    low_fill(step_fill(h, t), c)
                    if c == 0:
                        if output_due:
                            output(st - 2)
                        inverse(st - 1)

            STEP = NS + 2

            def head(h, first=False, last=False):
                queries_keys(qk_fill(h), 0)
                if first:
                    for c in range(NS):
                        chunk_max(0, c)
                    row_max()
                else:
                    step_of(h, 0, h * NT)
                values(v_fill(h), 0)
                if not last:
                    split_weights(h + 1)
                t0 = 1
                if first:
                    step_of(h, 1, 1, output_due=False)
                    t0 = 2
                with dve.Fori(t0, NT) as t:
                    step.enter((t - t0) * STEP, STEP)
                    step_of(h, t, h * NT + t)
                step.leave(NT - t0)

            split_weights(0)
            head(0, first=True)
            with dve.Fori(1, LAST) as h:
                step.enter((h - 1) * (STEP * NT), STEP * NT)
                outer = step.outer
                head(h)
            step.base, step.n = outer + (LAST - 1) * STEP * NT, 0
            head(LAST, last=True)
            for c in range(NS):
                low_fill(END_FILL, c)
                if c == 0:
                    output(HEADS * NT - 2)
                    inverse(HEADS * NT - 1)
            output(HEADS * NT - 1)

        @block.tensor
        def _(pe):
            def wait_bank(n, lag=1):
                if isinstance(n, int):
                    if n - lag > 0:
                        pe.wait_ge(b_free, n - lag)
                else:
                    pe.wait_ge(b_free, n - lag)

            def queries_keys(h, n, par):
                pe.wait_ge(w_ready, 2 * h + 2)
                for c in range(QB):
                    wait_bank(n + c, 0 if c == 0 else 1)
                    for k in range(RC):
                        ins = three_pass(pe, tb[(par + c) % 2][:, :], [t[:, k, :] for t in w_h],
                                         [t[:, k, c * BANK:(c + 1) * BANK] for t in cqT], k == 0, k == RC - 1)
                    ins.then_inc(b_full, 1)
                for c, (k0, w) in enumerate(SB):
                    wait_bank(n + QB + c)
                    for k in range(KC):
                        ins = three_pass(pe, tb[(par + QB + c) % 2][:, 0:w], [t[:, RC + k, :] for t in w_h],
                                         [t[:, k, k0:k0 + w] for t in ckvT], k == 0, k == KC - 1)
                    ins.then_inc(b_full, 1)

            def values(n, par):
                for c, (k0, w) in enumerate(SB):
                    wait_bank(n + c, 0 if c == 0 else 1)
                    for i in range(w // P):
                        keys = slice(k0 + i * P, k0 + (i + 1) * P)
                        for k in range(KC):
                            ins = three_pass(pe, tb[(par + c) % 2][:, i * P:(i + 1) * P], [t[:, k, keys] for t in ckvT],
                                             [t[:, RC + KC + k, :] for t in w_h], k == 0, k == KC - 1)
                    ins.then_inc(b_full, 1)

            def scores(h, t, st, c):
                k0, w = SB[c]
                q = ds(t * P, P) if not isinstance(t, int) else slice(t * P, (t + 1) * P)
                pe.wait_ge(s_free, st * NS + c + 1)
                out, keys = s_ps[:, c, 0:w], slice(k0, k0 + w)
                pe.matmul(out, qT[0][:, q], kT[0][:, keys], start=True, stop=False)
                pe.matmul(out, qT[0][:, q], kT[1][:, keys], start=False, stop=False)
                pe.matmul(out, qT[1][:, q], kT[0][:, keys], start=False, stop=False)
                r = qrT[:, ds(h, 1), q].rearrange("p a t -> p (a t)") if not isinstance(h, int) else qrT[:, h, q]
                pe.matmul(out, r, krT[0][:, keys], start=False, stop=False)
                pe.matmul(out, r, krT[1][:, keys], start=False, stop=True).then_inc(s_full, 1)

            def transpose_probs(n, c):
                k0, w = SB[c]
                wait_bank(n + c, 0 if c == 0 else 1)
                for i in range(w // P):
                    ins = pe.transpose(tb[c % 2][:, i * P:(i + 1) * P], prob[:, k0 + i * P:k0 + (i + 1) * P], ident[:, :])
                ins.then_inc(b_full, 1)

            def output(n, st):
                pe.wait_ge(o_ready, st + 1)
                for c, (k0, w) in enumerate(SB):
                    pe.wait_ge(b_free, n + c + 1)
                    for i in range(c * KPB, c * KPB + w // P):
                        pe.matmul(o_ps[:, 0:2 * VD], pT[0][:, i, :], v[:, i, :, :].rearrange("p s d -> p (s d)"),
                                  start=(i == 0), stop=False)
                        ins = pe.matmul(o_ps[:, 0:VD], pT[1][:, i, :], v[:, i, 0, :], start=False, stop=(i == KT - 1))
                ins.then_inc(o_full, 1)

            def step_of(h, t, st):
                for c in range(NS):
                    scores(h, t, st, c)
                    transpose_probs(step_fill(h, t), c)
                output(step_fill(h, t), st - 1)

            def head(h, first=False):
                queries_keys(h, qk_fill(h), 0)
                pe.wait_ge(b_free, qk_fill(h) + QKF)
                if first:
                    for c in range(NS):
                        scores(h, 0, 0, c)
                else:
                    step_of(h, 0, h * NT)
                values(v_fill(h), 0)
                with pe.Fori(1, NT) as t:
                    step_of(h, t, h * NT + t)

            head(0, first=True)
            with pe.Fori(1, HEADS) as h:
                head(h)
            pe.wait_ge(s_free, (HEADS * NT + 1) * NS)
            for c in range(NS):
                transpose_probs(END_FILL, c)
            output(END_FILL, HEADS * NT - 1)


SLOTS = SEQ
PBLK = SLOTS // BLK
LAST_BLOCK = SEQ * TOPK // BLK + EXPERTS - 2
NBMAX = LAST_BLOCK + 5
BIG = 1e30
HT = NT // 2
KNEG, IOTA, EOFF, THR, NCONST = 0, NBMAX, 2 * NBMAX, 2 * NBMAX + EXPERTS, 2 * NBMAX + EXPERTS + PBLK
SLOT_OF, BLOCKS_OF, FIRST_OF, NTABLE = 0, NBMAX, NBMAX + EXPERTS, NBMAX + 2 * EXPERTS


def route(nc, io, keep):
    ctx = ExitStack()
    with ctx:
        sb = lambda name, shape, dt=F32: ctx.enter_context(nc.sbuf_tensor(f"route_{name}", shape, dt))
        sem = lambda name: ctx.enter_context(nc.semaphore(f"route_{name}"))
        ident, g2b = keep["ident"], keep["g2b"]

        w_o = keep["w_o"]
        w_r = sb("w_r", [P, DC, 4 + EXPERTS])
        b_r = sb("b_r", [P, 4 + EXPERTS])
        at = sb("at", [P, 2, D])
        xt = sb("xt", [P, 2, D])
        aT = [sb(f"aT{s}", [P, 2, DC, P], F16) for s in ("hi", "lo")]
        yg = sb("yg", [P, D])
        x1 = sb("x1_t", [P, 2, D])
        h2 = sb("h2_t", [P, 2, D])
        h2T = sb("h2T", [P, 2, DC, P])
        sq = sb("sq", [P, D], BF16)
        g1b = sb("g1b", [P, D])
        A2b = sb("A2b", [P, D])
        B2b = sb("B2b", [P, D])
        rowb = [t[:, i, :] for t in (x1, h2) for i in range(2)]
        n2b = sb("n2b", [P, D])
        ss = sb("ss", [P, 2])
        rms = sb("rms", [P, 2])
        small = sb("small", [P, 8])
        eps_t = sb("eps_t", [P, 1])
        cst = sb("cst", [P, NCONST])
        tri = sb("tri", [P, P], F16)
        tri_f = sb("tri_f", [P, P])
        ones = sb("ones", [P, P], F16)
        tok = sb("tok", [P, TOPK, NT, 2], I32)
        lg = sb("lg", [P, NT, 4 + EXPERTS])

        w = {n: sb("r_" + n, shape, dt) for n, shape, dt in (
            ("dest_i", [P, TOPK * NT], I32), ("dest", [P, TOPK * NT], F32), ("ex", [P, NT, 5], F32),
            ("M", [P, NT, EXPERTS], F16), ("M1", [P, NT, EXPERTS], F16), ("M2", [P, NT, EXPERTS], F16),
            ("per_row", [P, 7 * NT], F32), ("eq", [P, NT, PER_GROUP], F32), ("ohg", [P, NT, GROUPS_E], F32),
            ("sel", [P, NT, PER_GROUP], F32), ("oh1", [P, NT, PER_GROUP], F32), ("oh2", [P, NT, PER_GROUP], F32),
            ("big", [P, NT * EXPERTS], F32), ("big2", [P, NBMAX * EXPERTS], F32), ("rank", [P, NT, EXPERTS], F32),
            ("per_e", [P, 3, EXPERTS], F32), ("tab_f", [P, 2, NBMAX], F32))}

        tb = [ctx.enter_context(nc.psum_tensor(f"route_rt{i}", [P, BANK], F32)) for i in range(2)]
        y_ps = [ctx.enter_context(nc.psum_tensor(f"route_y_ps{i}", [P, D], F32)) for i in range(2)]
        lg_ps = [ctx.enter_context(nc.psum_tensor(f"route_lg_ps{i}", [P, BANK], F32)) for i in range(2)]

        small_in = sem("small_in")
        at_in = [sem(f"at_in{i}") for i in range(2)]
        xt_in = [sem(f"xt_in{i}") for i in range(2)]
        rows_ready = sem("rows_ready")
        t_full = sem("t_full")
        t_hi = sem("t_hi")
        t_free = [sem(f"t_free{i}") for i in range(2)]
        y_full = sem("y_full")
        x1_ready = sem("x1_ready")
        rms_ready = sem("rms_ready")
        sq_done = sem("sq_done")
        h2_ready = sem("h2_ready")
        lg_full = sem("lg_full")
        lg_ready = sem("lg_ready")
        x1_out = [sem(f"x1_out{i}") for i in range(2)]
        h2_out = [sem(f"h2_out{i}") for i in range(2)]
        dve_step = sem("dve_step")
        sp_passed = sem("sp_passed")
        slots_empty = sem("slots_empty")
        exp_in = sem("exp_in")
        exp_out = sem("exp_out")
        m_ready = sem("m_ready")
        rank_full = sem("rank_full")
        dest_ready = sem("dest_ready")
        slots_out = sem("slots_out")

        def at_fill(n):
            return 2 * n if isinstance(n, int) and n < 2 else 4 * n - 4

        def h2_fill(n):
            if isinstance(n, int) and n >= NT - 2:
                return 4 * NT - 4 + 2 * (n - NT + 2)
            return 4 * n + 6

        mod_b = io["mod_b"].rearrange("(a n) -> a n", a=1)
        block = ctx.enter_context(nc.Block())

        @block.sync
        def _(sp):
            sp.dma_start(at[:, 0, :], io["attn"][0:P, :]).then_inc(at_in[0], 16)
            sp.dma_start(at[:, 1, :], io["attn"][P:2 * P, :]).then_inc(at_in[1], 16)
            for i, dst in enumerate((g1b, B2b, A2b, g2b)):
                sp.dma_start(dst[:, :], io["mod_rows"][:, i * D:(i + 1) * D].broadcast_to([P, D])).then_inc(small_in, 16)
                sp.dma_start(rowb[i], mod_b[:, (i + 2) * D:(i + 3) * D].broadcast_to([P, D])).then_inc(small_in, 16)
            sp.dma_start(n2b[:, :], io["norm2_g"].rearrange("(a n) -> a n", a=1).broadcast_to([P, D])).then_inc(small_in, 16)
            for n in range(2):
                sp.dma_start(xt[:, n, :], io["xc"][n * P:(n + 1) * P, :]).then_inc(xt_in[n], 16)
            sp.dma_start(b_r[:, :], io["b_r"].rearrange("(a n) -> a n", a=1).broadcast_to([P, 4 + EXPERTS])).then_inc(small_in, 16)
            sp.dma_start(w_r[:, :, :], io["w_r"].rearrange("(k p) n -> p k n", p=P)).then_inc(small_in, 16)
            sp.dma_start(cst[:, :], io["row_consts"].broadcast_to([P, NCONST])).then_inc(small_in, 16)
            sp.dma_start(tri_f[:, :], io["tri"]).then_inc(small_in, 16)
            sp.dma_start(tok[:, :, :, :], io["tok"]).then_inc(small_in, 16)
            sp.dma_start(io["slots"].rearrange("(p n) o -> p (n o)", p=P), io["empty_slots"]).then_inc(slots_empty, 16)

            def rows(n):
                return ds(n * P, P) if not isinstance(n, int) else slice(n * P, (n + 1) * P)

            def load_attn(n, par):
                wait_alone(sp, t_full, at_fill(n - 2) + 2, sp_passed)
                sp.dma_start(at[:, par, :], io["attn"][rows(n), :]).then_inc(at_in[par], 16)

            def store_x1(n, par):
                wait_alone(sp, x1_ready, n + 1, sp_passed)
                sp.dma_start(io["x1"][rows(n), :], x1[:, par, :]).then_inc(x1_out[par], 16)

            def load_x(n, par):
                sp.dma_start(xt[:, par, :], io["xc"][rows(n), :]).then_inc(xt_in[par], 16)

            def store_h2(n, par):
                wait_alone(sp, h2_ready, n + 1, sp_passed)
                sp.dma_start(io["h2"][rows(n), :], h2[:, par, :]).then_inc(h2_out[par], 16)

            def step(t, par, attn=True, x=True):
                if attn:
                    load_attn(t + 2, par)
                store_x1(t - 1, 1 - par)
                if x:
                    load_x(t + 1, 1 - par)
                store_h2(t - 1, 1 - par)

            load_attn(2, 0)
            step(1, 1)
            with sp.Fori(0, (NT - 4) // 2) as i:
                step(2 * i + 2, 0)
                step(2 * i + 3, 1)
            step(NT - 2, 0, attn=False)
            step(NT - 1, 1, attn=False, x=False)
            step(NT, 0, attn=False, x=False)
            sp.wait_ge(y_full, NT)
            for n, e in (("gate", 0), ("up", 0), ("down", 0), ("gate", 1)):
                for part in range(2):
                    load_weights(sp, io, keep, n, e, e, part)
            for i in range(2):
                sp.wait_ge(x1_out[i], 8 * NT)
                sp.wait_ge(h2_out[i], 8 * NT)

        @block.gpsimd
        def _(pool):
            pool.wait_ge(slots_empty, 16)
            pool.wait_ge(small_in, 16 * 14)
            for half, k in ((h, k) for h in range(2) for k in range(TOPK)):
                tiles = range(half * HT, (half + 1) * HT)
                pool.wait_ge(dest_ready, TOPK * half + k + 1)
                for t in tiles:
                    pool.indirect_dma_start(io["slots"], bass.IndirectOffsetOnAxis(ap=w["dest_i"][:, k * NT + t:k * NT + t + 1], axis=0),
                                            tok[:, k, t, :], None).then_inc(slots_out, 16)
            pool.wait_ge(slots_out, 16 * TOPK * NT)

        @block.scalar
        def _(act):
            act.preload_act_table(ACT.Sqrt)
            def attn_hi(n, par):
                for i in range(2):
                    act.wait_ge(t_full, at_fill(n) + i + 1)
                    act.activation(aT[0][:, par, 4 * i:4 * i + 4, :], tb[i][:, :].rearrange("p (k t) -> p k t", k=4),
                                   ACT.Copy).then_inc(t_hi, 1)

            def norm(n, par):
                act.wait_ge(x1_ready, n + 1)
                act.activation(sq[:, :], x1[:, par, :], ACT.Square, accum_out=ss[:, par:par + 1]).then_inc(sq_done, 1)
                act.wait_ge(sq_done, n + 1)
                act.activation(rms[:, par:par + 1], ss[:, par:par + 1], ACT.Sqrt, bias=eps_t[:, :], scale=1.0 / D).then_inc(rms_ready, 1)

            def h2_copies(n, par):
                for i in range(2):
                    act.wait_ge(t_full, h2_fill(n) + i + 1)
                    act.activation(h2T[:, par, 4 * i:4 * i + 4, :], tb[i][:, :].rearrange("p (k t) -> p k t", k=4),
                                   ACT.Copy).then_inc(t_free[i], 1)

            def step(t, par):
                attn_hi(t + 1, 1 - par)
                norm(t - 1, 1 - par)
                h2_copies(t - 1, 1 - par)

            attn_hi(0, 0)
            attn_hi(1, 1)
            act.wait_ge(rows_ready, 1)
            with act.Fori(0, (NT - 2) // 2) as i:
                step(2 * i + 1, 1)
                step(2 * i + 2, 0)
            for n in (NT - 2, NT - 1):
                norm(n, n % 2)
                h2_copies(n, n % 2)
            act.preload_act_table(ACT.Exp)
            act.wait_ge(exp_in, 1)
            act.activation(w["ex"][:, :, :], w["ex"][:, :, :], ACT.Exp).then_inc(exp_out, 1)
            for part in range(2):
                weights_hi(act, keep, "gate", 0, 0, part)

        @block.vector
        def _(dve):
            step = Steps(dve, dve_step)
            dve.memset(eps_t[:, :], EPS)
            step.did(dve.memset(ones[:, :], 1.0))
            def attn_lo(n, par):
                for i in range(2):
                    dve.wait_ge(t_hi, 2 * n + i + 1)
                    dve.tensor_tensor(aT[1][:, par, 4 * i:4 * i + 4, :], tb[i][:, :].rearrange("p (k t) -> p k t", k=4),
                                      aT[0][:, par, 4 * i:4 * i + 4, :], ALU.subtract).then_inc(t_free[i], 1)

            attn_lo(0, 0)
            attn_lo(1, 1)
            dve.wait_ge(small_in, 16 * 14)
            for i, dst in enumerate((g1b, B2b, A2b, g2b)):
                step.did(dve.tensor_tensor(dst[:, :], dst[:, :], rowb[i], ALU.add))
            step.did(dve.tensor_copy(tri[:, :], tri_f[:, :]))
            step.settle()
            step.did(dve.tensor_scalar(g1b[:, :], g1b[:, :], 1 / WS, None, ALU.mult))
            dve.scalar_tensor_tensor(out=A2b[:, :], in0=A2b[:, :], scalar=1.0, in1=n2b[:, :], op0=ALU.add, op1=ALU.mult).then_inc(rows_ready, 1)
            step.settle()
            dve.wait_ge(rows_ready, 1)

            def residual(n, par):
                dve.wait_ge(y_full, n + 1)
                step.did(dve.tensor_tensor(yg[:, :], y_ps[par][:, :], g1b[:, :], ALU.mult))
                dve.wait_ge(xt_in[par], 8 * (n - par) + 16)
                if not (isinstance(n, int) and n < 2):
                    dve.wait_ge(x1_out[par], 8 * (n - par))
                step.settle()
                dve.tensor_tensor(x1[:, par, :], yg[:, :], xt[:, par, :], ALU.add).then_inc(x1_ready, 1)

            def norm(n, par):
                r, m, u, v = (small[:, 4 * par + i:4 * par + i + 1] for i in range(4))
                dve.wait_ge(rms_ready, n + 1)
                step.did(dve.reciprocal(r, rms[:, par:par + 1]))
                step.did(dve.tensor_scalar(m, ss[:, par:par + 1], 1.0 / D, EPS, ALU.mult, ALU.add))
                step.settle()
                step.did(dve.scalar_tensor_tensor(out=u, in0=r, scalar=r, in1=m, op0=ALU.mult, op1=ALU.mult))
                step.settle()
                step.did(dve.tensor_scalar(v, u, -0.5, 1.5, ALU.mult, ALU.add))
                step.settle()
                step.did(dve.tensor_tensor(u, r, v, ALU.mult))
                if not (isinstance(n, int) and n < 2):
                    dve.wait_ge(h2_out[par], 8 * (n - par))
                step.settle()
                step.did(dve.scalar_tensor_tensor(out=h2[:, par, :], in0=x1[:, par, :], scalar=u, in1=A2b[:, :], op0=ALU.mult, op1=ALU.mult))
                step.settle()
                dve.tensor_tensor(h2[:, par, :], h2[:, par, :], B2b[:, :], ALU.add).then_inc(h2_ready, 1)

            def logits(n, par):
                dve.wait_ge(lg_full, n + 1)
                dst = lg[:, ds(n, 1), :].rearrange("p a n -> p (a n)") if not isinstance(n, int) else lg[:, n, :]
                dve.tensor_tensor(dst, lg_ps[par][:, 0:4 + EXPERTS], b_r[:, :], ALU.add).then_inc(lg_ready, 1)

            def body(t, par):
                residual(t - 1, 1 - par)
                attn_lo(t + 1, 1 - par)
                norm(t - 1, 1 - par)
                logits(t - 1, 1 - par)

            PER = 7
            def bodies(first, last):
                with dve.Fori(first, last) as i:
                    step.enter((i - first) * (2 * PER), 2 * PER)
                    body(2 * i + 1, 1)
                    body(2 * i + 2, 0)
                step.leave(last - first)

            body(1, 1)
            body(2, 0)
            bodies(1, HT // 2)
            dve.wait_ge(lg_ready, HT)
            choices(dve, step, lg, cst, w, 0, m_ready)
            body(HT + 1, 1)
            destinations(dve, step, cst, w, 0, lg_ps[1][:, BANK // 2:BANK], rank_full, dest_ready)
            body(HT + 2, 0)
            bodies(HT // 2 + 1, HT - 1)
            for n in (NT - 2, NT - 1):
                residual(n, n % 2)
                norm(n, n % 2)
                logits(n, n % 2)
            dve.wait_ge(lg_ready, NT)
            choices(dve, step, lg, cst, w, 1, m_ready)
            group_exps(dve, step, lg, w, exp_in)
            destinations(dve, step, cst, w, 1, y_ps[0][:, 0:HT * EXPERTS], rank_full, dest_ready)
            block_table(dve, step, cst, keep, w, y_ps[1][:, 0:EXPERTS])
            token_gates(dve, step, keep, w, exp_out)
            for part in range(2):
                weights_lo(dve, keep, "gate", 0, 0, part)

        @block.tensor
        def _(pe):
            def transposes(src, fill0, count, first=False):
                for i in range(2):
                    if not first:
                        pe.wait_ge(t_free[i], count)
                    for u in range(4):
                        k = 4 * i + u
                        ins = pe.transpose(tb[i][:, u * P:(u + 1) * P], src[:, k * P:(k + 1) * P], ident[:, :])
                    ins.then_inc(t_full, 1)

            def attn_T(n, par, first=False):
                pe.wait_ge(at_in[par], 8 * (n - par) + 16)
                f = at_fill(n)
                transposes(at[:, par, :], f, n if isinstance(n, int) and n < 2 else 2 * n - 2, first)

            def product(n, par):
                pe.wait_ge(t_free[1], n + 1 if isinstance(n, int) and n < 2 else 2 * n - 1)
                pe.wait_ge(t_free[0], n + 1 if isinstance(n, int) and n < 2 else 2 * n - 1)
                if not (isinstance(n, int) and n < 2):
                    pe.wait_ge(x1_ready, n - 1)
                for k in range(DC):
                    for c in range(2):
                        ins = three_pass(pe, y_ps[par][:, c * BANK:(c + 1) * BANK], [t[:, par, k, :] for t in aT],
                                         [t[:, k, c * BANK:(c + 1) * BANK] for t in w_o], k == 0, k == DC - 1)
                ins.then_inc(y_full, 1)

            def router(n, par):
                if isinstance(n, int) and n == 0:
                    pe.wait_ge(small_in, 16 * 14)
                pe.wait_ge(h2_ready, n + 1)
                late = isinstance(n, int) and n >= NT - 2
                cnt = (2 * NT - 2 + (n - NT + 2)) if late else 2 * n + 3
                transposes(h2[:, par, :], h2_fill(n), cnt)
                for i in range(2):
                    pe.wait_ge(t_free[i], cnt + 1)
                if not (isinstance(n, int) and n < 2):
                    pe.wait_ge(lg_ready, n - 1)
                for k in range(DC):
                    ins = pe.matmul(lg_ps[par][:, 0:4 + EXPERTS], h2T[:, par, k, :], w_r[:, k, :], start=(k == 0), stop=(k == DC - 1))
                ins.then_inc(lg_full, 1)

            attn_T(0, 0, first=True)
            attn_T(1, 1)
            product(0, 0)

            def step(t, par):
                attn_T(t + 1, 1 - par)
                product(t, par)
                router(t - 1, 1 - par)

            def ranks(half, out):
                M, t0 = w["M"], half * HT
                view = lambda a: a.rearrange("p (t e) -> p t e", e=EXPERTS)
                pe.wait_ge(m_ready, half + 1)
                ins = pe.matmul(out, tri[:, :], M[:, t0:t0 + HT, :].rearrange("p t e -> p (t e)"), start=True, stop=False)
                for t in range(t0 + HT - 1):
                    n = min(HT, t0 + HT - 1 - t)
                    ins = pe.matmul(view(out[:, (HT - n) * EXPERTS:HT * EXPERTS]), ones[:, :],
                                    M[:, t:t + 1, :].broadcast_to([P, n, EXPERTS]), start=False, stop=(t == t0 + HT - 2))
                return ins

            step(1, 1)
            step(2, 0)
            with pe.Fori(1, HT // 2) as i:
                step(2 * i + 1, 1)
                step(2 * i + 2, 0)
            attn_T(HT + 2, 0)
            product(HT + 1, 1)
            ranks(0, lg_ps[1][:, BANK // 2:BANK]).then_inc(rank_full, 1)
            router(HT, 0)
            step(HT + 2, 0)
            with pe.Fori(HT // 2 + 1, HT - 1) as i:
                step(2 * i + 1, 1)
                step(2 * i + 2, 0)
            product(NT - 1, 1)
            router(NT - 2, 0)
            router(NT - 1, 1)
            ranks(1, y_ps[0][:, 0:HT * EXPERTS])
            for t in range(NT):
                ins = pe.matmul(y_ps[1][:, 0:EXPERTS], ones[:, :], w["M"][:, t, :], start=(t == 0), stop=(t == NT - 1))
            ins.then_inc(rank_full, 1)


def per_tile(w, i, tiles=slice(0, NT)):
    return w["per_row"][:, i * NT + tiles.start:i * NT + tiles.stop]


GROUP_MAX, FIRST_LOGIT, SECOND_LOGIT, GROUP_AT, FIRST_AT, SECOND_AT, TOTAL = range(7)


def spread(a, n):
    return a.unsqueeze(2).broadcast_to([P, a.shape[1], n])


def row_of(cst, o, n, t=HT):
    return cst[:, o:o + n].unsqueeze(1).broadcast_to([P, t, n])


def choices(dve, step, lg, cst, w, half, m_ready):
    PG, E = PER_GROUP, EXPERTS
    tiles = slice(half * HT, (half + 1) * HT)
    gm, e1, e2, gi, i1, i2 = (per_tile(w, i, tiles) for i in range(6))
    G4 = lg[:, tiles, 0:4]
    eq, ohg, sel, oh1, oh2 = (w[n][:, tiles, :] for n in ("eq", "ohg", "sel", "oh1", "oh2"))
    M1, M2, M = (w[n][:, tiles, :] for n in ("M1", "M2", "M"))

    def first_max(src, n, m, idx, onehot):
        step.did(dve.tensor_reduce(m, src, AX.X, ALU.max))
        step.settle()
        step.did(dve.tensor_tensor(eq[:, :, 0:n], src, spread(m, n), ALU.is_equal))
        step.settle()
        step.did(dve.tensor_tensor(eq[:, :, 0:n], eq[:, :, 0:n], row_of(cst, KNEG, n), ALU.mult))
        step.settle()
        step.did(dve.tensor_reduce(idx, eq[:, :, 0:n], AX.X, ALU.min))
        step.settle()
        step.did(dve.tensor_tensor(onehot, spread(idx, n), row_of(cst, KNEG, n), ALU.is_equal))
        step.settle()

    first_max(G4, 4, gm, gi, ohg)
    g4 = w["big"][:, 0:HT * E].rearrange("p (t g i) -> p t g i", g=4, i=PG)
    step.did(dve.tensor_tensor(g4, lg[:, tiles, 4:4 + E].rearrange("p t (g i) -> p t g i", g=4),
                               ohg.unsqueeze(3).broadcast_to([P, HT, 4, PG]), ALU.mult))
    step.settle()
    step.did(dve.tensor_reduce(sel, g4.rearrange("p t g i -> p t i g"), AX.X, ALU.add))
    step.settle()
    first_max(sel, PG, e1, i1, oh1)
    step.did(dve.scalar_tensor_tensor(out=sel, in0=oh1, scalar=-BIG, in1=sel, op0=ALU.mult, op1=ALU.add))
    step.settle()
    first_max(sel, PG, e2, i2, oh2)
    for m, oh in ((M1, oh1), (M2, oh2)):
        step.did(dve.tensor_tensor(m.rearrange("p t (g i) -> p t g i", g=4), ohg.unsqueeze(3).broadcast_to([P, HT, 4, PG]),
                                   oh.unsqueeze(2).broadcast_to([P, HT, 4, PG]), ALU.mult))
    step.settle()
    dve.tensor_tensor(M, M1, M2, ALU.add).then_inc(m_ready, 1)


def group_exps(dve, step, lg, w, exp_in):
    ex = w["ex"]
    step.did(dve.tensor_tensor(ex[:, :, 0:4], lg[:, :, 0:4], spread(per_tile(w, GROUP_MAX), 4), ALU.subtract))
    step.did(dve.tensor_tensor(ex[:, :, 4], per_tile(w, SECOND_LOGIT), per_tile(w, FIRST_LOGIT), ALU.subtract))
    step.settle()
    dve.nop().then_inc(exp_in, 1)


def destinations(dve, step, cst, w, half, ranks, rank_full, dest_ready):
    E = EXPERTS
    tiles = slice(half * HT, (half + 1) * HT)
    rank, big = w["rank"][:, tiles, :], w["big"][:, 0:HT * E].rearrange("p (t e) -> p t e", e=E)
    dve.wait_ge(rank_full, half + 1)
    step.did(dve.tensor_tensor(rank, ranks.rearrange("p (t e) -> p t e", e=E), row_of(cst, EOFF, E), ALU.add))
    step.settle()
    for k, m in enumerate((w["M1"], w["M2"])):
        cols = slice(k * NT + tiles.start, k * NT + tiles.stop)
        step.did(dve.tensor_tensor(big, rank, m[:, tiles, :], ALU.mult))
        step.settle()
        step.did(dve.tensor_reduce(w["dest"][:, cols], big, AX.X, ALU.add))
        step.settle()
        dve.tensor_copy(w["dest_i"][:, cols], w["dest"][:, cols]).then_inc(dest_ready, 1)


def block_table(dve, step, cst, keep, w, counts):
    E = EXPERTS
    iota = lambda o, n: cst[:, o:o + n]
    cnt, nb, be = (w["per_e"][:, i, :] for i in range(3))
    step.did(dve.tensor_copy(cnt, counts))
    step.settle()
    big2 = w["big2"]
    v = big2[:, 0:E * PBLK].rearrange("p (e m) -> p e m", m=PBLK)
    step.did(dve.tensor_tensor(v, cnt.unsqueeze(2).broadcast_to([P, E, PBLK]),
                               iota(THR, PBLK).unsqueeze(1).broadcast_to([P, E, PBLK]), ALU.is_gt))
    step.settle()
    step.did(dve.tensor_reduce(nb, v, AX.X, ALU.add))
    step.settle()
    step.did(dve.tensor_scalar(nb, nb, 1.0, None, ALU.max))
    step.settle()
    v = big2[:, 0:E * E].rearrange("p (e m) -> p e m", m=E)
    ie = iota(IOTA, E)
    step.did(dve.tensor_tensor(v, ie.unsqueeze(1).broadcast_to([P, E, E]), ie.unsqueeze(2).broadcast_to([P, E, E]), ALU.is_le))
    step.settle()
    step.did(dve.tensor_tensor(v, v, nb.unsqueeze(1).broadcast_to([P, E, E]), ALU.mult))
    step.settle()
    step.did(dve.tensor_reduce(be, v, AX.X, ALU.add))
    step.settle()
    v = big2[:, :].rearrange("p (j e) -> p j e", e=E)
    ends = be.unsqueeze(1).broadcast_to([P, NBMAX, E])
    tab_f = w["tab_f"]
    step.did(dve.tensor_tensor(v, ends, iota(IOTA, NBMAX).unsqueeze(2).broadcast_to([P, NBMAX, E]), ALU.is_le))
    step.settle()
    step.did(dve.tensor_reduce(tab_f[:, 0, :], v, AX.X, ALU.add))
    step.settle()
    step.did(dve.tensor_tensor(v, v, ends, ALU.mult))
    step.settle()
    step.did(dve.tensor_reduce(tab_f[:, 1, :], v, AX.X, ALU.max))
    step.did(dve.tensor_scalar(tab_f[:, 0, :], tab_f[:, 0, :], float(E - 1), None, ALU.min))
    step.settle()
    step.did(dve.tensor_tensor(tab_f[:, 1, :], iota(IOTA, NBMAX), tab_f[:, 1, :], ALU.subtract))
    step.settle()
    step.did(dve.tensor_scalar(tab_f[:, 1, :], tab_f[:, 1, :], float(BLK), None, ALU.mult))
    step.settle()
    step.did(dve.scalar_tensor_tensor(out=tab_f[:, 1, :], in0=tab_f[:, 0, :], scalar=float(SLOTS), in1=tab_f[:, 1, :], op0=ALU.mult, op1=ALU.add))
    step.settle()
    step.did(dve.tensor_scalar(tab_f[:, 1, :], tab_f[:, 1, :], float(E * SLOTS - BLK), None, ALU.min))
    step.settle()
    step.did(dve.tensor_tensor(be, be, nb, ALU.subtract))
    step.settle()
    for o, src in ((SLOT_OF, tab_f[:, 1, :]), (BLOCKS_OF, nb), (FIRST_OF, be)):
        step.did(dve.tensor_copy(keep["tables"][:, o:o + src.shape[1]], src))


def token_gates(dve, step, keep, w, exp_out):
    ex, z, t_ = w["ex"], per_tile(w, TOTAL), w["ex"][:, :, 4]
    dve.wait_ge(exp_out, 1)
    g1, g2 = keep["gates"][:, 0:NT], keep["gates"][:, NT:2 * NT]
    step.did(dve.tensor_reduce(z, ex[:, :, 0:4], AX.X, ALU.add))
    step.settle()
    step.did(dve.scalar_tensor_tensor(out=z, in0=t_, scalar=1.0, in1=z, op0=ALU.add, op1=ALU.mult))
    step.settle()
    step.did(dve.reciprocal(g1, z))
    step.settle()
    step.did(dve.tensor_tensor(g2, t_, g1, ALU.mult))
    step.settle()


WEIGHT_SHAPES = {"gate": [DC, FF], "up": [DC, FF], "down": [FC, D]}


def weight_slot(keep, n, par, part):
    k = WEIGHT_SHAPES[n][0] // 2
    return keep["raw"][n][par if n == "gate" else 0][:, part * k:(part + 1) * k, :]


def weight_halves(keep, n, par, part):
    k = WEIGHT_SHAPES[n][0] // 2
    return [t[:, par, part * k:(part + 1) * k, :] for t in keep["w"][n]]


def load_weights(sp, io, keep, n, e, par, part):
    k = WEIGHT_SHAPES[n][0] // 2
    v = io[f"w_{n}"].rearrange("e (k p) n -> e p k n", p=P)
    v = (v[ds(e, 1)] if not isinstance(e, int) else v[e:e + 1])[:, :, part * k:(part + 1) * k, :]
    sp.dma_start(weight_slot(keep, n, par, part), v.rearrange("a p k n -> p (a k) n")).then_inc(
        keep["w_in"][n, part, par if n == "gate" else 0], 16)


def weights_hi(act, keep, n, e, par, part):
    act.wait_ge(keep["w_in"][n, part, par if n == "gate" else 0], 8 * (e - par) + 16 if n == "gate" else 16 * e + 16)
    act.activation(weight_halves(keep, n, par, part)[0], weight_slot(keep, n, par, part), ACT.Copy, scale=WS).then_inc(keep["w_hi"][n], 1)


def weights_lo(dve, keep, n, e, par, part):
    hi, lo = weight_halves(keep, n, par, part)
    dve.wait_ge(keep["w_hi"][n], 2 * e + part + 1)
    dve.scalar_tensor_tensor(out=lo, in0=weight_slot(keep, n, par, part), scalar=WS, in1=hi,
                             op0=ALU.mult, op1=ALU.subtract).then_inc(keep["w_ready"][n], 1)


def experts(nc, io, keep):
    ctx = ExitStack()
    with ctx:
        sb = lambda name, shape, dt=F32: ctx.enter_context(nc.sbuf_tensor(f"experts_{name}", shape, dt))
        sem = lambda name: ctx.enter_context(nc.semaphore(f"experts_{name}"))
        bank = lambda name: ctx.enter_context(nc.psum_tensor(f"experts_{name}", [P, BANK], F32))
        ident, tables = keep["ident"], keep["tables"]

        w = keep["w"]
        for n in ("up", "down"):
            w[n] = [sb(f"{n}_{s}", [P, 2] + WEIGHT_SHAPES[n], F16) for s in ("hi", "lo")]
        w_ready = keep["w_ready"]
        slots = sb("slots", [P, NTABLE, 2], I32)
        source = sb("source", [P, 1], I32)
        target = sb("target", [P, 1], I32)
        xe = sb("xe", [P, D])
        xT = [sb(f"xT{s}", [P, DC, P], F16) for s in ("hi", "lo")]
        act_g = sb("act_g", [P, FF])
        hid = sb("hid", [P, FF])
        hidT = [sb(f"hidT{s}", [P, FC, P], F16) for s in ("hi", "lo")]
        y_out = sb("y_out", [P, D])

        g_ps, h_ps = bank("g_ps"), bank("h_ps")
        u_ps = [bank(f"u_ps{i}") for i in range(2)]
        x_ps = [bank(f"x_ps{i}") for i in range(2)]
        y_ps = [bank(f"ye_ps{i}") for i in range(2)]

        slots_in = sem("slots_in")
        picked = sem("picked")
        y_gone = sem("y_gone")
        xe_in = sem("xe_in")
        x_full = sem("x_full")
        x_hi = sem("x_hi")
        x_ready = sem("x_ready")
        g_full = sem("g_full")
        act_ready = sem("act_ready")
        u_full = sem("u_full")
        hid_ready = sem("hid_ready")
        h_full = sem("h_full")
        h_hi = sem("h_hi")
        h_ready = sem("h_ready")
        y_full = sem("y_full")
        y_left = sem("y_left")
        y_right = sem("y_right")
        y_stored = sem("y_stored")
        sp_passed = sem("sp_passed")
        pool_passed = sem("pool_passed")

        def over_experts(eng, first, body, before=None):
            first()

            def one(e, par, last):
                if before:
                    before(e, par, last)
                index = lambda o: tables[0:1, ds(o + e, 1)] if not isinstance(e, int) else tables[0:1, o + e:o + e + 1]
                count = eng.value_load(index(BLOCKS_OF), min_val=1, max_val=PBLK)
                start = eng.value_load(index(FIRST_OF), min_val=0, max_val=LAST_BLOCK)
                body(e, par, count, start, last)

            with eng.Fori(0, EXPERTS // 2 - 1) as ee:
                one(2 * ee, 0, False)
                one(2 * ee + 1, 1, False)
            one(EXPERTS - 2, 0, False)
            one(EXPERTS - 1, 1, True)

        SPLIT_A = (("gate", 0), ("gate", 1), ("up", 0))
        SPLIT_B = (("up", 1), ("down", 0), ("down", 1))
        block = ctx.enter_context(nc.Block())

        @block.sync
        def _(sp):
            def refill(n, e, par, part):
                wait_alone(sp, w_ready[n], 2 * (e - (2 if n == "gate" else 1)) + part + 1, sp_passed)
                load_weights(sp, io, keep, n, e, par, part)

            sp.wait_ge(xe_in, 16)
            for n, e in (("up", 1), ("gate", 2), ("down", 1)):
                for part in range(2):
                    refill(n, e, e % 2, part)
            with sp.Fori(0, EXPERTS // 2 - 2) as i:
                for par in range(2):
                    e = 2 * i + par
                    for n, ahead in (("gate", 3), ("up", 2), ("down", 2)):
                        for part in range(2):
                            refill(n, e + ahead, (par + ahead) % 2, part)
            for e in range(EXPERTS - 4, EXPERTS - 2):
                for n, ahead in (("gate", 3), ("up", 2), ("down", 2)):
                    for part in range(2):
                        if e + ahead < EXPERTS:
                            refill(n, e + ahead, (e + ahead) % 2, part)

        @block.gpsimd
        def _(pool):
            def load_slots(j):
                slot = pool.value_load(tables[0:1, ds(SLOT_OF + j, 1)] if not isinstance(j, int) else tables[0:1, j:j + 1],
                                       min_val=0, max_val=EXPERTS * SLOTS - BLK)
                dst = slots[:, ds(j, 1), :] if not isinstance(j, int) else slots[:, j:j + 1, :]
                pool.dma_start(dst.rearrange("p a n -> p (a n)"), io["slots"][ds(slot, BLK), :]).then_inc(slots_in, 16)

            def pick(dst, j, column, n):
                src = slots[:, ds(j, 1), column] if not isinstance(j, int) else slots[:, j:j + 1, column]
                pool.tensor_copy(dst[:, :], src).then_inc(picked, 1)
                wait_alone(pool, picked, n + 1, pool_passed)

            def gather(j, n):
                pick(source, j, 0, n)
                pool.indirect_dma_start(xe[:, :], None, io["h2"], bass.IndirectOffsetOnAxis(ap=source[:, 0:1], axis=0)).then_inc(xe_in, 16)

            def first():
                for j in range(3):
                    load_slots(j)
                    pool.wait_ge(slots_in, 16 * j + 16)
                    if j == 0:
                        gather(0, 0)
                pool.wait_ge(x_full, 2)
                gather(1, 1)

            def body(e, par, count, start, last):
                with pool.Fori(0, count) as i:
                    j = start + i
                    load_slots(j + 3)
                    wait_alone(pool, x_full, 2 * j + 4, pool_passed)
                    wait_alone(pool, xe_in, 16 * j + 32, pool_passed)
                    gather(j + 2, 2 * j + 2)
                    pool.wait_ge(y_left, j + 2)
                    wait_alone(pool, y_right, j + 2, pool_passed)
                    pick(target, j, 1, 2 * j + 3)
                    pool.indirect_dma_start(io["y"], bass.IndirectOffsetOnAxis(ap=target[:, 0:1], axis=0), y_out[:, :], None).then_inc(y_stored, 16)
                    wait_alone(pool, y_stored, 16 * j + 16, pool_passed)
                    wait_alone(pool, slots_in, 16 * j + 64, y_gone)

            over_experts(pool, first, body)

        @block.scalar
        def _(act):
            act.sem_inc(y_left, 1)
            act.preload_act_table(ACT.Silu)

            def split(e, par, n, part):
                weights_hi(act, keep, n, e, par, part)

            def rows_hi(j, i):
                act.wait_ge(x_full, 2 * j + i + 1)
                act.activation(xT[0][:, 4 * i:4 * i + 4, :], x_ps[i][:, :].rearrange("p (k t) -> p k t", k=4), ACT.Copy).then_inc(x_hi, 1)

            def first():
                for i in range(2):
                    rows_hi(0, i)
                for n in ("up", "down"):
                    for part in range(2):
                        split(0, 0, n, part)

            def before(e, par, last):
                if not last:
                    for n, part in SPLIT_A:
                        split(e + 1, 1 - par, n, part)

            def blk(j, more=None):
                act.wait_ge(g_full, j + 1)
                act.wait_ge(hid_ready, 2 * j + 1)
                act.activation(act_g[:, :], g_ps[:, :], ACT.Silu, scale=1 / WS).then_inc(act_ready, 1)
                rows_hi(j + 1, 0)
                act.wait_ge(h_full, j + 2)
                act.activation(hidT[0][:, :, :], h_ps[:, :].rearrange("p (k t) -> p k t", k=FC), ACT.Copy).then_inc(h_hi, 1)
                rows_hi(j + 1, 1)
                if more:
                    more()
                act.wait_ge(y_full, j + 2)
                act.wait_ge(y_gone, j + 1)
                act.activation(y_out[:, 0:BANK], y_ps[0][:, :], ACT.Copy, scale=1 / WS).then_inc(y_left, 1)

            def body(e, par, count, start, last):
                def more():
                    for n, part in SPLIT_B:
                        split(e + 1, 1 - par, n, part)
                blk(start, None if last else more)
                with act.If(count > 1):
                    with act.Fori(1, count) as k:
                        blk(start + k)

            act.sem_inc(y_gone, 1)
            over_experts(act, first, body, before)

        @block.vector
        def _(dve):
            for signal in (hid_ready, h_ready, y_right):
                dve.sem_inc(signal, 1)
            def split(e, par, n, part):
                weights_lo(dve, keep, n, e, par, part)

            def rows_lo(j, i):
                dve.wait_ge(x_hi, 2 * j + i + 1)
                dve.tensor_tensor(xT[1][:, 4 * i:4 * i + 4, :], x_ps[i][:, :].rearrange("p (k t) -> p k t", k=4),
                                  xT[0][:, 4 * i:4 * i + 4, :], ALU.subtract).then_inc(x_ready, 1)

            def first():
                for i in range(2):
                    rows_lo(0, i)
                for n in ("up", "down"):
                    for part in range(2):
                        split(0, 0, n, part)

            def before(e, par, last):
                if not last:
                    for n, part in SPLIT_A:
                        split(e + 1, 1 - par, n, part)

            def blk(j, more=None):
                dve.wait_ge(act_ready, j + 1)
                dve.wait_ge(h_full, j + 1)
                for i in range(2):
                    cols = slice(i * FF // 2, (i + 1) * FF // 2)
                    dve.wait_ge(u_full, 2 * j + i + 1)
                    dve.scalar_tensor_tensor(out=hid[:, cols], in0=u_ps[i][:, 0:FF // 2], scalar=1 / WS, in1=act_g[:, cols],
                                             op0=ALU.mult, op1=ALU.mult).then_inc(hid_ready, 1)
                rows_lo(j + 1, 0)
                dve.wait_ge(h_hi, j + 1)
                dve.tensor_tensor(hidT[1][:, :, :], h_ps[:, :].rearrange("p (k t) -> p k t", k=FC), hidT[0][:, :, :],
                                  ALU.subtract).then_inc(h_ready, 1)
                rows_lo(j + 1, 1)
                if more:
                    more()
                dve.wait_ge(y_full, j + 2)
                dve.wait_ge(y_gone, j + 1)
                dve.tensor_scalar(y_out[:, BANK:D], y_ps[1][:, :], 1 / WS, None, ALU.mult).then_inc(y_right, 1)

            def body(e, par, count, start, last):
                def more():
                    for n, part in SPLIT_B:
                        split(e + 1, 1 - par, n, part)
                blk(start, None if last else more)
                with dve.If(count > 1):
                    with dve.Fori(1, count) as k:
                        blk(start + k)

            over_experts(dve, first, body, before)

        @block.tensor
        def _(pe):
            for signal in (y_full, h_full):
                pe.sem_inc(signal, 1)
            def transpose_rows(j, i):
                for u in range(4):
                    k = 4 * i + u
                    ins = pe.transpose(x_ps[i][:, u * P:(u + 1) * P], xe[:, k * P:(k + 1) * P], ident[:, :])
                ins.then_inc(x_full, 1)

            def first():
                pe.wait_ge(xe_in, 16)
                transpose_rows(0, 0)
                transpose_rows(0, 1)

            def body(e, par, count, start, last):
                with pe.Fori(0, count) as i:
                    j = start + i
                    pe.wait_ge(x_ready, 2 * j + 2)
                    pe.wait_ge(hid_ready, 2 * j + 1)
                    for n, out, cols, full in (("gate", g_ps[:, :], slice(0, FF), g_full),
                                               ("up", u_ps[0][:, 0:FF // 2], slice(0, FF // 2), u_full),
                                               ("up", u_ps[1][:, 0:FF // 2], slice(FF // 2, FF), u_full)):
                        pe.wait_ge(w_ready[n], 2 * e + 2)
                        for k in range(DC):
                            ins = three_pass(pe, out, [t[:, k, :] for t in xT], [t[:, par, k, cols] for t in w[n]], k == 0, k == DC - 1)
                        ins.then_inc(full, 1)
                    pe.wait_ge(xe_in, 16 * j + 32)
                    transpose_rows(j + 1, 0)
                    for k in range(FC):
                        if k % 2 == 0:
                            pe.wait_ge(hid_ready, 2 * j + k // 2 + 2)
                        ins = pe.transpose(h_ps[:, k * P:(k + 1) * P], hid[:, k * P:(k + 1) * P], ident[:, :])
                    ins.then_inc(h_full, 1)
                    transpose_rows(j + 1, 1)
                    pe.wait_ge(h_hi, j + 1)
                    pe.wait_ge(y_left, j + 1)
                    pe.wait_ge(y_right, j + 1)
                    pe.wait_ge(w_ready["down"], 2 * e + 2)
                    for part, k, low in [(0, k, low) for k in range(FC) for low in range(2)] + [(1, k, 0) for k in range(FC)]:
                        if part == 1 and k == 0:
                            pe.wait_ge(h_ready, j + 2)
                        for c in range(2):
                            ins = pe.matmul(y_ps[c][:, :], hidT[part][:, k, :], w["down"][low][:, par, k, c * BANK:(c + 1) * BANK],
                                            start=(part == 0 and k == 0 and low == 0), stop=(part == 1 and k == FC - 1))
                    ins.then_inc(y_full, 1)

            over_experts(pe, first, body)


def combine(nc, io, keep):
    ctx = ExitStack()
    with ctx:
        sb = lambda name, shape, dt=F32: ctx.enter_context(nc.sbuf_tensor(f"combine_{name}", shape, dt))
        sem = lambda name: ctx.enter_context(nc.semaphore(f"combine_{name}"))
        gates, g2b = keep["gates"], keep["g2b"]
        BUFS = 4
        ya = sb("ya", [P, BUFS, D])
        yb = sb("yb", [P, BUFS, D])
        xr = sb("xr", [P, BUFS, D])
        res = sb("res", [P, BUFS, D])
        sq = sb("sq", [P, D], BF16)
        fg = sb("fg", [P, D])
        ss = sb("ss", [P, BUFS])
        rms = sb("rms", [P, BUFS])
        rstd = sb("rstd", [P, BUFS])
        eps_t = sb("eps_t", [P, 1])


        fg_in = sem("fg_in")
        ya_in = [sem(f"ya_in{i}") for i in range(BUFS)]
        yb_in = [sem(f"yb_in{i}") for i in range(BUFS)]
        xr_in = [sem(f"xr_in{i}") for i in range(BUFS)]
        out_done = [sem(f"out_done{i}") for i in range(BUFS)]
        ya_scaled = sem("ya_scaled")
        x2_ready = sem("x2_ready")
        sq_done = sem("sq_done")
        rms_ready = sem("rms_ready")
        res_ready = sem("res_ready")
        eps_ready = sem("eps_ready")
        dve_step = sem("dve_step")
        sp_passed = sem("sp_passed")
        block = ctx.enter_context(nc.Block())

        @block.sync
        def _(sp):
            for signal in out_done:
                sp.sem_inc(signal, 1)
            sp.dma_start(fg[:, :], io["final_g"].rearrange("(a n) -> a n", a=1).broadcast_to([P, D])).then_inc(fg_in, 16)

            def load(t, par):
                rows = lambda o: ds(t * P + o, P) if not isinstance(t, int) else slice(t * P + o, t * P + o + P)
                sp.dma_start(ya[:, par, :], io["y"][rows(0), :]).then_inc(ya_in[par], 16)
                sp.dma_start(yb[:, par, :], io["y"][rows(SEQ), :]).then_inc(yb_in[par], 16)
                sp.dma_start(xr[:, par, :], io["x1"][rows(0), :]).then_inc(xr_in[par], 16)

            for t in range(BUFS):
                load(t, t)
            with sp.Fori(0, NT // BUFS - 1) as i:
                for par in range(BUFS):
                    t = BUFS * i + par
                    wait_alone(sp, res_ready, t + 1, sp_passed)
                    sp.dma_start(io["out"][ds(t * P, P), :], res[:, par, :]).then_inc(out_done[par], 16)
                    load(t + BUFS, par)
            for t in range(NT - BUFS, NT):
                sp.wait_ge(res_ready, t + 1)
                sp.dma_start(io["out"][t * P:(t + 1) * P, :], res[:, t % BUFS, :]).then_inc(out_done[t % BUFS], 16)
            for par in range(BUFS):
                sp.wait_ge(out_done[par], 16 * NT // BUFS + 1)

        @block.scalar
        def _(act):
            act.sem_inc(rms_ready, 1)
            act.preload_act_table(ACT.Sqrt)
            act.wait_ge(eps_ready, 1)

            def scale_first(i, b):
                t = BUFS * i + b
                act.wait_ge(ya_in[b], 16 * i + 16)
                gate = gates[:, ds(t, 1)] if not isinstance(t, int) else gates[:, t:t + 1]
                act.activation(ya[:, b, :], ya[:, b, :], ACT.Copy, scale=gate).then_inc(ya_scaled, 1)

            def root(t, b):
                act.wait_ge(x2_ready, t + 1)
                act.wait_ge(rms_ready, t + 1)
                act.activation(sq[:, :], xr[:, b, :], ACT.Square, accum_out=ss[:, b:b + 1]).then_inc(sq_done, 1)
                act.wait_ge(sq_done, t + 1)
                act.activation(rms[:, b:b + 1], ss[:, b:b + 1], ACT.Sqrt, bias=eps_t[:, :], scale=1.0 / D).then_inc(rms_ready, 1)

            def tiles(i, last=False):
                for b in range(BUFS):
                    if b < BUFS - 1:
                        scale_first(i, b + 1)
                    elif not last:
                        scale_first(i + 1, 0)
                    root(BUFS * i + b, b)

            scale_first(0, 0)
            with act.Fori(0, NT // BUFS - 1) as i:
                tiles(i)
            tiles(NT // BUFS - 1, last=True)

        @block.vector
        def _(dve):
            step = Steps(dve, dve_step)
            dve.memset(eps_t[:, :], EPS).then_inc(eps_ready, 1)
            dve.wait_ge(fg_in, 16)
            PER = 3

            def add_up(i, b):
                t = BUFS * i + b
                y = yb[:, b, :]
                gate = gates[:, ds(NT + t, 1)] if not isinstance(t, int) else gates[:, NT + t:NT + t + 1]
                dve.wait_ge(ya_scaled, t + 1)
                dve.wait_ge(yb_in[b], 16 * i + 16)
                step.did(dve.scalar_tensor_tensor(out=y, in0=y, scalar=gate, in1=ya[:, b, :], op0=ALU.mult, op1=ALU.add))
                step.settle()
                step.did(dve.tensor_tensor(y, y, g2b[:, :], ALU.mult))
                dve.wait_ge(xr_in[b], 16 * i + 16)
                step.settle()
                dve.tensor_tensor(xr[:, b, :], xr[:, b, :], y, ALU.add).then_inc(x2_ready, 1)

            def finish(i, b):
                t = BUFS * i + b
                dve.wait_ge(rms_ready, t + 2)
                step.did(dve.reciprocal(rstd[:, b:b + 1], rms[:, b:b + 1]))
                dve.wait_ge(out_done[b], 16 * i + 1)
                step.settle()
                dve.scalar_tensor_tensor(out=res[:, b, :], in0=xr[:, b, :], scalar=rstd[:, b:b + 1],
                                         in1=fg[:, :], op0=ALU.mult, op1=ALU.mult).then_inc(res_ready, 1)

            def tiles(i, last=False):
                for b in range(BUFS):
                    if b < BUFS - 1:
                        add_up(i, b + 1)
                    elif not last:
                        add_up(i + 1, 0)
                    finish(i, b)

            add_up(0, 0)
            with dve.Fori(0, NT // BUFS - 1) as i:
                step.enter(i * (BUFS * PER), BUFS * PER)
                tiles(i)
            step.leave(NT // BUFS - 1)
            tiles(NT // BUFS - 1, last=True)




def build(nc, io):
    scratch = lambda name, shape, dt=F32: nc.dram_tensor(name, shape, dt, kind="Internal").ap()
    io["mod_rows"] = scratch("mod_rows", (1, 4 * D))
    io["attn"] = scratch("attn", (SEQ, HEADS * VD))
    io["x1"] = scratch("x1", (SEQ, D))
    io["h2"] = scratch("h2", (SEQ, D))
    io["slots"] = scratch("slots", (EXPERTS * SLOTS, 2), I32)
    io["y"] = scratch("y", (TOPK * SEQ + BLK, D))
    with ExitStack() as whole:
        sb = lambda name, shape, dt=F32: whole.enter_context(nc.sbuf_tensor(name, shape, dt))
        shared = sb("shared", [P, 2, DC * D], F16)
        keep = {"ident": sb("ident", [P, P]), "shared": shared,
                "w_o": [shared[:, i, :].rearrange("p (k n) -> p k n", k=DC) for i in range(2)]}
        with ExitStack() as latents:
            sb_l = lambda name, shape: latents.enter_context(nc.sbuf_tensor(name, shape, F16))
            keep["cqT"] = [sb_l(f"cqT_{s}", [P, RC, SEQ]) for s in ("hi", "lo")]
            keep["ckvT"] = [sb_l(f"ckvT_{s}", [P, KC, KEYS]) for s in ("hi", "lo")]
            keep["krT"] = [sb_l(f"krT_{s}", [P, KEYS]) for s in ("hi", "lo")]
            keep["qrT"] = sb_l("qrT", [P, HEADS, SEQ])
            project(nc, io, keep)
            attend(nc, io, keep)
        keep.update({"g2b": sb("g2b", [P, D]), "gates": sb("gates", [P, TOPK * NT]), "tables": sb("tables", [P, NTABLE], I32)})
        with ExitStack() as moe:
            sem = lambda name: moe.enter_context(nc.semaphore(name))
            keep["raw"] = {n: [shared[:, i, :].bitcast(F32).rearrange("p (k n) -> p k n", k=DC)] for i, n in enumerate(("gate", "up"))}
            keep["raw"]["gate"].append(moe.enter_context(nc.sbuf_tensor("gate_raw1", [P, DC, FF], F32))[:, :, :])
            keep["raw"]["down"] = [moe.enter_context(nc.sbuf_tensor("down_raw", [P, FC, D], F32))[:, :, :]]
            keep["w"] = {"gate": [moe.enter_context(nc.sbuf_tensor(f"gate_{s}", [P, 2, DC, FF], F16)) for s in ("hi", "lo")]}
            keep["w_in"] = {(n, part, slot): sem(f"{n}_in{part}{slot}") for n in WEIGHT_SHAPES for part in range(2)
                            for slot in range(2 if n == "gate" else 1)}
            keep["w_hi"] = {n: sem(f"{n}_hi") for n in WEIGHT_SHAPES}
            keep["w_ready"] = {n: sem(f"{n}_ready") for n in WEIGHT_SHAPES}
            route(nc, io, keep)
            experts(nc, io, keep)
        combine(nc, io, keep)


def rotary_tables():
    n = ROPE // 4
    freq = (np.float32(ROPE_THETA) ** (-np.arange(n, dtype=np.float32) / np.float32(n))).astype(np.float32)
    t = np.arange(SEQ)
    row, col = (t // GRID_W).astype(np.float32), (t % GRID_W).astype(np.float32)
    angle = np.concatenate([row[:, None] * freq, col[:, None] * freq], -1)
    tile = lambda a: np.ascontiguousarray(a.astype(np.float32).reshape(KT, P, HALF).transpose(1, 0, 2))
    return (tile(np.concatenate([np.cos(angle), np.ones((CTX, HALF))])),
            tile(np.concatenate([np.sin(angle), np.zeros((CTX, HALF))])))


def constants():
    cos, sin = rotary_tables()
    e, s = np.arange(EXPERTS), np.arange(EXPERTS * SLOTS // P)
    token = np.arange(SEQ, dtype=np.int32).reshape(NT, P).T
    return {
        "ident": np.eye(P, dtype=np.float32), "cos": cos, "sin": sin,
        "tri": np.triu(np.ones((P, P), np.float32), 1),
        "row_consts": np.concatenate([np.arange(NBMAX) - NBMAX, np.arange(NBMAX), e * SLOTS, np.arange(PBLK) * BLK])[None].astype(np.float32),
        "tok": np.stack([np.stack([token, token + k * SEQ], -1) for k in range(TOPK)], 1).astype(np.int32),
        "empty_slots": np.broadcast_to(np.stack([0 * s, TOPK * SEQ + s % BLK], -1).reshape(-1), (P, 2 * len(s))).astype(np.int32),
    }


def kernel(**inputs):
    import concourse.bacc as bacc
    from concourse.bass_utils import run_bass_kernel_spmd

    a = {k: np.asarray(v) for k, v in inputs.items()}
    w_uq = a["mla_w_uq"][0].reshape(Q_RANK, HEADS, QK)
    w_ukv = a["mla_w_ukv"][0].reshape(KV_RANK, HEADS, KV)
    arrays = {
        "xc": np.concatenate([a["x"][0], a["ctx"][0]]), "c": a["c"][0], "c_ctx": a["c_ctx"],
        "mod_w": a["mod_w"][0], "mod_b": a["mod_b"][0], "norm1_g": a["norm1_g"][0], "norm2_g": a["norm2_g"][0],
        "final_g": a["final_g"], "g_q": a["mla_g_q"][0], "g_kv": a["mla_g_kv"][0],
        "w_dq": a["mla_w_dq"][0], "w_dkv": a["mla_w_dkv"][0],
        "w_uq_rope": w_uq[:, :, NOPE:].reshape(Q_RANK, HEADS * ROPE),
        "w_uq": w_uq[:, :, :NOPE].transpose(1, 0, 2),
        "w_uk": w_ukv[:, :, :NOPE].transpose(1, 0, 2), "w_uv": w_ukv[:, :, NOPE:].transpose(1, 0, 2),
        "w_o": a["mla_w_o"][0],
        "w_r": np.concatenate([a["moe_w_grp"][0], a["moe_w_rt"][0]], 1),
        "b_r": np.concatenate([a["moe_b_grp"][0], a["moe_b_rt"][0]]),
        "w_gate": a["moe_w_gate"][0], "w_up": a["moe_w_up"][0], "w_down": a["moe_w_down"][0],
        **constants(),
    }
    arrays = {f"in_{k}": np.ascontiguousarray(v) for k, v in arrays.items()}
    nc = bacc.Bacc("TRN2", target_bir_lowering=False, num_devices=1)
    io = {k[3:]: nc.dram_tensor(k, v.shape, mybir.dt.from_np(v.dtype), kind="ExternalInput").ap() for k, v in arrays.items()}
    io["out"] = nc.dram_tensor("out", (SEQ, D), F32, kind="ExternalOutput").ap()
    build(nc, io)
    r = run_bass_kernel_spmd(nc, [arrays], core_ids=[0])
    return r.results[0]["out"].reshape(1, SEQ, D)
```
